# Optimizing a Trainium2 kernel written in Bass

```python
import math
import jax, jax.numpy as jnp
from jax import lax
import numpy as np

D_MODEL = 1024
BATCH = 1
SEQ = 256
DEPTH = 1
DEC_BATCH = 8
DEC_SEQ = 8
PAST_LEN = 2048
PAGE_SIZE = 128

MIX_WIDTH = D_MODEL
ATTN_WIDTH = MIX_WIDTH // 2
CONV_CH = MIX_WIDTH - ATTN_WIDTH
N_HEADS = 8
HEAD_DIM = ATTN_WIDTH // N_HEADS
MOBA_BLOCK = 256
MOBA_TOPK = 3
Q_CHUNK = 32
CONV_K = 31
GN_GROUPS = 8
D_FF = ((8 * D_MODEL // 3 + 255) // 256) * 256
DEEPNORM_ALPHA = (2.0 * DEPTH) ** 0.25
DEEPNORM_BETA = (8.0 * DEPTH) ** -0.25
LN_EPS = 1e-5
NEG_INF = -1e30

kernel_name = 'hymba_moba_conformer_macaron_decoder_step'

def _layernorm(x, g, b):
    xf = x.astype(jnp.float32)
    mu = jnp.mean(xf, -1, keepdims=True)
    var = jnp.mean(jnp.square(xf - mu), -1, keepdims=True)
    y = (xf - mu) * lax.rsqrt(var + LN_EPS) * g.astype(jnp.float32) + b.astype(jnp.float32)
    return y.astype(x.dtype)

def _groupnorm_channels(x, g, b):
    shp = x.shape
    xf = x.astype(jnp.float32).reshape(shp[:-1] + (GN_GROUPS, shp[-1] // GN_GROUPS))
    mu = jnp.mean(xf, -1, keepdims=True)
    var = jnp.mean(jnp.square(xf - mu), -1, keepdims=True)
    y = ((xf - mu) * lax.rsqrt(var + LN_EPS)).reshape(shp)
    return (y * g.astype(jnp.float32) + b.astype(jnp.float32)).astype(x.dtype)

def _alibi_slopes():
    return 2.0 ** (-8.0 * jnp.arange(1, N_HEADS + 1, dtype=jnp.float32) / N_HEADS)

def _swiglu(h, wg, wu, wd):
    return (jax.nn.silu(h @ wg) * (h @ wu)) @ wd

def _split_heads(t):
    b, s, _ = t.shape
    return t.reshape(b, s, N_HEADS, HEAD_DIM).transpose(0, 2, 1, 3)

def _merge_heads(t):
    b, h, s, d = t.shape
    return t.transpose(0, 2, 1, 3).reshape(b, s, h * d)

def _project(h, w_in):
    u = h @ w_in
    q, k, v, ga, gb = jnp.split(u, [ATTN_WIDTH, 2 * ATTN_WIDTH, 3 * ATTN_WIDTH, 3 * ATTN_WIDTH + CONV_CH], axis=-1)
    return _split_heads(q), _split_heads(k), _split_heads(v), ga * jax.nn.sigmoid(gb)

def _conv_branch(buf, w_dw, b_dw, gn_g, gn_b):
    y = lax.conv_general_dilated(buf, w_dw[:, None, :], (1,), 'VALID',
                                 dimension_numbers=('NWC', 'WIO', 'NWC'),
                                 feature_group_count=CONV_CH) + b_dw
    return jax.nn.silu(_groupnorm_channels(y, gn_g, gn_b))

def _merge(attn, conv, beta_attn, beta_conv, w_out):
    return jnp.concatenate([_merge_heads(attn) * beta_attn, conv * beta_conv], axis=-1) @ w_out

def _moba_softmax(q, q_pos, sel_k, sel_v, sel_pos, sel_ok, own_k, own_v, own_pos, slopes):
    scale = HEAD_DIM ** -0.5
    m = slopes[None, :, None, None]
    rel_sel = (q_pos[:, None] - sel_pos).astype(jnp.float32)
    s_sel = jnp.einsum('bhqd,bhqkd->bhqk', q, sel_k, preferred_element_type=jnp.float32) * scale - m * rel_sel
    s_sel = jnp.where(sel_ok, s_sel, NEG_INF)
    rel_own = q_pos[:, None] - own_pos[None, :]
    s_own = jnp.einsum('bhqd,bhkd->bhqk', q, own_k, preferred_element_type=jnp.float32) * scale \
        - m * rel_own.astype(jnp.float32)
    s_own = jnp.where(rel_own >= 0, s_own, NEG_INF)
    p = jax.nn.softmax(jnp.concatenate([s_sel, s_own], axis=-1), axis=-1)
    ks = sel_k.shape[3]
    out = jnp.einsum('bhqk,bhqkd->bhqd', p[..., :ks].astype(sel_v.dtype), sel_v, preferred_element_type=jnp.float32) \
        + jnp.einsum('bhqk,bhkd->bhqd', p[..., ks:].astype(own_v.dtype), own_v, preferred_element_type=jnp.float32)
    return out.astype(q.dtype)

def _moba_prompt(q, k, v, slopes):
    b, h, s, dh = q.shape
    nb = -(-s // MOBA_BLOCK)
    pad = nb * MOBA_BLOCK - s
    kb = jnp.pad(k, ((0, 0), (0, 0), (0, pad), (0, 0))).reshape(b, h, nb, MOBA_BLOCK, dh)
    vb = jnp.pad(v, ((0, 0), (0, 0), (0, pad), (0, 0))).reshape(b, h, nb, MOBA_BLOCK, dh)
    kmean = jnp.mean(kb, axis=3, dtype=jnp.float32)
    k_eff = min(MOBA_TOPK, nb - 1)
    n_chunks = s // Q_CHUNK
    qc = q.reshape(b, h, n_chunks, Q_CHUNK, dh).transpose(2, 0, 1, 3, 4)
    bi = jnp.arange(b)[:, None, None, None]
    hi = jnp.arange(h)[None, :, None, None]
    blk_pos = jnp.arange(MOBA_BLOCK)

    def chunk(args):
        qi, ci = args
        start = ci * Q_CHUNK
        q_pos = start + jnp.arange(Q_CHUNK)
        qb = start // MOBA_BLOCK
        own_k = lax.dynamic_index_in_dim(kb, qb, axis=2, keepdims=False)
        own_v = lax.dynamic_index_in_dim(vb, qb, axis=2, keepdims=False)
        own_pos = qb * MOBA_BLOCK + blk_pos
        if k_eff > 0:
            gate = jnp.einsum('bhqd,bhnd->bhqn', qi.astype(jnp.float32), kmean)
            gate = jnp.where(jnp.arange(nb) < qb, gate, -jnp.inf)
            _, idx = lax.top_k(gate, k_eff)
            sel_k = kb[bi, hi, idx].reshape(b, h, Q_CHUNK, k_eff * MOBA_BLOCK, dh)
            sel_v = vb[bi, hi, idx].reshape(b, h, Q_CHUNK, k_eff * MOBA_BLOCK, dh)
            sel_pos = (idx[..., None] * MOBA_BLOCK + blk_pos).reshape(b, h, Q_CHUNK, -1)
            sel_ok = jnp.broadcast_to((idx < qb)[..., None], idx.shape + (MOBA_BLOCK,)).reshape(b, h, Q_CHUNK, -1)
        else:
            sel_k = jnp.zeros((b, h, Q_CHUNK, 0, dh), k.dtype)
            sel_v = jnp.zeros((b, h, Q_CHUNK, 0, dh), v.dtype)
            sel_pos = jnp.zeros((b, h, Q_CHUNK, 0), jnp.int32)
            sel_ok = jnp.zeros((b, h, Q_CHUNK, 0), bool)
        return _moba_softmax(qi, q_pos, sel_k, sel_v, sel_pos, sel_ok, own_k, own_v, own_pos, slopes)

    out = lax.map(chunk, (qc, jnp.arange(n_chunks)))
    return out.transpose(1, 2, 0, 3, 4).reshape(b, h, s, dh)

def _moba_sample(q, k, v, pool_k, pool_v, page_table, slopes):
    db, h, t, dh = q.shape
    ppb = MOBA_BLOCK // PAGE_SIZE
    nbp = PAST_LEN // MOBA_BLOCK
    rp = (PAST_LEN - nbp * MOBA_BLOCK) // PAGE_SIZE
    q_pos = PAST_LEN + jnp.arange(t)
    own_pages = page_table[:, nbp * ppb: nbp * ppb + rp]
    past_k = pool_k[own_pages].transpose(0, 2, 1, 3, 4).reshape(db, h, rp * PAGE_SIZE, dh)
    past_v = pool_v[own_pages].transpose(0, 2, 1, 3, 4).reshape(db, h, rp * PAGE_SIZE, dh)
    own_k = jnp.concatenate([past_k, k], axis=2)
    own_v = jnp.concatenate([past_v, v], axis=2)
    own_pos = jnp.concatenate([nbp * MOBA_BLOCK + jnp.arange(rp * PAGE_SIZE), q_pos])
    k_eff = min(MOBA_TOPK, nbp)
    if k_eff > 0:
        def seq_block_means(pt_row):
            rows = pool_k[pt_row[:nbp * ppb]].reshape(nbp, ppb, h, PAGE_SIZE, dh)
            return jnp.mean(rows, axis=(1, 3), dtype=jnp.float32)
        kmean = lax.map(seq_block_means, page_table).transpose(0, 2, 1, 3)
        gate = jnp.einsum('bhqd,bhnd->bhqn', q.astype(jnp.float32), kmean)
        _, idx = lax.top_k(gate, k_eff)
        logical = idx[..., None] * ppb + jnp.arange(ppb)
        phys = page_table[jnp.arange(db)[:, None, None, None, None], logical]
        hsel = jnp.arange(h)[None, :, None, None, None]
        sel_k = pool_k[phys, hsel].reshape(db, h, t, k_eff * MOBA_BLOCK, dh)
        sel_v = pool_v[phys, hsel].reshape(db, h, t, k_eff * MOBA_BLOCK, dh)
        sel_pos = (idx[..., None] * MOBA_BLOCK + jnp.arange(MOBA_BLOCK)).reshape(db, h, t, -1)
        sel_ok = jnp.ones(sel_pos.shape, bool)
    else:
        sel_k = jnp.zeros((db, h, t, 0, dh), k.dtype)
        sel_v = jnp.zeros((db, h, t, 0, dh), v.dtype)
        sel_pos = jnp.zeros((db, h, t, 0), jnp.int32)
        sel_ok = jnp.zeros((db, h, t, 0), bool)
    return _moba_softmax(q, q_pos, sel_k, sel_v, sel_pos, sel_ok, own_k, own_v, own_pos, slopes)

def _trunk_layer(x, c, mixer, w_ada, b_ada, f1g, f1u, f1d, f2g, f2u, f2d, ln_g, ln_b):
    ada = (jax.nn.silu(c) @ w_ada + b_ada).reshape(c.shape[0], 3, 3, D_MODEL)

    def mod(t, i):
        return t * (1.0 + ada[:, i, 1, None, :]) + ada[:, i, 0, None, :]

    def post(t, y, i):
        return _layernorm(DEEPNORM_ALPHA * t + ada[:, i, 2, None, :] * y, ln_g[i], ln_b[i])

    x = post(x, 0.5 * _swiglu(mod(x, 0), f1g, f1u, f1d), 0)
    m, st = mixer(mod(x, 1))
    x = post(x, m, 1)
    x = post(x, 0.5 * _swiglu(mod(x, 2), f2g, f2u, f2d), 2)
    return x, st

def setup_inputs(seed: int = 0) -> dict:
    key = jax.random.key(seed)
    ks = jax.random.split(key, 32)
    n_pages = PAST_LEN // PAGE_SIZE
    n_pool = (DEC_BATCH * n_pages * 5) // 4
    f32 = jnp.float32

    def nrm(k, shape, s):
        return jax.random.normal(k, shape, f32) * s

    w_in = nrm(ks[8], (DEPTH, D_MODEL, 3 * ATTN_WIDTH + 2 * CONV_CH), D_MODEL ** -0.5)
    w_in = w_in.at[:, :, 2 * ATTN_WIDTH:3 * ATTN_WIDTH].multiply(DEEPNORM_BETA)
    page_table = jax.random.permutation(ks[5], n_pool)[:DEC_BATCH * n_pages].reshape(DEC_BATCH, n_pages).astype(jnp.int32)
    return {
        'x_prompt': nrm(ks[0], (BATCH, SEQ, D_MODEL), 1.0),
        'x_sample': nrm(ks[1], (DEC_BATCH, DEC_SEQ, D_MODEL), 1.0),
        'cache_k': nrm(ks[2], (DEPTH, n_pool, N_HEADS, PAGE_SIZE, HEAD_DIM), 1.0),
        'cache_v': nrm(ks[3], (DEPTH, n_pool, N_HEADS, PAGE_SIZE, HEAD_DIM), 1.0),
        'state_conv': nrm(ks[4], (DEPTH, DEC_BATCH, CONV_K - 1, CONV_CH), 1.0),
        'page_table': page_table,
        'c_prompt': nrm(ks[6], (BATCH, D_MODEL), 1.0),
        'c_sample': nrm(ks[7], (DEC_BATCH, D_MODEL), 1.0),
        'w_ada': nrm(ks[9], (DEPTH, D_MODEL, 9 * D_MODEL), D_MODEL ** -0.5),
        'b_ada': nrm(ks[10], (DEPTH, 9 * D_MODEL), 0.02),
        'ffn1_wg': nrm(ks[11], (DEPTH, D_MODEL, D_FF), D_MODEL ** -0.5),
        'ffn1_wu': nrm(ks[12], (DEPTH, D_MODEL, D_FF), D_MODEL ** -0.5),
        'ffn1_wd': nrm(ks[13], (DEPTH, D_FF, D_MODEL), D_FF ** -0.5 * DEEPNORM_BETA),
        'w_in': w_in,
        'w_dw': nrm(ks[14], (DEPTH, CONV_K, CONV_CH), CONV_K ** -0.5),
        'b_dw': nrm(ks[15], (DEPTH, CONV_CH), 0.02),
        'gn_g': 1.0 + nrm(ks[16], (DEPTH, CONV_CH), 0.05),
        'gn_b': nrm(ks[17], (DEPTH, CONV_CH), 0.02),
        'beta_attn': 1.0 + nrm(ks[18], (DEPTH, ATTN_WIDTH), 0.05),
        'beta_conv': 1.0 + nrm(ks[19], (DEPTH, CONV_CH), 0.05),
        'w_out': nrm(ks[20], (DEPTH, MIX_WIDTH, D_MODEL), MIX_WIDTH ** -0.5 * DEEPNORM_BETA),
        'ffn2_wg': nrm(ks[21], (DEPTH, D_MODEL, D_FF), D_MODEL ** -0.5),
        'ffn2_wu': nrm(ks[22], (DEPTH, D_MODEL, D_FF), D_MODEL ** -0.5),
        'ffn2_wd': nrm(ks[23], (DEPTH, D_FF, D_MODEL), D_FF ** -0.5 * DEEPNORM_BETA),
        'ln_g': 1.0 + nrm(ks[24], (DEPTH, 3, D_MODEL), 0.05),
        'ln_b': nrm(ks[25], (DEPTH, 3, D_MODEL), 0.02),
    }

def reference(x_prompt, x_sample, cache_k, cache_v, state_conv, page_table, c_prompt, c_sample,
              w_ada, b_ada, ffn1_wg, ffn1_wu, ffn1_wd, w_in, w_dw, b_dw, gn_g, gn_b,
              beta_attn, beta_conv, w_out, ffn2_wg, ffn2_wu, ffn2_wd, ln_g, ln_b):
    slopes = _alibi_slopes()
    y_prompt, y_sample = x_prompt, x_sample
    kp_l, vp_l, cp_l, ks_l, vs_l, cs_l = [], [], [], [], [], []
    for l in range(DEPTH):
        def mixer_prompt(h, l=l):
            q, k, v, glu = _project(h, w_in[l])
            attn = _moba_prompt(q, k, v, slopes)
            buf = jnp.pad(glu, ((0, 0), (CONV_K - 1, 0), (0, 0)))
            conv = _conv_branch(buf, w_dw[l], b_dw[l], gn_g[l], gn_b[l])
            return _merge(attn, conv, beta_attn[l], beta_conv[l], w_out[l]), (k, v, glu[:, -(CONV_K - 1):])

        def mixer_sample(h, l=l):
            q, k, v, glu = _project(h, w_in[l])
            attn = _moba_sample(q, k, v, cache_k[l], cache_v[l], page_table, slopes)
            buf = jnp.concatenate([state_conv[l].astype(glu.dtype), glu], axis=1)
            conv = _conv_branch(buf, w_dw[l], b_dw[l], gn_g[l], gn_b[l])
            return _merge(attn, conv, beta_attn[l], beta_conv[l], w_out[l]), (k, v, buf[:, -(CONV_K - 1):])

        y_prompt, (kp, vp, cp) = _trunk_layer(y_prompt, c_prompt, mixer_prompt, w_ada[l], b_ada[l],
                                              ffn1_wg[l], ffn1_wu[l], ffn1_wd[l], ffn2_wg[l], ffn2_wu[l], ffn2_wd[l],
                                              ln_g[l], ln_b[l])
        y_sample, (ksm, vsm, csm) = _trunk_layer(y_sample, c_sample, mixer_sample, w_ada[l], b_ada[l],
                                                 ffn1_wg[l], ffn1_wu[l], ffn1_wd[l], ffn2_wg[l], ffn2_wu[l], ffn2_wd[l],
                                                 ln_g[l], ln_b[l])
        b, h, s, dh = kp.shape
        kp_l.append(kp.reshape(b, h, s // PAGE_SIZE, PAGE_SIZE, dh).transpose(0, 2, 1, 3, 4))
        vp_l.append(vp.reshape(b, h, s // PAGE_SIZE, PAGE_SIZE, dh).transpose(0, 2, 1, 3, 4))
        cp_l.append(cp)
        ks_l.append(ksm)
        vs_l.append(vsm)
        cs_l.append(csm)
    k_prompt_new = jnp.stack(kp_l, 0)
    v_prompt_new = jnp.stack(vp_l, 0)
    conv_prompt_new = jnp.stack(cp_l, 0)
    k_sample_new = jnp.stack(ks_l, 0)
    v_sample_new = jnp.stack(vs_l, 0)
    conv_sample_new = jnp.stack(cs_l, 0)
    return (y_prompt, y_sample, k_prompt_new, v_prompt_new, conv_prompt_new, k_sample_new, v_sample_new, conv_sample_new)


_drawn_inputs = setup_inputs


def setup_inputs(seed=0):
    import zlib

    import numpy as np

    out = dict(_drawn_inputs(seed))
    spreads = {}
    factors = {'b_dw': 8.0, 'gn_g': 7.606, 'gn_b': 22.089, 'beta_attn': 64.0, 'beta_conv': 8.0}
    for name, (base, spread) in spreads.items():
        noise = np.random.default_rng([zlib.crc32(name.encode()), seed]).standard_normal(out[name].shape)
        drawn = base * np.exp(spread * noise) if base else spread * noise
        out[name] = __import__('jax').numpy.asarray(drawn.astype(out[name].dtype))
    for name, factor in factors.items():
        out[name] = (out[name] * factor).astype(out[name].dtype)
    return out
```

```python
from contextlib import ExitStack

import numpy as np

import concourse.bass as bass
from concourse import mybir

F32 = mybir.dt.float32
F32R = mybir.dt.float32r
I32 = mybir.dt.int32
U32 = mybir.dt.uint32
ALU = mybir.AluOpType
ACT = mybir.ActivationFunctionType
AX = mybir.AxisListType.X

P = 128
D = 1024
NCH = D // P
SEQ = 256
DB, DT = 8, 8
NS = DB * DT
T = SEQ + NS
NH, HD = 8, 64
AW = NH * HD
NHP = AW // P
CC = 512
NCC = CC // P
TAPS = 31
ST = TAPS - 1
PAST, PAGE, BLK = 2048, 128, 256
NPG = PAST // PAGE
NBLK = PAST // BLK
NPOOL = 160
FF = 2816
NF = FF // P
ALPHA = 2.0 ** 0.25
EPS = 1e-5
NEG = -1e30
UC = 256
RING = 4
UMAX = NF // 2 * UC
CB = ST + SEQ + DB * (ST + DT)
SB = ST + DT
QPITCH = P + DT
QB = 64 + P + DT + NHP * 2 * QPITCH

C_ID, C_LN, C_GN, C_REL, C_SEL = 0, P, 2 * P, 3 * P, 6 * P
C_POS = C_SEL + 16
C_OWN = C_POS + P
C_IOTA = C_OWN + 120
C_RC = C_IOTA + 8
C_M = C_RC + 8
C_EPS = C_M + 1
C_SUM = C_EPS + 1
C_SWAP = C_SUM + P
C_N = C_SWAP + P


def constants():
    c = np.zeros((P, C_N), np.float32)
    p = np.arange(P)
    c[:, C_ID:C_ID + P] = np.eye(P)
    c[:, C_LN:C_LN + P] = 1.0 / D
    c[:, C_GN:C_GN + P] = (p[:, None] // 64 == p[None, :] // 64) / 64.0
    for at, q0, keys in ((0, 0, P), (P, P, 2 * P)):
        rel = np.arange(keys)[None, :] - (q0 + p[:, None])
        c[:, C_REL + at:C_REL + at + keys] = np.where(rel <= 0, rel, -3e34)
    for r in range(18):
        c[r, C_SEL + r % 9] = 1.0
    c[:, C_POS:C_POS + P] = (p // 64 * P + 2 * (p % 64))[None, :]
    r, h, t = p // 64, p % 64 // 8, p % 8
    m = 2.0 ** (-(h + 1.0))
    key = np.arange(120) - 56
    ok = (key[None, :] >= 0) & (key[None, :] <= t[:, None]) & (r[:, None] == 0)
    c[:, C_OWN:C_OWN + 120] = np.where(ok, m[:, None] * (key[None, :] - t[:, None]), NEG)
    c[:, C_IOTA:C_IOTA + 8] = np.arange(8)[None, :]
    c[:, C_RC:C_RC + 8] = m[:, None] * (BLK * np.arange(8)[None, :] - PAST + (r - t)[:, None])
    c[:, C_M] = m
    c[:, C_EPS] = EPS
    c[:, C_SUM:C_SUM + P] = p[:, None] % 64 == p[None, :] % 64
    c[:, C_SWAP:C_SWAP + P] = (p[:, None] + 64) % P == p[None, :]
    return c


ADA, UP1, DN1, WIN, WOUT, UP2, DN2 = (0, 0, 36), (36, 36, 22), (58, 58, 8), (66, 66, 10), (76, 140, 4), (80, 144, 22), (102, 166, 8)
KV0, KVN = 76, 64
WIN_ORDER = [8, 9, 6, 7, 2, 3, 4, 5, 0, 1]
MIX_ORDER = [4, 5, 6, 7, 0, 1, 2, 3]


def raw_count(turn):
    before = KV0 // RING
    return 16 * (turn + 1) if turn < before else 16 * (turn + 1 - KVN // RING) + 64 * (KVN // RING)


def raw_count_w(phase, u, turns=0):
    return raw_count((phase[1] + u) // RING) + 16 * turns


def raw_count_kv(kvi, turns=0):
    return 16 * (KV0 // RING) + 64 * (kvi // RING + 1) + 64 * turns


def build(nc, i, o):
    es = ExitStack()
    with es:
        def sb(name, shape, dt=F32, stack=es):
            return stack.enter_context(nc.sbuf_tensor(name, shape, dt))

        def sem(name):
            return es.enter_context(nc.semaphore(name))

        bank = es.enter_context(nc.psum_tensor("bank", [P, 8, 512], F32))
        con = sb("con", [P, C_N])
        xT = sb("xT", [P, NCH, T])
        yT = sb("yT", [P, NCH, T])
        mh = sb("mh", [P, NCH, T], F32R)
        ml = sb("ml", [P, NCH, T], F32R)
        adaT = sb("adaT", [P, 72, 9])
        raw = sb("raw", [P, RING, UMAX])
        whi = sb("whi", [P, 2, UMAX], F32R)
        wlo = sb("wlo", [P, 2, UMAX], F32R)
        par1 = sb("par1", [P, 120])
        par2 = sb("par2", [P, 20])
        dwT = sb("dwT", [P, TAPS * NCC])
        cT = sb("cT", [P, 72])
        chl = sb("chl", [P, NCH, 18], F32R)
        pages = sb("pages", [1, DB * NPG], I32)
        tmp = sb("tmp", [P, 4, T])
        rows = tmp[:, :, :].rearrange("p a t -> p (a t)")[0:18, 0:2 * UC].rearrange("p (s c) -> p s c", s=2)

        with ExitStack() as scope:
            hh = sb("hh", [P, NF, T], F32R, scope)
            hl = sb("hl", [P, NF, T], F32R, scope)
        with ExitStack() as scope:
            xrow = sb("xrow", [P, 3, D], F32, scope)
            prow = sb("prow", [P, 4, P], F32, scope)
        with ExitStack() as scope:
            yrow = sb("yrow", [P, 3, D], F32, scope)
        with ExitStack() as scope:
            uT = sb("uT", [P, 12, T], F32, scope)
            cbuf = sb("cbuf", [P, NCC, CB], F32, scope)
            s = sb("s", [P, 2, PAST // 2 + NS], F32, scope)
            pT = sb("pT", [P, 2 * NBLK * P], F32, scope)
            po = sb("po", [NS, 2 * P], F32, scope)
            qbh = sb("qbh", [P, QB], F32R, scope)
            qbl = sb("qbl", [P, QB], F32R, scope)
            koh = sb("koh", [P, NH, NS], F32R, scope)
            kol = sb("kol", [P, NH, NS], F32R, scope)
            vtok = sb("vtok", [P, 2, AW], F32, scope)
            vsam = sb("vsam", [NS, AW], F32, scope)
            gsum = sb("gsum", [P, 2, 8], F32, scope)
            gate = sb("gate", [P, 2, 8], F32, scope)
            gmax = sb("gmax", [P, 2, 8], F32, scope)
            gidx = sb("gidx", [P, 2, 8], U32, scope)
            gidf = sb("gidf", [P, 2, 8], F32, scope)
            hit = sb("hit", [P, 2, 8, 3], F32, scope)
            ebase = sb("ebase", [P, 2, 8], F32, scope)
            bmax = sb("bmax", [P, 2, 9], F32, scope)
            nmax = sb("nmax", [P, 2], F32, scope)
            ebias = sb("ebias", [P, 2], F32, scope)
            rt = sb("rt", [P, 2], F32, scope)
            ri = sb("ri", [P, 2], F32, scope)
            aodd = sb("aodd", [P, NHP, 2, DT], F32, scope)
            pm = sb("pm", [P, 2, 2], F32, scope)
            pz = sb("pz", [P, 2, 2], F32, scope)
            pr = sb("pr", [P, 2, 2], F32, scope)
        khn, kln, qh, ql = (t_[:, n, 0:NHP * NS].rearrange("p (m t) -> p m t", m=NHP)
                            for t_, n in ((mh, 0), (ml, 0), (mh, 1), (ml, 1)))
        sflat = s[:, :, :].rearrange("p b c -> p (b c)")
        strow = pT[0:4 * ST, 0:2 * CC].rearrange("p (g c) -> p g c", g=2)
        ps_ = sflat[:, 0:768].rearrange("p (a c) -> p a c", a=2)
        ksam = sflat[0:NS, 768:768 + AW]
        cout = sflat[0:ST, 1280:1280 + CC]
        ppT = pT[:, 0:768].rearrange("p (a c) -> p a c", a=2)
        ktok = pT[:, 1024:2048].rearrange("p (g c) -> p g c", g=2)
        csam = tmp[:, :, :].rearrange("p a t -> p (a t)")[0:NS, 2 * T:2 * T + CC]
        gsam = yT[:, 0, 0:NCC * NS].rearrange("p (c k) -> p c k", c=NCC)
        kh = whi[:, :, 0:2048].rearrange("p s (m c) -> p s m c", m=NHP)
        kl = wlo[:, :, 0:2048].rearrange("p s (m c) -> p s m c", m=NHP)

        ident = con[:, C_ID:C_ID + P]
        lnones = con[:, C_LN:C_LN + P]
        gnones = con[:, C_GN:C_GN + P]

        ld_con, ld_par, ld_x, ld_pages, ld_state = sem("ld_con"), sem("ld_par"), sem("ld_x"), sem("ld_pages"), sem("ld_state")
        raw_in = [sem(f"raw_in{k}") for k in range(RING)]
        w_hi, w_lo, w_used = sem("w_hi"), sem("w_lo"), sem("w_used")
        par_t, x_t, c_silu, c_hi, c_lo, par_ready, x_in = (sem(n) for n in ("par_t", "x_t", "c_silu", "c_hi", "c_lo", "par_ready", "x_in"))
        ada_row, ada_t, ada_out = (sem(n) for n in ("ada_row", "ada_t", "ada_out"))
        m_ready, mh_ready, ml_ready, ax_ready, y_ready = (sem(n) for n in ("m_ready", "mh_ready", "ml_ready", "ax_ready", "y_ready"))
        mean_ready, yc_ready, sq_ready, sq_used, var_ready, std_ready, xn_ready, x_ready = (
            sem(n) for n in ("mean_ready", "yc_ready", "sq_ready", "sq_used", "var_ready", "std_ready", "xn_ready", "x_ready"))
        g_ready = [sem("g_ready1"), sem("g_ready2")]
        silu_ready = [sem("silu_ready1"), sem("silu_ready2")]
        u_ready = [sem("u_ready1"), sem("u_ready2")]
        h_ready = [sem("h_ready1"), sem("h_ready2")]
        hh_ready = [sem("hh_ready1"), sem("hh_ready2")]
        hl_ready = [sem("hl_ready1"), sem("hl_ready2")]
        n_ready = sem("n_ready")
        dve_step, act_step, pool_step = sem("dve_step"), sem("act_step"), sem("pool_step")
        win_mm, sig_ready, glu_ready, u_out = (sem(n) for n in ("win_mm", "sig_ready", "glu_ready", "u_out"))
        tok_t, tok_out, st_t, st_in, gl_t, gl_out = (sem(n) for n in ("tok_t", "tok_out", "st_t", "st_in", "gl_t", "gl_out"))
        pad_ready, conv_ready = sem("pad_ready"), sem("conv_ready")
        ps_mm, ps_ready, pmax_ready, pexp, pp_ready, pp_t, pp_out, pv_mm, pv_out = (
            sem(n) for n in ("ps_mm", "ps_ready", "pmax_ready", "pexp", "pp_ready", "pp_t", "pp_out", "pv_mm", "pv_out"))
        ko_hi, ko_lo, q_zero, q_hi, q_lo = (
            sem(n) for n in ("ko_hi", "ko_lo", "q_zero", "q_hi", "q_lo"))
        qs_hi, qs_lo, gs_copy, gsum_ready, gate_mm, nmax_ready, swap_mm, rsum_mm = (
            sem(n) for n in ("qs_hi", "qs_lo", "gs_copy", "gsum_ready", "gate_mm", "nmax_ready", "swap_mm", "rsum_mm"))
        kt_ready, kt_hi, kt_lo, k_used, s_evac, own_ready, eb_ready, ex_ready, p_ready, pt_ready, pt_evac, v_used, av_evac = (
            sem(n) for n in ("kt_ready", "kt_hi", "kt_lo", "k_used", "s_evac", "own_ready", "eb_ready", "ex_ready", "p_ready",
                             "pt_ready", "pt_evac", "v_used", "av_evac"))
        gm_mm, gc_ready, gq_ready, gv_mm, gs_ready, gx_ready, gy_ready = (
            sem(n) for n in ("gm_mm", "gc_ready", "gq_ready", "gv_mm", "gs_ready", "gx_ready", "gy_ready"))
        out_t, out_row, stored = sem("out_t"), sem("out_row"), sem("stored")
        stored_early = sem("stored_early")
        N_EARLY = 1 + 3 * DB + 4

        block = es.enter_context(nc.Block())

        def up_pairs(eng, body):
            body(0, 0)
            with eng.Fori(0, 4) as g:
                body(1 + 2 * g, 1)
                body(2 + 2 * g, 2)
            body(9, 9)
            body(10, 10)

        @block.sync
        def _(sp):
            sp.dma_start(con[:, :], i["consts"]).then_inc(ld_con, 16)
            sp.dma_start(prow[0:72, 0, :], i["b_ada"].rearrange("o (r f) -> (o r) f", f=P)).then_inc(ld_par, 16)
            sp.dma_start(prow[72:96, 0, :], i["ln_g"].rearrange("o j (r f) -> (o j r) f", f=P)).then_inc(ld_par, 16)
            sp.dma_start(prow[96:120, 0, :], i["ln_b"].rearrange("o j (r f) -> (o j r) f", f=P)).then_inc(ld_par, 16)
            for n, name in enumerate(("b_dw", "gn_g", "gn_b", "beta_attn", "beta_conv")):
                sp.dma_start(prow[4 * n:4 * n + 4, 1, :], i[name].rearrange("o (r f) -> (o r) f", f=P)).then_inc(ld_par, 16)
            sp.dma_start(prow[0:TAPS * NCC, 2, :], i["w_dw"].rearrange("o k (r f) -> (o k r) f", f=P)).then_inc(ld_par, 16)
            sp.dma_start(prow[0:8, 3, :], i["c_prompt"].rearrange("b (r f) -> (b r) f", f=P)).then_inc(ld_par, 16)
            sp.dma_start(prow[8:72, 3, :], i["c_sample"].rearrange("b (r f) -> (b r) f", f=P)).then_inc(ld_par, 16)

            def slot_of(phase, u):
                return (phase[1] + u) % RING

            def load(phase, u, src, size, wait, turns=0):
                if wait is not None:
                    sp.wait_ge(*wait)
                k = slot_of(phase, u)
                sp.dma_start(raw[:, k, 0:size].rearrange("p (k c) -> p k c", c=UC), src).then_inc(raw_in[k], 16)

            def w_free(phase, u):
                return (w_lo, phase[0] + u - RING + 1)

            def cols(w, c):
                return w[0].rearrange("(k p) c -> p k c", p=P)[:, :, c]

            for u in range(4):
                load(ADA, u, cols(i["w_ada"], slice(UC * u, UC * u + UC)), NCH * UC, None)
            sp.dma_start(xrow[:, 0:2, :], i["x_prompt"][0].rearrange("(t p) f -> p t f", p=P)).then_inc(ld_x, 16)
            sp.dma_start(xrow[0:NS, 2, :], i["x_sample"].rearrange("b t f -> (b t) f")).then_inc(ld_x, 16)
            sp.dma_start(pages[:, :], i["page_table"].rearrange("b n -> (b n)").unsqueeze(0)).then_inc(ld_pages, 16)
            sp.dma_start(o["conv_sample_new"][0, :, 0:ST - DT, :], i["state_conv"][0, :, DT:ST, :]).then_inc(stored, 16)
            with sp.Fori(1, ADA[2] // RING) as turn:
                for k in range(RING):
                    u = RING * turn + k
                    load(ADA, k, cols(i["w_ada"], bass.ds(UC * u, UC)), NCH * UC, w_free(ADA, u))

            def load_up(phase, ffn):
                def body(pair, pair_):
                    for x, w in enumerate((i[f"ffn{ffn}_wg"], i[f"ffn{ffn}_wu"])):
                        load(phase, 2 * pair_ + x, cols(w, bass.ds(UC * pair, UC)), NCH * UC, w_free(phase, 2 * pair + x))
                up_pairs(sp, body)

            def load_down(phase, ffn):
                w = i[f"ffn{ffn}_wd"][0].rearrange("(h k p) c -> p h k c", p=P, h=2)
                for u in range(8):
                    load(phase, u, w[:, u % 2, :, UC * (u // 2):UC * (u // 2) + UC], UMAX, w_free(phase, u))

            load_up(UP1, 1)
            load_down(DN1, 1)
            for u, b in enumerate(WIN_ORDER):
                load(WIN, u, cols(i["w_in"], slice(UC * b, UC * b + UC)), NCH * UC, w_free(WIN, u))
            sp.wait_ge(w_used, DN1[0] + 8)
            for g in range(2):
                sp.dma_start(strow[:, g, :], i["state_conv"][0, 4 * g:4 * g + 4].rearrange("b k c -> (b k) c")).then_inc(ld_state, 16)
            sp.wait_ge(ld_pages, 16)

            def load_pages(cache, seq, c, k, wait):
                sp.wait_ge(*wait)
                for x in range(4):
                    page = sp.value_load(pages[0:1, bass.ds(NPG * seq + 4 * c + x, 1)], min_val=0, max_val=NPOOL - 1)
                    sp.dma_start(raw[64 * (x % 2):64 * (x % 2) + 64, k % RING, 1024 * (x // 2):1024 * (x // 2) + 1024]
                                 .rearrange("p (h f) -> p h f", h=NH),
                                 cache[0][bass.ds(page, 1)].rearrange("a h (p r) d -> p (a h) (r d)", r=2)).then_inc(raw_in[k % RING], 16)

            for k in range(8):
                load_pages(i["cache_k"], k // 4, k % 4, k,
                           (w_lo, WIN[0] + WIN[2] - RING + k + 1) if k < RING else (kt_ready, 2 * (k - RING) + 2))

            def kv_round(j, j_is_1):
                for k in range(8):
                    if k >= RING:
                        wait = (kt_ready, 16 * j + 2 * (k - RING) + 2)
                    elif j_is_1:
                        wait = (kt_ready, 2 * (k + RING) + 2)
                    else:
                        wait = (v_used, 8 * (j - 2) + k + RING + 1)
                    load_pages(i["cache_k"], 2 * j + k // 4, k % 4, k, wait)
                for k in range(8):
                    wait = (kt_ready, 16 * j + 2 * (k + RING) + 2) if k < RING else (v_used, 8 * (j - 1) + k - RING + 1)
                    load_pages(i["cache_v"], 2 * (j - 1) + k // 4, k % 4, k, wait)

            kv_round(1, True)
            with sp.Fori(2, 4) as j:
                kv_round(j, False)
            for k in range(8):
                load_pages(i["cache_v"], 6 + k // 4, k % 4, k, (v_used, 8 * 2 + k + RING + 1) if k < RING else (v_used, 24 + k - RING + 1))
            for u in range(WOUT[2]):
                load(WOUT, u, cols(i["w_out"], slice(UC * u, UC * u + UC)), NCH * UC, (v_used, 24 + RING + u + 1))
            load_up(UP2, 2)
            load_down(DN2, 2)
            for tt in range(3):
                n = P if tt < 2 else NS
                sp.wait_ge(out_row, 2 * tt + 2)
                dst = o["y_prompt"][0, P * tt:P * tt + P, :] if tt < 2 else o["y_sample"].rearrange("b t f -> (b t) f")
                sp.dma_start(dst, yrow[0:n, tt, :]).then_inc(stored, 16)
            sp.wait_ge(stored, 16 * (1 + 3))
            sp.wait_ge(stored_early, 16 * N_EARLY)

        @block.gpsimd
        def _(pool):
            def scale_x(n):
                pool.wait_ge(m_ready, (8, 16, 32)[n])
                pool.tensor_scalar(xT[:, :, :], xT[:, :, :], ALPHA, None, ALU.mult).then_inc(ax_ready, 1)

            scale_x(0)
            pool.wait_ge(w_used, DN1[0] + 8)
            pool.memset(cbuf[:, :, 0:ST], 0.0).then_inc(pad_ready, 1)
            pool.memset(qbh[:, :].bitcast(F32), 0.0).then_inc(q_zero, 1)
            pool.memset(qbl[:, :].bitcast(F32), 0.0).then_inc(q_zero, 1)
            pool.memset(koh[:, :, :].bitcast(F32), 0.0).then_inc(q_zero, 1)
            pool.memset(kol[:, :, :].bitcast(F32), 0.0).then_inc(q_zero, 1)
            scale_x(1)
            pool.wait_ge(glu_ready, NCC)
            pool.wait_ge(st_in, 2)
            pool.wait_ge(pad_ready, 1)
            steps = 0
            for c in range(NCC):
                acc = yT[:, NCC + c, :]
                sam = cbuf[:, c, ST + SEQ:CB].rearrange("p (b k) -> p b k", b=DB)
                for k in range(TAPS):
                    w = dwT[:, NCC * k + c:NCC * k + c + 1]
                    to = acc if k == 0 else tmp[:, k % 2, :]
                    more = (par2[:, c:c + 1], ALU.mult, ALU.add) if k == 0 else (None, ALU.mult)
                    pool.tensor_scalar(to[:, 0:SEQ], cbuf[:, c, k:k + SEQ], w, *more)
                    pool.tensor_scalar(to[:, SEQ:T].rearrange("p (b t) -> p b t", b=DB), sam[:, :, k:k + DT], w, *more).then_inc(pool_step, 1)
                    steps += 1
                    if k:
                        pool.wait_ge(pool_step, steps)
                        last = k == TAPS - 1
                        pool.tensor_tensor(acc, acc, to, ALU.add).then_inc(conv_ready if last else pool_step, 1)
                        steps += not last
                pool.wait_ge(conv_ready, c + 1)
            scale_x(2)

        @block.scalar
        def _(act):
            def hi(phase, u, size=NCH * UC, more=0):
                k = (phase[1] + u) % RING
                act.wait_ge(raw_in[k], raw_count_w(phase, u) + 16 // RING * more)
                if phase[0] + u >= 2:
                    act.wait_ge(w_used, phase[0] + u - 1 + more)
                act.copy(whi[:, u % 2, 0:size], raw[:, k, 0:size]).then_inc(w_hi, 1)

            act.wait_ge(par_t, 1)
            act.activation(cT[:, :], bank[:, 1, 0:72], ACT.Silu).then_inc(c_silu, 1)
            act.wait_ge(c_silu, 1)
            act.copy(chl[:, :, 0:9].rearrange("p k r -> p r k"), cT[:, :].rearrange("p (r k) -> p r k", r=9)).then_inc(c_hi, 1)
            hi(ADA, 0)
            hi(ADA, 1)
            for n in range(6):
                act.wait_ge(x_t, n + 1)
                tt, half = n // 2, n % 2
                w = P if tt < 2 else NS
                act.copy(xT[:, 4 * half:4 * half + 4, P * tt:P * tt + w],
                         bank[:, 2 + n, :].rearrange("p (c t) -> p c t", t=P)[:, :, 0:w]).then_inc(x_in, 1)

            def ada_unit(u, u_, more=0):
                act.wait_ge(w_used, u + 1)
                if u_ >= 2:
                    act.wait_ge(ada_t, u - 1)
                act.copy(rows[:, u_ % 2, :], bank[0:18, u_ % 2, 0:UC]).then_inc(ada_row, 1)
                hi(ADA, u_ + 2, more=more)

            for u in range(4):
                ada_unit(u, u)
            with act.Fori(1, 9) as turn:
                for k in range(RING):
                    ada_unit(RING * turn + k, RING + k, RING * (turn - 1))

            def split_m(n0):
                for n in range(NCH):
                    act.wait_ge(m_ready, n0 + n + 1)
                    act.copy(mh[:, n, :], yT[:, n, :]).then_inc(mh_ready, 1)

            def up(ffn, phase, down):
                gr, sr, hr, hhr = g_ready[ffn], silu_ready[ffn], h_ready[ffn], hh_ready[ffn]

                def body(pair, pair_):
                    more = 2 * (pair - pair_)
                    for cc in range(2):
                        if cc == 0:
                            act.wait_ge(gr, pair + 1)
                        else:
                            act.wait_ge(w_used, phase[0] + 2 * pair + 1)
                        if pair_:
                            act.wait_ge(hr, 2 * pair + cc - 1)
                        act.activation(tmp[:, cc, :], bank[:, cc, 0:T], ACT.Silu).then_inc(sr, 1)
                    for x in range(2):
                        if pair_ < 10:
                            hi(phase, 2 * pair_ + 2 + x, more=more)
                        else:
                            hi(down, x, UMAX)
                    for cc in range(2):
                        act.wait_ge(hr, 2 * pair + cc + 1)
                        act.copy(hh[:, bass.ds(2 * pair + cc, 1), :].rearrange("p a t -> p (a t)"), tmp[:, 2 + cc, :]).then_inc(hhr, 1)
                up_pairs(act, body)

            def down(phase, nxt):
                for u in range(8):
                    if u < 6:
                        hi(phase, u + 2, UMAX)
                    elif nxt is not None:
                        hi(nxt, u - 6)

            def norm(n):
                for q in range(4):
                    act.wait_ge(yc_ready, 4 * n + q + 1)
                    if q >= 2:
                        act.wait_ge(sq_used, 3 * n + q - 1)
                    act.activation(tmp[:, 2 * (q % 2):2 * (q % 2) + 2, :], yT[:, 2 * q:2 * q + 2, :], ACT.Square).then_inc(sq_ready, 1)
                act.wait_ge(var_ready, n + 1)
                act.activation(tmp[:, 0, :], bank[:, 1, 0:T], ACT.Sqrt, bias=con[:, C_EPS:C_EPS + 1]).then_inc(std_ready, 1)
                for q in range(NCH):
                    act.wait_ge(xn_ready, 4 * n + q // 2 + 1)
                    act.activation(xT[:, q, :], yT[:, q, :], ACT.Identity, scale=par1[:, 72 + 8 * n + q:73 + 8 * n + q],
                                   bias=par1[:, 96 + 8 * n + q:97 + 8 * n + q]).then_inc(x_ready, 1)
                    if n < 2 and q >= 1:
                        act.wait_ge(m_ready, 8 * (1 + 2 * n) + q)
                        act.copy(mh[:, q - 1, :], yT[:, q - 1, :]).then_inc(mh_ready, 1)
                if n < 2:
                    act.wait_ge(m_ready, 8 * (2 + 2 * n))
                    act.copy(mh[:, 7, :], yT[:, 7, :]).then_inc(mh_ready, 1)

            split_m(0)
            up(0, UP1, DN1)
            down(DN1, WIN)
            norm(0)

            for u, b in enumerate(WIN_ORDER):
                for cc in range(2):
                    act.wait_ge(*((win_mm, u + 1) if cc == 0 else (w_used, WIN[0] + u + 1)))
                    c = 2 * b + cc
                    src = bank[:, 2 * (u % 2) + cc, 0:T]
                    if c >= 16:
                        act.activation(yT[:, c - 16, :], src, ACT.Sigmoid).then_inc(sig_ready, 1)
                    elif c < 4:
                        act.mul(uT[:, c, :], src, HD ** -0.5).then_inc(u_out, 1)
                    elif c < 12:
                        act.copy(uT[:, c, :], src).then_inc(u_out, 1)
                if u < 8:
                    hi(WIN, u + 2)

            for g in range(2):
                act.wait_ge(st_t, g + 1)
                act.copy(cbuf[:, :, ST + SEQ + 4 * g * SB:ST + SEQ + 4 * (g + 1) * SB].rearrange("p c (b k) -> p c b k", b=4)[:, :, :, 0:ST],
                         bank[:, 4 + g, 0:480].rearrange("p (c b k) -> p c b k", c=NCC, b=4)).then_inc(st_in, 1)
            dst = [vtok[:, 0, :], vtok[:, 1, :], vsam[:, :], ktok[:, 0, :], ktok[:, 1, :], ksam]
            for n in range(6):
                act.wait_ge(tok_t, n + 1)
                w = P if n % 3 < 2 else NS
                act.copy(dst[n], bank[0:w, n % 4, :]).then_inc(tok_out, 1)
            act.wait_ge(glu_ready, NCC)
            act.copy(gsam.rearrange("p c (b t) -> p c b t", b=DB),
                     cbuf[:, :, ST + SEQ:CB].rearrange("p c (b k) -> p c b k", b=DB)[:, :, :, ST:SB]).then_inc(gs_copy, 1)
            act.wait_ge(gl_t, 1)
            act.copy(cout, bank[0:ST, 6, :]).then_inc(gl_out, 1)
            act.wait_ge(gl_t, 2)
            act.copy(csam, bank[0:NS, 7, :]).then_inc(gl_out, 1)
            act.wait_ge(u_out, 12)
            act.wait_ge(q_zero, 4)
            act.copy(khn, uT[:, 4:8, SEQ:T])
            act.copy(qh, uT[:, 0:NHP, SEQ:T]).then_inc(qs_hi, 1)
            act.wait_ge(qs_hi, 1)
            for e in range(2):
                ins = act.copy(koh[0:64, :, :].rearrange("p (m e) t -> p m e t", e=2)[:, :, e, :], khn[64 * e:64 * e + 64, :, :].bitcast(F32))
            ins.then_inc(ko_hi, 1)
            act.wait_ge(tok_out, 6)
            act.wait_ge(gl_out, 2)
            for t_, name in ((vtok, "v_prompt_new"), (ktok, "k_prompt_new")):
                for pg in range(2):
                    act.dma_start(o[name][0, 0, pg].rearrange("h p d -> p h d"), t_[:, pg, :].rearrange("p (h d) -> p h d", h=NH)).then_inc(stored_early, 16)
            for b in range(DB):
                r = slice(DT * b, DT * b + DT)
                act.dma_start(o["v_sample_new"][0, b].rearrange("h t d -> t h d"), vsam[r, :].rearrange("t (h d) -> t h d", h=NH)).then_inc(stored_early, 16)
                act.dma_start(o["k_sample_new"][0, b].rearrange("h t d -> t h d"), ksam[r, :].rearrange("t (h d) -> t h d", h=NH)).then_inc(stored_early, 16)
                act.dma_start(o["conv_sample_new"][0, b, ST - DT:ST, :], csam[r, :]).then_inc(stored_early, 16)
            act.dma_start(o["conv_prompt_new"][0, 0], cout).then_inc(stored_early, 16)

            def prompt_exp(h):
                act.wait_ge(pmax_ready, h + 1)
                for q, (a, b) in enumerate(((0, P), (P, 3 * P))):
                    ins = act.activation(ps_[:, h % 2, a:b], ps_[:, h % 2, a:b], ACT.Exp, bias=pm[:, h % 2, q:q + 1],
                                         accum_out=pz[:, h % 2, q:q + 1])
                ins.then_inc(pexp, 1)

            def prompt_turned(h):
                act.wait_ge(pp_t, h + 1)
                if h >= 2:
                    act.wait_ge(pv_mm, h - 1)
                act.copy(ppT[:, h % 2, :], bank[:, 2 + h % 2, 0:384]).then_inc(pp_out, 1)
                if h % 2:
                    act.wait_ge(pv_mm, h + 1)
                    act.copy(yT[:, h // 2, 0:SEQ], bank[:, 4 + h // 2 % 2, 0:SEQ]).then_inc(pv_out, 1)

            for h in range(NH):
                prompt_exp(h)
                if h:
                    prompt_turned(h - 1)
            prompt_turned(NH - 1)

            def q_high(j, b2, first=False):
                if first:
                    act.wait_ge(qs_hi, 1)
                elif b2:
                    act.wait_ge(own_ready, 2 * j + 1)
                else:
                    act.wait_ge(own_ready, 2 * j)
                for r in range(2):
                    for e in range(2):
                        at = 64 * r + QPITCH * e
                        ins = act.copy(qbh[64 * r:64 * r + 64, at:at + NHP * 2 * QPITCH].rearrange("p (m c) -> p m c", m=NHP)[:, :, 0:DT],
                                       qh[64 * e:64 * e + 64, :, bass.ds(DT * (2 * j + b2), DT)].bitcast(F32))
                ins.then_inc(q_hi, 1)

            q_high(0, 0, True)

            def pair_body(j, first=False, last=False):
                for k in range(8):
                    for hf in range(2):
                        act.wait_ge(kt_ready, 16 * j + 2 * k + hf + 1)
                        if hf == 0 and not (first and k < 2):
                            act.wait_ge(k_used, 8 * j + k - 1)
                        act.copy(kh[:, k % 2, 2 * hf:2 * hf + 2, :], bank[:, 2 * hf:2 * hf + 2, :]).then_inc(kt_hi, 1)
                    if k == 4:
                        q_high(j, 1)
                act.wait_ge(eb_ready, j + 1)
                for b2 in range(2):
                    ins = act.activation(s[:, b2, :], s[:, b2, :], ACT.Exp, bias=ebias[:, b2:b2 + 1], accum_out=rt[:, b2:b2 + 1])
                ins.then_inc(ex_ready, 1)
                if not last:
                    q_high(j + 1, 0)
                for r in range(4):
                    act.wait_ge(pt_ready, 5 * j + r + 1)
                    act.copy(pT[:, 512 * r:512 * r + 512], bank[:, 4 + r % 2, :]).then_inc(pt_evac, 1)
                act.wait_ge(pt_ready, 5 * j + 5)
                act.copy(po[:, :], bank[0:NS, 6, 0:2 * P]).then_inc(pt_evac, 1)

            act.wait_ge(stored_early, 16 * N_EARLY)
            pair_body(0, first=True)
            with act.Fori(1, 3) as j:
                pair_body(j)
            pair_body(3, last=True)

            for c in range(NCC):
                act.wait_ge(gc_ready, c + 1)
                act.activation(tmp[:, c, :], yT[:, NCC + c, :], ACT.Square).then_inc(gq_ready, 1)
            for c in range(NCC):
                act.wait_ge(gv_mm, c + 1)
                act.activation(tmp[:, c, :], bank[:, c, 0:T], ACT.Sqrt, bias=con[:, C_EPS:C_EPS + 1]).then_inc(gs_ready, 1)
            for c in range(NCC):
                act.wait_ge(gx_ready, c + 1)
                act.activation(tmp[:, c, :], yT[:, NCC + c, :], ACT.Silu, scale=par2[:, 4 + c:5 + c], bias=par2[:, 8 + c:9 + c]).then_inc(gy_ready, 1)
            for n, c in enumerate(MIX_ORDER):
                act.wait_ge(m_ready, 16 + n + 1)
                act.copy(mh[:, c, :], yT[:, c, :]).then_inc(mh_ready, 1)
                if n == NCC - 1:
                    act.wait_ge(k_used, 32)
                    hi(WOUT, 0)
                    hi(WOUT, 1)
            for u in range(WOUT[2]):
                if u < 2:
                    hi(WOUT, u + 2)
                else:
                    hi(UP2, u - 2)
            norm(1)
            up(1, UP2, DN2)
            down(DN2, None)
            norm(2)
            for n in range(6):
                act.wait_ge(out_t, n + 1)
                tt, half = n // 2, n % 2
                w = P if tt < 2 else NS
                act.copy(yrow[0:w, tt, 512 * half:512 * half + 512], bank[0:w, 2 + n, :]).then_inc(out_row, 1)

        @block.vector
        def _(dve):
            step = [0]

            def link(ins):
                ins.then_inc(dve_step, 1)
                step[0] = step[0] + 1
                dve.wait_ge(dve_step, step[0])

            def lo(phase, u, size=NCH * UC, more=0):
                k = (phase[1] + u) % RING
                dve.wait_ge(w_hi, phase[0] + u + 1 + more)
                dve.tensor_tensor(wlo[:, u % 2, 0:size], raw[:, k, 0:size], whi[:, u % 2, 0:size].bitcast(F32), ALU.subtract).then_inc(w_lo, 1)

            dve.wait_ge(par_t, 1)
            dve.tensor_copy(par1[:, :], bank[:, 0, 0:120]).then_inc(par_ready, 1)
            dve.tensor_copy(par2[:, :], bank[:, 0, 128:148])
            dve.tensor_copy(dwT[:, :], bank[:, 0, 256:380]).then_inc(par_ready, 1)
            dve.wait_ge(par_ready, 2)
            one = par1[:, 0:72].rearrange("p (a b n) -> p a b n", a=3, b=3)[:, :, 1, :]
            link(dve.tensor_scalar(one, one, 1.0, None, ALU.add))
            dve.wait_ge(c_hi, 1)
            dve.tensor_tensor(chl[:, :, 9:18].rearrange("p k r -> p r k"), cT[:, :].rearrange("p (r k) -> p r k", r=9),
                              chl[:, :, 0:9].rearrange("p k r -> p r k").bitcast(F32), ALU.subtract).then_inc(c_lo, 1)
            lo(ADA, 0)
            lo(ADA, 1)

            def ada_turn(u, u_):
                dve.wait_ge(ada_t, u + 1)
                dve.tensor_tensor(adaT[:, bass.ds(2 * u, 2), :], bank[:, 2 + u_ % 2, 0:18].rearrange("p (c r) -> p c r", c=2),
                                  par1[:, bass.ds(2 * u, 2)].unsqueeze(2).to_broadcast([P, 2, 9]), ALU.add).then_inc(ada_out, 1)

            def ada_unit(u, u_, more=0):
                lo(ADA, u_ + 2, more=more)
                if u_ >= 1:
                    ada_turn(u - 1, u_ - 1)

            for u in range(4):
                ada_unit(u, u)
            with dve.Fori(1, 9) as turn:
                for k in range(RING):
                    ada_unit(RING * turn + k, RING + k, RING * (turn - 1))
            ada_turn(35, 35)
            dve.wait_ge(ada_out, 36)
            for sub in (0, 2):
                g = adaT[:, (3 * sub + 2) * NCH:(3 * sub + 3) * NCH, :]
                link(dve.tensor_scalar(g, g, 0.5, None, ALU.mult))

            def samples(ap):
                return ap[:, SEQ:T].rearrange("p (b t) -> p b t", b=DB)

            def vec(sub, kind, n):
                return adaT[:, (3 * sub + kind) * NCH + n, :]

            def per_seq(v):
                return v[:, 1:9].unsqueeze(2).to_broadcast([P, DB, DT])

            def modulate(sub, n, count):
                x, y = xT[:, n, :], yT[:, n, :]
                sc, sh = vec(sub, 1, n), vec(sub, 0, n)
                dve.tensor_scalar(y[:, 0:SEQ], x[:, 0:SEQ], sc[:, 0:1], sh[:, 0:1], ALU.mult, ALU.add)
                link(dve.tensor_tensor(samples(y), samples(x), per_seq(sc), ALU.mult))
                dve.tensor_tensor(samples(y), samples(y), per_seq(sh), ALU.add).then_inc(m_ready, 1)

            def low(n, count):
                dve.wait_ge(mh_ready, count)
                dve.tensor_tensor(ml[:, n, :], yT[:, n, :], mh[:, n, :].bitcast(F32), ALU.subtract).then_inc(ml_ready, 1)

            def add_residual(sub, n, src, ready):
                dve.wait_ge(*ready)
                g = vec(sub, 2, n)
                dve.scalar_tensor_tensor(yT[:, n, 0:SEQ], src[:, 0:SEQ], g[:, 0:1], xT[:, n, 0:SEQ], ALU.mult, ALU.add)
                link(dve.tensor_tensor(samples(yT[:, n, :]), samples(src), per_seq(g), ALU.mult))
                dve.tensor_tensor(samples(yT[:, n, :]), samples(yT[:, n, :]), samples(xT[:, n, :]), ALU.add).then_inc(y_ready, 1)

            def up(ffn, phase, down):
                sr, ur, hr, hhr, hlr = silu_ready[ffn], u_ready[ffn], h_ready[ffn], hh_ready[ffn], hl_ready[ffn]

                def low_next(pair, pair_, x):
                    if pair_ < 10:
                        lo(phase, 2 * pair_ + 2 + x, more=2 * (pair - pair_))
                    else:
                        lo(down, x, UMAX)

                def body(pair, pair_):
                    low_next(pair, pair_, 0)
                    for cc in range(2):
                        dve.wait_ge(sr, 2 * pair + cc + 1)
                        dve.wait_ge(*((ur, pair + 1) if cc == 0 else (w_used, phase[0] + 2 * pair + 2)))
                        if pair_:
                            dve.wait_ge(hlr, 2 * pair + cc - 1)
                        dve.tensor_tensor(tmp[:, 2 + cc, :], bank[:, 2 + cc, 0:T], tmp[:, cc, :], ALU.mult).then_inc(hr, 1)
                    low_next(pair, pair_, 1)
                    for cc in range(2):
                        dve.wait_ge(hhr, 2 * pair + cc + 1)
                        f = bass.ds(2 * pair + cc, 1)
                        dve.tensor_tensor(hl[:, f, :].rearrange("p a t -> p (a t)"), tmp[:, 2 + cc, :],
                                          hh[:, f, :].rearrange("p a t -> p (a t)").bitcast(F32), ALU.subtract).then_inc(hlr, 1)
                up_pairs(dve, body)

            def down(sub, phase, nxt, n0):
                dve.wait_ge(ax_ready, sub + 1)
                for u in range(8):
                    if u < 6:
                        lo(phase, u + 2, UMAX)
                    elif nxt is not None:
                        lo(nxt, u - 6)
                    if u % 2:
                        for cc in range(2):
                            n = u - 1 + cc
                            add_residual(sub, n, bank[:, 4 + 2 * (u // 2 % 2) + cc, :],
                                         (n_ready, n0 + u // 2 + 1) if cc == 0 else (w_used, phase[0] + u + 1))

            def norm(n):
                dve.wait_ge(mean_ready, n + 1)
                dve.wait_ge(y_ready, 8 * (n + 1))
                for q in range(4):
                    y = yT[:, 2 * q:2 * q + 2, :]
                    dve.tensor_tensor(y, y, bank[:, 0:1, 0:T].to_broadcast([P, 2, T]), ALU.subtract).then_inc(yc_ready, 1)
                dve.wait_ge(std_ready, n + 1)
                link(dve.reciprocal(tmp[:, 1, :], tmp[:, 0, :]))
                dve.wait_ge(sq_ready, 4 * n + 4)

                def scale(q):
                    y = yT[:, 2 * q:2 * q + 2, :]
                    dve.tensor_tensor(y, y, tmp[:, 1:2, :].to_broadcast([P, 2, T]), ALU.mult).then_inc(xn_ready, 1)

                scale(0)
                for q in range(NCH):
                    if q % 2 == 0 and q < 6:
                        scale(q // 2 + 1)
                    if n < 2:
                        dve.wait_ge(x_ready, 8 * n + q + 1)
                        modulate(n + 1, q, None)
                        if q:
                            low(q - 1, 8 * (n + 1 + (n == 1)) + q)
                if n < 2:
                    low(7, 8 * (n + 1 + (n == 1)) + 8)

            dve.wait_ge(x_in, 6)
            for n in range(NCH):
                modulate(0, n, None)
                if n:
                    low(n - 1, n)
            low(7, 8)
            up(0, UP1, DN1)
            down(0, DN1, WIN, 0)
            norm(0)

            for u, b in enumerate(WIN_ORDER):
                if u < 8:
                    lo(WIN, u + 2)
                if u in (2, 3):
                    for cc in range(2):
                        c = 2 * (u - 2) + cc
                        dve.wait_ge(*((win_mm, u + 1) if cc == 0 else (w_used, WIN[0] + u + 1)))
                        dve.wait_ge(sig_ready, c + 1)
                        src = bank[:, 2 * (u % 2) + cc, :]
                        dve.tensor_tensor(cbuf[:, c, ST:ST + SEQ], src[:, 0:SEQ], yT[:, c, 0:SEQ], ALU.mult)
                        dve.tensor_tensor(cbuf[:, c, ST + SEQ:CB].rearrange("p (b k) -> p b k", b=DB)[:, :, ST:SB],
                                          samples(src), samples(yT[:, c, :]), ALU.mult).then_inc(glu_ready, 1)

            def prompt_scores(h):
                dve.wait_ge(ps_mm, h + 1)
                if h >= 2:
                    dve.wait_ge(pp_t, h - 1)
                sc = ps_[:, h % 2, :]
                dve.scalar_tensor_tensor(sc, con[:, C_REL:C_REL + 384], 2.0 ** -(h + 1), bank[:, h % 2, 0:384], ALU.mult, ALU.add).then_inc(ps_ready, 1)
                dve.wait_ge(ps_ready, h + 1)
                dve.tensor_reduce(pm[:, h % 2, 0:1], sc[:, 0:P], AX, ALU.max, negate=True)
                dve.tensor_reduce(pm[:, h % 2, 1:2], sc[:, P:3 * P], AX, ALU.max, negate=True).then_inc(pmax_ready, 1)

            def prompt_probs(h):
                dve.wait_ge(pexp, h + 1)
                link(dve.reciprocal(pr[:, h % 2, :], pz[:, h % 2, :]))
                dve.tensor_scalar(ps_[:, h % 2, 0:P], ps_[:, h % 2, 0:P], pr[:, h % 2, 0:1], None, ALU.mult)
                dve.tensor_scalar(ps_[:, h % 2, P:3 * P], ps_[:, h % 2, P:3 * P], pr[:, h % 2, 1:2], None, ALU.mult).then_inc(pp_ready, 1)

            for h in range(NH):
                prompt_scores(h)
                if h:
                    prompt_probs(h - 1)
            prompt_probs(NH - 1)
            dve.wait_ge(qs_hi, 1)
            dve.tensor_tensor(kln, uT[:, 4:8, SEQ:T], khn.bitcast(F32), ALU.subtract)
            dve.tensor_tensor(ql, uT[:, 0:NHP, SEQ:T], qh.bitcast(F32), ALU.subtract).then_inc(qs_lo, 1)
            dve.wait_ge(qs_lo, 1)
            dve.wait_ge(ko_hi, 1)
            for e in range(2):
                ins = dve.tensor_copy(kol[0:64, :, :].rearrange("p (m e) t -> p m e t", e=2)[:, :, e, :], kln[64 * e:64 * e + 64, :, :].bitcast(F32))
            ins.then_inc(ko_lo, 1)

            def q_low(j, b2, first=False):
                if first:
                    dve.wait_ge(qs_lo, 1)
                dve.wait_ge(q_hi, 2 * j + b2 + 1)
                for r in range(2):
                    for e in range(2):
                        at = 64 * r + QPITCH * e
                        ins = dve.tensor_copy(qbl[64 * r:64 * r + 64, at:at + NHP * 2 * QPITCH].rearrange("p (m c) -> p m c", m=NHP)[:, :, 0:DT],
                                              ql[64 * e:64 * e + 64, :, bass.ds(DT * (2 * j + b2), DT)].bitcast(F32))
                ins.then_inc(q_lo, 1)

            def score_chunk(j, g):
                b2, n = g // 2, 4 * (g % 2)
                dve.wait_ge(k_used, 8 * j + 2 * g + 2)
                sbk = bank[:, 4 + g % 2, :].rearrange("p (n k) -> p n k", n=4)
                sc = s[:, b2, P * n:P * n + 512].rearrange("p (n k) -> p n k", n=4)
                dve.tensor_reduce(gsum[:, b2, n:n + 4], sbk, AX, ALU.add)
                dve.scalar_tensor_tensor(sc, con[:, C_POS:C_POS + P].unsqueeze(1).to_broadcast([P, 4, P]), con[:, C_M:C_M + 1], sbk,
                                         ALU.mult, ALU.add).then_inc(s_evac, 1)
                dve.wait_ge(s_evac, 4 * j + g + 1)
                dve.tensor_reduce(bmax[:, b2, n:n + 4], sc, AX, ALU.max)

            def attn_out(j):
                dve.wait_ge(v_used, 8 * j + 8)
                acc = bank[:, 7, 0:2 * P].rearrange("p (b m e r t) -> p m e b r t", b=2, m=NHP, e=2, r=2)
                for e in range(2):
                    ins = dve.tensor_copy(aodd[64 * e:64 * e + 64, :, :, :], acc[64:P, :, e, :, 1, :])
                link(ins)
                for e in range(2):
                    r = slice(64 * e, 64 * e + 64)
                    ins = dve.tensor_tensor(yT[r, 0:NHP, bass.ds(SEQ + 2 * DT * j, 2 * DT)].rearrange("p m (b t) -> p m b t", b=2),
                                            acc[0:64, :, e, :, 0, :], aodd[r, :, :, :], ALU.add)
                ins.then_inc(av_evac, 1)

            def pair_body(j, first=False, last=False):
                for k in range(8):
                    for hf in range(2):
                        dve.wait_ge(kt_hi, 16 * j + 2 * k + hf + 1)
                        dve.tensor_tensor(kl[:, k % 2, 2 * hf:2 * hf + 2, :], bank[:, 2 * hf:2 * hf + 2, :],
                                          kh[:, k % 2, 2 * hf:2 * hf + 2, :].bitcast(F32), ALU.subtract).then_inc(kt_lo, 1)
                    if k == 2 and not first:
                        dve.wait_ge(pt_ready, 5 * j)
                    if k == 4:
                        q_low(j, 1)
                    if k % 2 == 0 and k:
                        score_chunk(j, k // 2 - 1)
                score_chunk(j, 3)
                dve.wait_ge(own_ready, 2 * j + 2)
                for b2 in range(2):
                    ins = dve.tensor_tensor(s[:, b2, PAST // 2:], bank[:, 6, NS * b2:NS * b2 + NS],
                                            con[:, bass.ds(C_OWN + 56 - DT * (2 * j + b2), NS)], ALU.add)
                ins.then_inc(gsum_ready, 1)
                dve.wait_ge(gsum_ready, j + 1)
                dve.wait_ge(gate_mm, j + 1)
                link(dve.tensor_copy(gate[:, :, :], bank[:, 6, 256:272].rearrange("p (b n) -> p b n", b=2)))
                dve.tensor_reduce(bmax[:, 0:1, 8:9], s[:, 0:1, PAST // 2:], AX, ALU.max)
                for b2 in range(2):
                    ins = dve.max(gmax[:, b2, :], gate[:, b2, :])
                link(ins)
                dve.tensor_reduce(bmax[:, 1:2, 8:9], s[:, 1:2, PAST // 2:], AX, ALU.max)
                for b2 in range(2):
                    ins = dve.max_index(gidx[:, b2, :], gmax[:, b2, :], gate[:, b2, :])
                link(ins)
                link(dve.tensor_copy(gidf[:, :, :], gidx[:, :, :]))
                for b2 in range(2):
                    ins = dve.tensor_tensor(hit[:, b2], con[:, C_IOTA:C_IOTA + 8].unsqueeze(2).to_broadcast([P, 8, 3]),
                                            gidf[:, b2, 0:3].unsqueeze(1).to_broadcast([P, 8, 3]), ALU.is_equal)
                link(ins)
                link(dve.tensor_reduce(ebase[:, :, :], hit[:, :, :, :], AX, ALU.add))
                link(dve.tensor_scalar(ebase[:, :, :], ebase[:, :, :], -1.0, -NEG, ALU.add, ALU.mult))
                link(dve.tensor_tensor(ebase[:, :, :], ebase[:, :, :], con[:, C_RC:C_RC + 8].unsqueeze(1).to_broadcast([P, 2, 8]), ALU.add))
                link(dve.tensor_tensor(bmax[:, :, 0:8], bmax[:, :, 0:8], ebase[:, :, :], ALU.add))
                dve.tensor_reduce(nmax[:, :], bmax[:, :, :], AX, ALU.max, negate=True).then_inc(nmax_ready, 1)
                for b2 in range(2):
                    sc = s[:, b2, 0:PAST // 2].rearrange("p (n k) -> p n k", n=NBLK)
                    dve.tensor_tensor(sc, sc, ebase[:, b2, :].unsqueeze(2).to_broadcast([P, NBLK, P]), ALU.add)
                dve.wait_ge(swap_mm, j + 1)
                dve.tensor_tensor(ebias[:, :], nmax[:, :], bank[:, 6, 288:290], ALU.min).then_inc(eb_ready, 1)
                dve.wait_ge(rsum_mm, j + 1)
                link(dve.reciprocal(ri[:, :], bank[:, 6, 320:322]))
                dve.tensor_scalar(s[:, 0, :], s[:, 0, :], ri[:, 0:1], None, ALU.mult)
                dve.tensor_scalar(s[:, 1, :], s[:, 1, :], ri[:, 1:2], None, ALU.mult).then_inc(p_ready, 1)
                if not first:
                    attn_out(j - 1)
                if not last:
                    q_low(j + 1, 0)

            q_low(0, 0, True)
            dve.wait_ge(stored_early, 16 * N_EARLY)
            pair_body(0, first=True)
            before = step[0]
            PAIR_STEPS = 11
            with dve.Fori(1, 3) as j:
                step[0] = before + PAIR_STEPS * (j - 1)
                pair_body(j)
            step[0] = before + 2 * PAIR_STEPS
            pair_body(3, last=True)

            for c in range(NCC):
                dve.wait_ge(gm_mm, c + 1)
                y = yT[:, NCC + c, :]
                dve.tensor_tensor(y, y, bank[:, c, 0:T], ALU.subtract).then_inc(gc_ready, 1)
            for c in range(NCC):
                dve.wait_ge(gs_ready, c + 1)
                y = yT[:, NCC + c, :]
                link(dve.reciprocal(tmp[:, c, :], tmp[:, c, :]))
                dve.tensor_tensor(y, y, tmp[:, c, :], ALU.mult).then_inc(gx_ready, 1)
            for c in range(NCC):
                dve.wait_ge(gy_ready, c + 1)
                dve.tensor_scalar(yT[:, NCC + c, :], tmp[:, c, :], par2[:, 16 + c:17 + c], None, ALU.mult).then_inc(m_ready, 1)
                if c:
                    low(NCC + c - 1, 16 + c)
            low(7, 16 + NCC)
            lo(WOUT, 0)
            lo(WOUT, 1)
            attn_out(3)
            dve.wait_ge(av_evac, 4)
            dve.wait_ge(pv_out, 4)
            for c in range(NHP):
                dve.tensor_scalar(yT[:, c, :], yT[:, c, :], par2[:, 12 + c:13 + c], None, ALU.mult).then_inc(m_ready, 1)
                if c:
                    low(c - 1, 16 + NCC + c)
            low(NHP - 1, 24)

            dve.wait_ge(ax_ready, 2)
            for u in range(WOUT[2]):
                if u < 2:
                    lo(WOUT, u + 2)
                else:
                    lo(UP2, u - 2)
                for cc in range(2):
                    n = 2 * u + cc
                    add_residual(1, n, bank[:, 4 + 2 * (u % 2) + cc, :], (n_ready, 4 + u + 1) if cc == 0 else (w_used, WOUT[0] + u + 1))
            norm(1)
            up(1, UP2, DN2)
            down(2, DN2, None, 8)
            norm(2)

        @block.tensor
        def _(pe):
            pe.wait_ge(ld_con, 16)
            pe.wait_ge(ld_par, 16 * 11)
            pe.transpose(bank[:, 0, 0:120], prow[0:120, 0, :], ident[0:120, 0:120])
            pe.transpose(bank[:, 0, 128:148], prow[0:20, 1, :], ident[0:20, 0:20])
            pe.transpose(bank[:, 0, 256:380], prow[0:TAPS * NCC, 2, :], ident[0:124, 0:124])
            pe.transpose(bank[:, 1, 0:72], prow[0:72, 3, :], ident[0:72, 0:72]).then_inc(par_t, 1)
            pe.wait_ge(ld_x, 32)
            for n in range(6):
                tt, half = n // 2, n % 2
                w = P if tt < 2 else NS
                for c in range(4):
                    ins = pe.transpose(bank[:, 2 + n, P * c:P * c + w], xrow[0:w, tt, 512 * half + P * c:512 * half + P * c + P], ident[0:w, 0:w])
                ins.then_inc(x_t, 1)

            def ada_turn(u, u_):
                pe.wait_ge(ada_row, u + 1)
                if u_ >= 2:
                    pe.wait_ge(ada_out, u - 1)
                for cc in range(2):
                    ins = pe.matmul(bank[:, 2 + u_ % 2, 9 * cc:9 * cc + 9], rows[:, u_ % 2, P * cc:P * cc + P], con[0:18, C_SEL:C_SEL + 9],
                                    start=True, stop=True)
                ins.then_inc(ada_t, 1)

            def ada_unit(u, u_):
                pe.wait_ge(w_lo, u + 1)
                if u_ >= 2:
                    pe.wait_ge(ada_row, u - 1)
                for kk in range(NCH):
                    for x, w in enumerate((whi, wlo)):
                        ins = pe.matmul(bank[0:18, u_ % 2, 0:UC], chl[:, kk, :], w[:, u_ % 2, UC * kk:UC * kk + UC],
                                        start=(kk == 0 and x == 0), stop=(kk == NCH - 1 and x == 1))
                ins.then_inc(w_used, 1)
                if u_ >= 1:
                    ada_turn(u - 1, u_ - 1)

            pe.wait_ge(c_lo, 1)
            pe.wait_ge(par_ready, 2)
            pe.wait_ge(x_in, 6)
            for u in range(4):
                ada_unit(u, u)
            with pe.Fori(1, 9) as turn:
                for k in range(RING):
                    ada_unit(RING * turn + k, RING + k)
            ada_turn(35, 35)

            def product(b, slot, cc, parts, start=True, stop=True, ready=None):
                for n, (kk, h_, l_) in enumerate(parts):
                    if ready is not None:
                        ready(n)
                    c = slice(UC * kk + P * cc, UC * kk + P * cc + P)
                    pe.matmul(bank[:, b, 0:T], whi[:, slot, c], h_, start=(start and n == 0), stop=False)
                    pe.matmul(bank[:, b, 0:T], whi[:, slot, c], l_, start=False, stop=False)
                    ins = pe.matmul(bank[:, b, 0:T], wlo[:, slot, c], h_, start=False, stop=(stop and n == len(parts) - 1))
                return ins

            def m_parts(order):
                return [(kk, mh[:, kk, :], ml[:, kk, :]) for kk in order]

            def up(ffn, phase, ml0):
                gr, sr, ur, hr = g_ready[ffn], silu_ready[ffn], u_ready[ffn], h_ready[ffn]

                def body(pair, pair_):
                    for x in range(2):
                        pe.wait_ge(w_lo, phase[0] + 2 * pair + x + 1)
                        for cc in range(2):
                            if pair_:
                                pe.wait_ge((sr, hr)[x], 2 * pair + cc - 1)
                            ready = (lambda n: pe.wait_ge(ml_ready, ml0 + n + 1)) if pair_ == 0 and x == 0 and cc == 0 else None
                            ins = product(2 * x + cc, x, cc, m_parts(range(NCH)), ready=ready)
                            ins.then_inc((gr, ur)[x] if cc == 0 else w_used, 1)
                up_pairs(pe, body)

            def down(ffn, phase, n0):
                hlr = hl_ready[ffn]
                for u in range(8):
                    nb, half = u // 2, u % 2
                    pe.wait_ge(w_lo, phase[0] + u + 1)
                    for cc in range(2):
                        if nb >= 2:
                            pe.wait_ge(y_ready, n0 + 2 * (nb - 2) + cc + 1)
                        ready = (lambda n: pe.wait_ge(hlr, 11 * half + n + 1)) if nb == 0 and cc == 0 else None
                        parts = [(kk, hh[:, 11 * half + kk, :], hl[:, 11 * half + kk, :]) for kk in range(11)]
                        ins = product(4 + 2 * (nb % 2) + cc, u % 2, cc, parts, start=half == 0, stop=half == 1, ready=ready)
                        if cc:
                            ins.then_inc(w_used, 1)
                        elif half:
                            ins.then_inc(n_ready, 1)

            def norm(n):
                for q in range(NCH):
                    pe.wait_ge(y_ready, 8 * n + q + 1)
                    ins = pe.matmul(bank[:, 0, 0:T], lnones, yT[:, q, :], start=(q == 0), stop=(q == NCH - 1))
                ins.then_inc(mean_ready, 1)
                for q in range(4):
                    pe.wait_ge(sq_ready, 4 * n + q + 1)
                    for x in range(2):
                        ins = pe.matmul(bank[:, 1, 0:T], lnones, tmp[:, 2 * (q % 2) + x, :], start=(q == 0 and x == 0), stop=(q == 3 and x == 1))
                    ins.then_inc(sq_used if q < 3 else var_ready, 1)

            up(0, UP1, 0)
            down(0, DN1, 0)
            norm(0)

            for u, b in enumerate(WIN_ORDER):
                pe.wait_ge(w_lo, WIN[0] + u + 1)
                for cc in range(2):
                    if u in (2, 3):
                        pe.wait_ge(sig_ready, 2 * (u - 2) + cc + 1)
                    elif u in (4, 5):
                        pe.wait_ge(glu_ready, 2 * (u - 4) + cc + 1)
                    elif u >= 6:
                        pe.wait_ge(u_out, 2 * (u - 6) + cc + 1)
                    else:
                        pe.wait_ge(x_ready, 1)
                    ready = (lambda n: pe.wait_ge(ml_ready, 8 + n + 1)) if u == 0 and cc == 0 else None
                    ins = product(2 * (u % 2) + cc, u % 2, cc, m_parts(range(NCH)), ready=ready)
                    ins.then_inc(win_mm if cc == 0 else w_used, 1)

            pe.wait_ge(ld_state, 32)
            for g in range(2):
                for c in range(NCC):
                    ins = pe.transpose(bank[:, 4 + g, 120 * c:120 * c + 120], strow[:, g, P * c:P * c + P], ident[0:120, 0:120])
                ins.then_inc(st_t, 1)
            pe.wait_ge(u_out, 12)
            for n in range(6):
                w = P if n % 3 < 2 else NS
                if n >= 4:
                    pe.wait_ge(tok_out, n - 3)
                for c in range(NHP):
                    ins = pe.transpose(bank[0:w, n % 4, P * c:P * c + P], uT[:, (8 if n < 3 else 4) + c, P * (n % 3):P * (n % 3) + w], ident)
                ins.then_inc(tok_t, 1)
            pe.wait_ge(glu_ready, NCC)
            for c in range(NCC):
                ins = pe.transpose(bank[0:ST, 6, P * c:P * c + P], cbuf[:, c, SEQ:SEQ + ST], ident)
            ins.then_inc(gl_t, 1)
            pe.wait_ge(gs_copy, 1)
            for c in range(NCC):
                ins = pe.transpose(bank[0:NS, 7, P * c:P * c + P], gsam[:, c, :], ident)
            ins.then_inc(gl_t, 1)

            def prompt_qk(h):
                r = slice(64 * (h % 2), 64 * (h % 2) + 64)
                if h >= 2:
                    pe.wait_ge(ps_ready, h - 1)
                q, k = uT[r, h // 2, :], uT[r, 4 + h // 2, :]
                pe.matmul(bank[:, h % 2, 0:P], q[:, 0:P], k[:, 0:P], start=True, stop=True)
                pe.matmul(bank[:, h % 2, P:3 * P], q[:, P:2 * P], k[:, 0:2 * P], start=True, stop=True).then_inc(ps_mm, 1)

            def prompt_turn(h):
                pe.wait_ge(pp_ready, h + 1)
                if h >= 2:
                    pe.wait_ge(pp_out, h - 1)
                for n in range(3):
                    ins = pe.transpose(bank[:, 2 + h % 2, P * n:P * n + P], ps_[:, h % 2, P * n:P * n + P], ident)
                ins.then_inc(pp_t, 1)

            def prompt_pv(h):
                pe.wait_ge(pp_out, h + 1)
                if h >= 4:
                    pe.wait_ge(pv_out, h // 2 - 1)
                r = slice(64 * (h % 2), 64 * (h % 2) + 64)
                b = 4 + h // 2 % 2
                v = [vtok[:, n, HD * h:HD * h + HD] for n in range(2)]
                p_ = ppT[:, h % 2, :]
                pe.matmul(bank[r, b, 0:P], v[0], p_[:, 0:P], start=True, stop=True)
                pe.matmul(bank[r, b, P:2 * P], v[0], p_[:, P:2 * P], start=True, stop=False)
                pe.matmul(bank[r, b, P:2 * P], v[1], p_[:, 2 * P:3 * P], start=False, stop=True).then_inc(pv_mm, 1)

            pe.wait_ge(tok_out, 6)
            pe.wait_ge(st_in, 2)
            prompt_qk(0)
            for h in range(NH):
                if h + 1 < NH:
                    prompt_qk(h + 1)
                prompt_turn(h)
                prompt_pv(h)

            def scores(j, k, hf, first):
                g, b2 = k // 2, k // 4
                pe.wait_ge(kt_lo, 16 * j + 2 * k + hf + 1)
                if hf == 0 and k % 4 == 0:
                    pe.wait_ge(q_lo, 2 * j + b2 + 1)
                if hf == 0 and k % 2 == 0 and not (first and g < 2):
                    pe.wait_ge(s_evac, 4 * j + g - 1)
                for h in range(4 * hf, 4 * hf + 4):
                    for x, (q, kk) in enumerate(((qbh, kh), (qbh, kl), (qbl, kh))):
                        ins = pe.matmul(bank[:, 4 + g % 2, BLK * (k % 2):BLK * (k % 2) + BLK], q[:, P * h:P * h + P],
                                        kk[:, k % 2, h // 2, BLK * (h % 2):BLK * (h % 2) + BLK],
                                        start=(h == 0 and x == 0), stop=(h == NH - 1 and x == 2))
                if hf:
                    ins.then_inc(k_used, 1)

            def own_scores(b2):
                for h in range(NH):
                    for x, (q, kk) in enumerate(((qbh, koh), (qbh, kol), (qbl, koh))):
                        ins = pe.matmul(bank[:, 6, NS * b2:NS * b2 + NS], q[:, P * h:P * h + P], kk[:, h, :],
                                        start=(h == 0 and x == 0), stop=(h == NH - 1 and x == 2))
                ins.then_inc(own_ready, 1)

            def page_view(k, pp, h):
                at = 1024 * pp + P * h
                return raw[:, k % RING, at:at + P]

            def raw_wait(k, kv4, turns):
                pe.wait_ge(raw_in[k % RING], raw_count_kv(RING * (kv4 + k // RING)) + turns)

            def pair_keys(j, kv4, turns, first=False):
                for k in range(8):
                    raw_wait(k, kv4, turns)
                    for hf in range(2):
                        if not (first and k == 0):
                            pe.wait_ge(kt_lo, 16 * j + 2 * k + hf - 1)
                        for h in range(4 * hf, 4 * hf + 4):
                            for pp in range(2):
                                at = BLK * (h % 2) + P * pp
                                ins = pe.transpose(bank[:, h // 2, at:at + P], page_view(k, pp, h), ident)
                        ins.then_inc(kt_ready, 1)
                        if k:
                            scores(j, k - 1, hf, first)
                        if k == 4 and hf:
                            own_scores(0)
                scores(j, 7, 0, first)
                scores(j, 7, 1, first)
                own_scores(1)

            def parities(ready, count, matrix, at, src, n, done):
                pe.wait_ge(ready, count)
                pe.matmul(bank[:, 6, at:at + n], con[:, matrix:matrix + P], src, start=True, stop=True).then_inc(done, 1)

            def gate_sum(j):
                parities(gsum_ready, j + 1, C_SUM, 256, gsum[:, :, :].rearrange("p b n -> p (b n)"), 16, gate_mm)

            def max_swap(j):
                parities(nmax_ready, j + 1, C_SWAP, 288, nmax[:, :], 2, swap_mm)

            def prob_sum(j):
                parities(ex_ready, j + 1, C_SUM, 320, rt[:, :], 2, rsum_mm)

            def pair_probs(j):
                pe.wait_ge(p_ready, j + 1)
                for r in range(4):
                    if r >= 2:
                        pe.wait_ge(pt_evac, 5 * j + r - 1)
                    for x in range(4):
                        n = 4 * (r % 2) + x
                        ins = pe.transpose(bank[:, 4 + r % 2, P * x:P * x + P], s[:, r // 2, P * n:P * n + P], ident)
                    ins.then_inc(pt_ready, 1)
                for b2 in range(2):
                    ins = pe.transpose(bank[0:NS, 6, P * b2:P * b2 + P], s[:, b2, PAST // 2:], ident)
                ins.then_inc(pt_ready, 1)

            def pair_values(j, kv4, turns, first=False, between=None):
                pe.wait_ge(pt_evac, 5 * j + 5)
                if not first:
                    pe.wait_ge(av_evac, j)
                for k in range(8):
                    c, b2 = k % 4, k // 4
                    raw_wait(k, kv4, turns)
                    for pp in range(2):
                        n = NBLK * b2 + 2 * c + pp
                        probs = pT[:, P * n:P * n + P].rearrange("p (r h t) -> p h r t", r=2, h=NH)
                        for h in range(NH):
                            at = P * b2 + 16 * h
                            ins = pe.matmul(bank[:, 7, at:at + 16], page_view(k, pp, h), probs[:, h], start=(k == 0 and pp == 0 and h == 0),
                                            stop=False, skip_group_check=True)
                    if k < 7:
                        ins.then_inc(v_used, 1)
                    if between is not None and k in between:
                        between[k]()
                for b2 in range(2):
                    for h in range(NH):
                        at = P * b2 + 16 * h
                        ins = pe.matmul(bank[0:64, 7, at:at + DT], vsam[:, HD * h:HD * h + HD], po[:, P * b2 + DT * h:P * b2 + DT * h + DT],
                                        start=False, stop=True, skip_group_check=True)
                ins.then_inc(v_used, 1)

            pe.wait_ge(ko_lo, 1)
            pe.wait_ge(gl_out, 2)
            pe.wait_ge(pv_out, 4)
            pair_keys(0, 0, 0, first=True)
            gate_sum(0)
            max_swap(0)
            prob_sum(0)
            pair_probs(0)

            def next_pair(j, kv4, turns, first=False):
                pe.wait_ge(pt_evac, 5 * j)
                pair_keys(j, kv4, turns)
                pair_values(j - 1, kv4 + 2, turns, first, {0: lambda: gate_sum(j), 2: lambda: max_swap(j), 5: lambda: prob_sum(j)})
                pair_probs(j)

            next_pair(1, 2, 0, first=True)
            with pe.Fori(2, 4) as j:
                next_pair(j, 6, 64 * 4 * (j - 2))

            pe.wait_ge(pt_evac, 20)
            pe.wait_ge(conv_ready, NCC)
            for c in range(NCC):
                pe.matmul(bank[:, c, 0:T], gnones, yT[:, NCC + c, :], start=True, stop=True).then_inc(gm_mm, 1)
            for c in range(NCC):
                pe.wait_ge(gq_ready, c + 1)
                pe.matmul(bank[:, c, 0:T], gnones, tmp[:, c, :], start=True, stop=True).then_inc(gv_mm, 1)
            pair_values(3, 14, 0)

            for u in range(WOUT[2]):
                pe.wait_ge(w_lo, WOUT[0] + u + 1)
                for cc in range(2):
                    if u >= 2:
                        pe.wait_ge(y_ready, 8 + 2 * (u - 2) + cc + 1)
                    ready = (lambda n: pe.wait_ge(ml_ready, 16 + n + 1)) if u == 0 and cc == 0 else None
                    ins = product(4 + 2 * (u % 2) + cc, u % 2, cc, m_parts(MIX_ORDER), ready=ready)
                    ins.then_inc(n_ready if cc == 0 else w_used, 1)
            norm(1)
            up(1, UP2, 24)
            down(1, DN2, 16)
            norm(2)
            for n in range(6):
                tt, half = n // 2, n % 2
                w = P if tt < 2 else NS
                pe.wait_ge(x_ready, 16 + 4 * half + 4)
                for c in range(4):
                    ins = pe.transpose(bank[0:w, 2 + n, P * c:P * c + P], xT[:, 4 * half + c, P * tt:P * tt + w], ident)
                ins.then_inc(out_t, 1)


_INS = ["x_prompt", "x_sample", "cache_k", "cache_v", "state_conv", "page_table", "c_prompt", "c_sample", "w_ada", "b_ada",
        "ffn1_wg", "ffn1_wu", "ffn1_wd", "w_in", "w_dw", "b_dw", "gn_g", "gn_b", "beta_attn", "beta_conv", "w_out",
        "ffn2_wg", "ffn2_wu", "ffn2_wd", "ln_g", "ln_b"]
_OUTS = [("y_prompt", (1, SEQ, D)), ("y_sample", (DB, DT, D)), ("k_prompt_new", (1, 1, SEQ // PAGE, NH, PAGE, HD)),
         ("v_prompt_new", (1, 1, SEQ // PAGE, NH, PAGE, HD)), ("conv_prompt_new", (1, 1, ST, CC)),
         ("k_sample_new", (1, DB, NH, DT, HD)), ("v_sample_new", (1, DB, NH, DT, HD)), ("conv_sample_new", (1, DB, ST, CC))]


def kernel(**inputs):
    import concourse.bacc as bacc
    from concourse.bass_utils import run_bass_kernel_spmd

    nc = bacc.Bacc("TRN2", target_bir_lowering=False, num_devices=1)
    arrays, ins, outs = {}, {}, {}
    for name in _INS + ["consts"]:
        a = constants() if name == "consts" else np.ascontiguousarray(inputs[name])
        arrays[f"in_{name}"] = a
        ins[name] = nc.dram_tensor(f"in_{name}", a.shape, mybir.dt.from_np(a.dtype), kind="ExternalInput").ap()
    for name, shape in _OUTS:
        outs[name] = nc.dram_tensor(f"out_{name}", shape, F32, kind="ExternalOutput").ap()
    build(nc, ins, outs)
    r = run_bass_kernel_spmd(nc, [arrays], core_ids=[0])
    return tuple(r.results[0][f"out_{name}"] for name, _ in _OUTS)
```

```python
from contextlib import ExitStack

import numpy as np

import concourse.bass as bass
from concourse import mybir

F32 = mybir.dt.float32
F32R = mybir.dt.float32r
I32 = mybir.dt.int32
U32 = mybir.dt.uint32
ALU = mybir.AluOpType
ACT = mybir.ActivationFunctionType
AX = mybir.AxisListType.X

P = 128
D = 1024
NCH = D // P
SEQ = 256
DB, DT = 8, 8
NS = DB * DT
T = SEQ + NS
NH, HD = 8, 64
AW = NH * HD
NHP = AW // P
CC = 512
NCC = CC // P
TAPS = 31
ST = TAPS - 1
PAST, PAGE, BLK = 2048, 128, 256
NPG = PAST // PAGE
NBLK = PAST // BLK
NPOOL = 160
FF = 2816
NF = FF // P
ALPHA = 2.0 ** 0.25
EPS = 1e-5
NEG = -1e30
UC = 256
RING = 4
UMAX = NCH * UC
CB = ST + SEQ + DB * (ST + DT)
SB = ST + DT
QPITCH = P + DT
QB = 64 + P + DT + NHP * 2 * QPITCH

C_ID, C_LN, C_GN, C_REL, C_SEL = 0, P, 2 * P, 3 * P, 6 * P
C_POS = C_SEL + 16
C_OWN = C_POS + P
C_IOTA = C_OWN + 120
C_RC = C_IOTA + 8
C_M = C_RC + 8
C_EPS = C_M + 1
C_SUM = C_EPS + 1
C_SWAP = C_SUM + P
C_HEAD = C_SWAP + P
C_N = C_HEAD + 4


def constants():
    c = np.zeros((P, C_N), np.float32)
    p = np.arange(P)
    c[:, C_ID:C_ID + P] = np.eye(P)
    c[:, C_LN:C_LN + P] = 1.0 / D
    c[:, C_GN:C_GN + P] = (p[:, None] // 64 == p[None, :] // 64) / 64.0
    for at, q0, keys in ((0, 0, P), (P, P, 2 * P)):
        rel = np.arange(keys)[None, :] - (q0 + p[:, None])
        c[:, C_REL + at:C_REL + at + keys] = np.where(rel <= 0, rel, -3e34)
    for r in range(18):
        c[r, C_SEL + r % 9] = 1.0
    c[:, C_POS:C_POS + P] = (p // 64 * P + 2 * (p % 64))[None, :]
    r, h, t = p // 64, p % 64 // 8, p % 8
    m = 2.0 ** (-(h + 1.0))
    key = np.arange(120) - 56
    ok = (key[None, :] >= 0) & (key[None, :] <= t[:, None]) & (r[:, None] == 0)
    c[:, C_OWN:C_OWN + 120] = np.where(ok, m[:, None] * (key[None, :] - t[:, None]), NEG)
    c[:, C_IOTA:C_IOTA + 8] = np.arange(8)[None, :]
    c[:, C_RC:C_RC + 8] = m[:, None] * (BLK * np.arange(8)[None, :] - PAST + (r - t)[:, None])
    c[:, C_M] = m
    c[:, C_EPS] = EPS
    c[:, C_SUM:C_SUM + P] = p[:, None] % 64 == p[None, :] % 64
    c[:, C_SWAP:C_SWAP + P] = (p[:, None] + 64) % P == p[None, :]
    c[:, C_HEAD:C_HEAD + 4] = h[:, None] % 4 == np.arange(4)[None, :]
    return c


ADA, UP1, DN1, WIN, WOUT, UP2, DN2 = (0, 0, 14), (14, 14, 44), (58, 58, 12), (70, 70, 10), (80, 144, 4), (84, 148, 22), (106, 170, 12)
KV0, KVN = 80, 64
ADAN = 9 * D // UC
DN_CHUNKS = (8, 8, 6)
WIN_ORDER = [8, 9, 6, 7, 2, 3, 4, 5, 0, 1]
MIX_ORDER = [4, 5, 6, 7, 0, 1, 2, 3]


def raw_count(turn):
    before = KV0 // RING
    return 16 * (turn + 1) if turn < before else 16 * (turn + 1 - KVN // RING) + 64 * (KVN // RING)


def raw_count_w(phase, u, turns=0):
    return raw_count((phase[1] + u) // RING) + 16 * turns


def raw_count_kv(kvi, turns=0):
    return 16 * (KV0 // RING) + 64 * (kvi // RING + 1) + 64 * turns


def slots(phase):
    return 3 if phase[0] < WOUT[0] else 2


def slot_w(phase, u):
    return (phase[0] + u) % slots(phase)


def build(nc, i, o):
    es = ExitStack()
    with es:
        def sb(name, shape, dt=F32, stack=es):
            return stack.enter_context(nc.sbuf_tensor(name, shape, dt))

        def sem(name):
            return es.enter_context(nc.semaphore(name))

        bank = es.enter_context(nc.psum_tensor("bank", [P, 8, 512], F32))
        con = sb("con", [P, C_N])
        xT = sb("xT", [P, NCH, T])
        yT = sb("yT", [P, NCH, T])
        mh = sb("mh", [P, NCH, T], F32R)
        ml = sb("ml", [P, NCH, T], F32R)
        adaT = sb("adaT", [P, 72, 9])
        raw = sb("raw", [P, RING, UMAX])
        whi = sb("whi", [P, 3, UMAX], F32R)
        wlo = sb("wlo", [P, 3, UMAX], F32R)
        par1 = sb("par1", [P, 120])
        par2 = sb("par2", [P, 20])
        dwT = sb("dwT", [P, TAPS * NCC])
        cT = sb("cT", [P, 72])
        chl = sb("chl", [P, NCH, 18], F32R)
        pages = sb("pages", [1, DB * NPG], I32)
        tmp = sb("tmp", [P, 4, T])
        rows = sb("rows", [18, 2, UC])

        with ExitStack() as scope:
            hh = sb("hh", [P, NF, T], F32R, scope)
            hl = sb("hl", [P, NF, T], F32R, scope)
        with ExitStack() as scope:
            xrow = sb("xrow", [P, 3, D], F32, scope)
            prow = sb("prow", [P, 4, P], F32, scope)
        with ExitStack() as scope:
            yrow = sb("yrow", [P, 3, D], F32, scope)
        with ExitStack() as scope:
            uT = sb("uT", [P, 12, T], F32, scope)
            cbuf = sb("cbuf", [P, NCC, CB], F32, scope)
            s = sb("s", [P, 2, PAST // 2 + NS], F32, scope)
            pT = sb("pT", [P, 2 * NBLK * P], F32, scope)
            po = sb("po", [NS, 2 * P], F32, scope)
            qbh = sb("qbh", [P, QB], F32R, scope)
            qbl = sb("qbl", [P, QB], F32R, scope)
            koh = sb("koh", [P, NH, NS], F32R, scope)
            kol = sb("kol", [P, NH, NS], F32R, scope)
            vtok = sb("vtok", [P, 2, AW], F32, scope)
            vsam = sb("vsam", [NS, AW], F32, scope)
            gsum = sb("gsum", [P, 2, 8], F32, scope)
            gate = sb("gate", [P, 2, 8], F32, scope)
            gmax = sb("gmax", [P, 2, 8], F32, scope)
            gidx = sb("gidx", [P, 2, 8], U32, scope)
            gidf = sb("gidf", [P, 2, 8], F32, scope)
            hit = sb("hit", [P, 2, 8, 3], F32, scope)
            ebase = sb("ebase", [P, 2, 8], F32, scope)
            bmax = sb("bmax", [P, 2, 9], F32, scope)
            nmax = sb("nmax", [P, 2], F32, scope)
            ebias = sb("ebias", [P, 2], F32, scope)
            rt = sb("rt", [P, 2], F32, scope)
            ri = sb("ri", [P, 2], F32, scope)
            ps_ = sb("ps_", [P, 3, 3 * P], F32, scope)
            pm = sb("pm", [P, 3, 2], F32, scope)
            pz = sb("pz", [P, 3, 2], F32, scope)
            pr = sb("pr", [P, 3, 2], F32, scope)
        khn, kln, qh, ql = (t_[:, n, 0:NHP * NS].rearrange("p (m t) -> p m t", m=NHP)
                            for t_, n in ((mh, 0), (ml, 0), (mh, 1), (ml, 1)))
        sflat = s[:, :, :].rearrange("p b c -> p (b c)")
        strow = pT[0:4 * ST, 0:2 * CC].rearrange("p (g c) -> p g c", g=2)
        ksam = sflat[0:NS, 768:768 + AW]
        cout = sflat[0:ST, 1280:1280 + CC]
        ppT = pT[:, 0:768].rearrange("p (a c) -> p a c", a=2)
        ktok = pT[:, 1024:2048].rearrange("p (g c) -> p g c", g=2)
        csam = tmp[:, :, :].rearrange("p a t -> p (a t)")[0:NS, 2 * T:2 * T + CC]
        tmp2 = tmp[:, 2:4, :].rearrange("p a t -> p (a t)")
        ahead = tmp2[:, 0:8 * HD].rearrange("p (b h d) -> p b h d", b=2, h=4)
        arow = tmp2[:, 8 * HD:10 * HD].rearrange("p (b d) -> p b d", b=2)
        gsam = yT[:, 0, 0:NCC * NS].rearrange("p (c k) -> p c k", c=NCC)
        kh = whi[:, 0:2, :].rearrange("p s (m c) -> p s m c", m=NHP)
        kl = wlo[:, 0:2, :].rearrange("p s (m c) -> p s m c", m=NHP)

        ident = con[:, C_ID:C_ID + P]
        lnones = con[:, C_LN:C_LN + P]
        gnones = con[:, C_GN:C_GN + P]

        ld_c, c_t = sem("ld_c"), sem("c_t")
        ld_con, ld_par, ld_x, ld_pages, ld_state = sem("ld_con"), sem("ld_par"), sem("ld_x"), sem("ld_pages"), sem("ld_state")
        raw_in = [sem(f"raw_in{k}") for k in range(RING)]
        w_hi, w_lo, w_used = sem("w_hi"), sem("w_lo"), sem("w_used")
        par_t, x_t, c_silu, c_hi, c_lo, par_ready, x_in = (sem(n) for n in ("par_t", "x_t", "c_silu", "c_hi", "c_lo", "par_ready", "x_in"))
        ada_row, ada_t, ada_out = (sem(n) for n in ("ada_row", "ada_t", "ada_out"))
        m_ready, mh_ready, ml_ready, ax_ready, y_ready = (sem(n) for n in ("m_ready", "mh_ready", "ml_ready", "ax_ready", "y_ready"))
        mean_ready, yc_ready, sq_ready, sq_used, var_ready, std_ready, xn_ready, x_ready = (
            sem(n) for n in ("mean_ready", "yc_ready", "sq_ready", "sq_used", "var_ready", "std_ready", "xn_ready", "x_ready"))
        g_ready = [sem("g_ready1"), sem("g_ready2")]
        silu_ready = [sem("silu_ready1"), sem("silu_ready2")]
        u_ready = [sem("u_ready1"), sem("u_ready2")]
        h_ready = [sem("h_ready1"), sem("h_ready2")]
        hh_ready = [sem("hh_ready1"), sem("hh_ready2")]
        hl_ready = [sem("hl_ready1"), sem("hl_ready2")]
        n_ready = sem("n_ready")
        dve_step, act_step, pool_step = sem("dve_step"), sem("act_step"), sem("pool_step")
        win_mm, sig_ready, glu_ready, u_out = (sem(n) for n in ("win_mm", "sig_ready", "glu_ready", "u_out"))
        tok_t, tok_out, st_t, st_in, gl_t, gl_out = (sem(n) for n in ("tok_t", "tok_out", "st_t", "st_in", "gl_t", "gl_out"))
        pad_ready, conv_ready = sem("pad_ready"), sem("conv_ready")
        ps_mm, ps_ready, pmax_ready, pexp, pp_ready, pp_t, pp_out, pv_mm, pv_out = (
            sem(n) for n in ("ps_mm", "ps_ready", "pmax_ready", "pexp", "pp_ready", "pp_t", "pp_out", "pv_mm", "pv_out"))
        ko_hi, ko_lo, q_zero, q_hi, q_lo = (
            sem(n) for n in ("ko_hi", "ko_lo", "q_zero", "q_hi", "q_lo"))
        qs_hi, qs_lo, gs_copy, gsum_ready, gate_mm, nmax_ready, swap_mm, rsum_mm = (
            sem(n) for n in ("qs_hi", "qs_lo", "gs_copy", "gsum_ready", "gate_mm", "nmax_ready", "swap_mm", "rsum_mm"))
        kt_ready, kt_hi, kt_lo, k_used, s_evac, own_ready, eb_ready, ex_ready, p_ready, pt_ready, pt_evac, v_used, av_evac = (
            sem(n) for n in ("kt_ready", "kt_hi", "kt_lo", "k_used", "s_evac", "own_ready", "eb_ready", "ex_ready", "p_ready",
                             "pt_ready", "pt_evac", "v_used", "av_evac"))
        acc_ready, arow_ready, at_mm = sem("acc_ready"), sem("arow_ready"), sem("at_mm")
        gm_mm, gc_ready, gq_ready, gv_mm, gs_ready, gx_ready, gy_ready = (
            sem(n) for n in ("gm_mm", "gc_ready", "gq_ready", "gv_mm", "gs_ready", "gx_ready", "gy_ready"))
        out_t, out_row, stored = sem("out_t"), sem("out_row"), sem("stored")
        stored_early = sem("stored_early")
        N_EARLY = 1 + 3 * DB + 4
        X_AT = 4
        MOD_AT = 10

        def mod_chunks(u):
            return range(2 * (u - MOD_AT), 2 * (u - MOD_AT) + 2) if MOD_AT <= u < MOD_AT + 4 else ()

        block = es.enter_context(nc.Block())

        def up_pairs(eng, ffn, body):
            body(0, 0)
            if ffn == 0:
                with eng.Fori(0, 3) as g:
                    for n in range(3):
                        body(1 + 3 * g + n, 1 + n)
            else:
                with eng.Fori(0, 4) as g:
                    body(1 + 2 * g, 1)
                    body(2 + 2 * g, 2)
                body(9, 9)
            body(10, 10)

        def stride(ffn):
            return 4 if ffn == 0 else 2

        def load_pages(eng, cache, seq, c, k, which, wait):
            engine = mybir.EngineType.SP if eng is nc.sync else mybir.EngineType.Activation
            page = [nc.values_load(pages[0:1, bass.ds(NPG * seq + 4 * c + x, 1)], engines=[engine], min_val=0, max_val=NPOOL - 1,
                                   skip_runtime_bounds_check_because="a page table holds indices into the pool, as the reference reads it")
                    for x in which]
            if wait is not None:
                eng.wait_ge(*wait)
            for x, at in zip(which, page):
                eng.dma_start(raw[64 * (x % 2):64 * (x % 2) + 64, k % RING, 1024 * (x // 2):1024 * (x // 2) + 1024]
                              .rearrange("p (h f) -> p h f", h=NH),
                              i["cache_" + cache][0][bass.ds(at, 1)].rearrange("a h (p r) d -> p (a h) (r d)", r=2)).then_inc(raw_in[k % RING], 16)

        @block.sync
        def _(sp):
            sp.dma_start(con[:, :], i["consts"]).then_inc(ld_con, 16)
            def slot_of(phase, u):
                return (phase[1] + u) % RING

            def load(phase, u, src, size, wait, turns=0):
                if wait is not None:
                    sp.wait_ge(*wait)
                k = slot_of(phase, u)
                sp.dma_start(raw[:, k, 0:size].rearrange("p (k c) -> p k c", c=UC), src).then_inc(raw_in[k], 16)

            def w_free(phase, u):
                return (w_lo, phase[0] + u - RING + 1)

            def cols(w, c):
                return w[0].rearrange("(k p) c -> p k c", p=P)[:, :, c]

            def load_ada(phase, u, n, wait):
                load(phase, u, cols(i["w_ada"], bass.ds(UC * n, UC)), NCH * UC, wait)

            for u in range(4):
                load_ada(ADA, u, u, None)
            sp.dma_start(xrow[:, 0:2, :], i["x_prompt"][0].rearrange("(t p) f -> p t f", p=P)).then_inc(ld_x, 16)
            sp.dma_start(xrow[0:NS, 2, :], i["x_sample"].rearrange("b t f -> (b t) f")).then_inc(ld_x, 16)
            for u in range(4, ADA[2]):
                load_ada(ADA, u, u, w_free(ADA, u))
            sp.dma_start(pages[:, :], i["page_table"].rearrange("b n -> (b n)").unsqueeze(0)).then_inc(ld_pages, 16)
            sp.dma_start(o["conv_sample_new"][0, :, 0:ST - DT, :], i["state_conv"][0, :, DT:ST, :]).then_inc(stored, 16)

            def load_up(phase, ffn):
                n = stride(ffn)

                def body(pair, pair_):
                    for x, w in enumerate((i[f"ffn{ffn + 1}_wg"], i[f"ffn{ffn + 1}_wu"])):
                        load(phase, n * pair_ + n // 2 * x, cols(w, bass.ds(UC * pair, UC)), NCH * UC, w_free(phase, n * pair + n // 2 * x))
                        if ffn == 0:
                            load_ada(phase, n * pair_ + 2 * x + 1, ADA[2] + 2 * pair + x, w_free(phase, n * pair + 2 * x + 1))
                up_pairs(sp, ffn, body)

            def load_down(phase, ffn):
                w = i[f"ffn{ffn + 1}_wd"][0].rearrange("(k p) c -> p k c", p=P)
                for u in range(DN1[2]):
                    n = DN_CHUNKS[u % 3]
                    load(phase, u, w[:, 8 * (u % 3):8 * (u % 3) + n, UC * (u // 3):UC * (u // 3) + UC], n * UC, w_free(phase, u))

            load_up(UP1, 0)
            load_down(DN1, 0)
            for u, b in enumerate(WIN_ORDER):
                load(WIN, u, cols(i["w_in"], slice(UC * b, UC * b + UC)), NCH * UC, w_free(WIN, u))
            sp.wait_ge(w_used, DN1[0] + DN1[2])
            for g in range(2):
                sp.dma_start(strow[:, g, :], i["state_conv"][0, 4 * g:4 * g + 4].rearrange("b k c -> (b k) c")).then_inc(ld_state, 16)
            sp.wait_ge(ld_pages, 16)

            def store_rows():
                sp.wait_ge(tok_out, 6)
                sp.wait_ge(gl_out, 2)
                for t_, name in ((vtok, "v_prompt_new"), (ktok, "k_prompt_new")):
                    for pg in range(2):
                        sp.dma_start(o[name][0, 0, pg].rearrange("h p d -> p h d"), t_[:, pg, :].rearrange("p (h d) -> p h d", h=NH)).then_inc(stored_early, 16)
                for b in range(DB):
                    r = slice(DT * b, DT * b + DT)
                    sp.dma_start(o["v_sample_new"][0, b].rearrange("h t d -> t h d"), vsam[r, :].rearrange("t (h d) -> t h d", h=NH)).then_inc(stored_early, 16)
                    sp.dma_start(o["k_sample_new"][0, b].rearrange("h t d -> t h d"), ksam[r, :].rearrange("t (h d) -> t h d", h=NH)).then_inc(stored_early, 16)
                    sp.dma_start(o["conv_sample_new"][0, b, ST - DT:ST, :], csam[r, :]).then_inc(stored_early, 16)
                sp.dma_start(o["conv_prompt_new"][0, 0], cout).then_inc(stored_early, 16)

            for k in range(8):
                load_pages(sp, "k", k // 4, k % 4, k, range(4) if k < RING else (0, 1),
                           (w_lo, WIN[0] + WIN[2] - RING + k + 1) if k < RING else (kt_ready, 2 * (k - RING) + 2))
                if k == RING - 1:
                    store_rows()

            def sp_pages(cache, seq, c, k, wait):
                load_pages(sp, cache, seq, c, k, (0, 1), wait)

            def kv_round(j, j_is_1):
                for k in range(8):
                    if k >= RING:
                        wait = (kt_ready, 16 * j + 2 * (k - RING) + 2)
                    elif j_is_1:
                        wait = (kt_ready, 2 * (k + RING) + 2)
                    else:
                        wait = (v_used, 8 * (j - 2) + k + RING + 1)
                    sp_pages("k", 2 * j + k // 4, k % 4, k, wait)
                for k in range(8):
                    wait = (kt_ready, 16 * j + 2 * (k + RING) + 2) if k < RING else (v_used, 8 * (j - 1) + k - RING + 1)
                    sp_pages("v", 2 * (j - 1) + k // 4, k % 4, k, wait)

            kv_round(1, True)
            with sp.Fori(2, 4) as j:
                kv_round(j, False)
            for k in range(8):
                sp_pages("v", 6 + k // 4, k % 4, k, (v_used, 8 * 2 + k + RING + 1) if k < RING else (v_used, 24 + k - RING + 1))
            for u in range(WOUT[2]):
                load(WOUT, u, cols(i["w_out"], slice(UC * u, UC * u + UC)), NCH * UC, (v_used, 24 + RING + u + 1))
            load_up(UP2, 1)
            load_down(DN2, 1)
            for tt in range(3):
                n = P if tt < 2 else NS
                sp.wait_ge(out_row, 2 * tt + 2)
                dst = o["y_prompt"][0, P * tt:P * tt + P, :] if tt < 2 else o["y_sample"].rearrange("b t f -> (b t) f")
                sp.dma_start(dst, yrow[0:n, tt, :]).then_inc(stored, 16)
            sp.wait_ge(stored, 16 * (1 + 3))
            sp.wait_ge(stored_early, 16 * N_EARLY)

        @block.gpsimd
        def _(pool):
            def scale_x(n):
                pool.wait_ge(m_ready, (8, 16, 32)[n])
                pool.tensor_scalar(xT[:, :, :], xT[:, :, :], ALPHA, None, ALU.mult).then_inc(ax_ready, 1)

            scale_x(0)
            pool.wait_ge(w_used, DN1[0] + DN1[2])
            pool.memset(cbuf[:, :, 0:ST], 0.0).then_inc(pad_ready, 1)
            pool.memset(qbh[:, :].bitcast(F32), 0.0).then_inc(q_zero, 1)
            pool.memset(qbl[:, :].bitcast(F32), 0.0).then_inc(q_zero, 1)
            pool.memset(koh[:, :, :].bitcast(F32), 0.0).then_inc(q_zero, 1)
            pool.memset(kol[:, :, :].bitcast(F32), 0.0).then_inc(q_zero, 1)
            scale_x(1)
            pool.wait_ge(glu_ready, NCC)
            pool.wait_ge(st_in, 2)
            pool.wait_ge(pad_ready, 1)
            steps = 0
            for c in range(NCC):
                acc = yT[:, NCC + c, :]
                sam = cbuf[:, c, ST + SEQ:CB].rearrange("p (b k) -> p b k", b=DB)
                for k in range(TAPS):
                    w = dwT[:, NCC * k + c:NCC * k + c + 1]
                    to = acc if k == 0 else tmp[:, k % 2, :]
                    more = (par2[:, c:c + 1], ALU.mult, ALU.add) if k == 0 else (None, ALU.mult)
                    pool.tensor_scalar(to[:, 0:SEQ], cbuf[:, c, k:k + SEQ], w, *more)
                    pool.tensor_scalar(to[:, SEQ:T].rearrange("p (b t) -> p b t", b=DB), sam[:, :, k:k + DT], w, *more).then_inc(pool_step, 1)
                    steps += 1
                    if k:
                        pool.wait_ge(pool_step, steps)
                        last = k == TAPS - 1
                        pool.tensor_tensor(acc, acc, to, ALU.add).then_inc(conv_ready if last else pool_step, 1)
                        steps += not last
                pool.wait_ge(conv_ready, c + 1)
            scale_x(2)

        @block.scalar
        def _(act):
            def hi(phase, u, size=NCH * UC, more=0):
                k = (phase[1] + u) % RING
                act.wait_ge(raw_in[k], raw_count_w(phase, u) + 16 // RING * more)
                n = phase[0] + u - slots(phase) + 1
                if n > 0:
                    act.wait_ge(w_used, n + more)
                act.copy(whi[:, slot_w(phase, u), 0:size], raw[:, k, 0:size]).then_inc(w_hi, 1)

            def hi_down(phase, u):
                hi(phase, u, DN_CHUNKS[u % 3] * UC)

            act.dma_start(prow[0:8, 3, :], i["c_prompt"].rearrange("b (r f) -> (b r) f", f=P)).then_inc(ld_c, 16)
            act.dma_start(prow[8:72, 3, :], i["c_sample"].rearrange("b (r f) -> (b r) f", f=P)).then_inc(ld_c, 16)
            act.dma_start(prow[0:72, 0, :], i["b_ada"].rearrange("o (r f) -> (o r) f", f=P)).then_inc(ld_par, 16)
            act.dma_start(prow[72:96, 0, :], i["ln_g"].rearrange("o j (r f) -> (o j r) f", f=P)).then_inc(ld_par, 16)
            act.dma_start(prow[96:120, 0, :], i["ln_b"].rearrange("o j (r f) -> (o j r) f", f=P)).then_inc(ld_par, 16)
            for n, name in enumerate(("b_dw", "gn_g", "gn_b", "beta_attn", "beta_conv")):
                act.dma_start(prow[4 * n:4 * n + 4, 1, :], i[name].rearrange("o (r f) -> (o r) f", f=P)).then_inc(ld_par, 16)
            act.dma_start(prow[0:TAPS * NCC, 2, :], i["w_dw"].rearrange("o k (r f) -> (o k r) f", f=P)).then_inc(ld_par, 16)
            act.wait_ge(c_t, 1)
            act.activation(cT[:, :], bank[:, 0, 384:456], ACT.Silu).then_inc(c_silu, 1)
            act.wait_ge(c_silu, 1)
            act.copy(chl[:, :, 0:9].rearrange("p k r -> p r k"), cT[:, :].rearrange("p (r k) -> p r k", r=9)).then_inc(c_hi, 1)
            for u in range(3):
                hi(ADA, u)

            def ada_rows(a, a_, used):
                act.wait_ge(w_used, used)
                if a_ >= 2:
                    act.wait_ge(ada_t, a - 1)
                act.copy(rows[:, a_ % 2, :], bank[0:18, 4 + a_ % 2, 0:UC]).then_inc(ada_row, 1)

            def split_m(u):
                for n in mod_chunks(u):
                    act.wait_ge(m_ready, n + 1)
                    act.copy(mh[:, n, :], yT[:, n, :]).then_inc(mh_ready, 1)

            for u in range(ADA[2]):
                ada_rows(u, u, u + 1)
                if u + 3 < ADA[2]:
                    hi(ADA, u + 3)
                else:
                    hi(UP1, u + 3 - ADA[2])
                if u == X_AT:
                    for n in range(6):
                        act.wait_ge(x_t, n + 1)
                        tt, half = n // 2, n % 2
                        w = P if tt < 2 else NS
                        act.copy(xT[:, 4 * half:4 * half + 4, P * tt:P * tt + w],
                                 bank[:, n % 4, :].rearrange("p (c t) -> p c t", t=P)[:, :, 0:w]).then_inc(x_in, 1)
                split_m(u - 1)
            split_m(ADA[2] - 1)

            def up(ffn, phase, down):
                gr, sr, hr, hhr = g_ready[ffn], silu_ready[ffn], h_ready[ffn], hh_ready[ffn]

                per = stride(ffn)

                def body(pair, pair_):
                    more = per * (pair - pair_)

                    def hi_next(n):
                        n += per * pair_
                        if n < phase[2]:
                            hi(phase, n, more=more)
                        else:
                            hi_down(down, n - phase[2])

                    for cc in range(2):
                        if cc == 0:
                            act.wait_ge(gr, pair + 1)
                        else:
                            act.wait_ge(w_used, phase[0] + per * pair + 1)
                        if pair_:
                            act.wait_ge(hr, 2 * pair + cc - 1)
                        act.activation(tmp[:, cc, :], bank[:, cc, 0:T], ACT.Silu).then_inc(sr, 1)
                    if ffn == 0:
                        hi_next(3)
                        ada_rows(ADA[2] + 2 * pair, ADA[2] + 2 * pair_, phase[0] + per * pair + 2)
                        hi_next(4)
                    else:
                        hi_next(2)
                        hi_next(3)
                    for cc in range(2):
                        act.wait_ge(hr, 2 * pair + cc + 1)
                        act.copy(hh[:, bass.ds(2 * pair + cc, 1), :].rearrange("p a t -> p (a t)"), tmp[:, 2 + cc, :]).then_inc(hhr, 1)
                    if ffn == 0:
                        hi_next(5)
                        ada_rows(ADA[2] + 2 * pair + 1, ADA[2] + 2 * pair_ + 1, phase[0] + per * pair + 4)
                        hi_next(6)
                up_pairs(act, ffn, body)

            def down(phase, nxt):
                ahead = slots(phase)
                for u in range(phase[2]):
                    if u + ahead < phase[2]:
                        hi_down(phase, u + ahead)
                    elif nxt is not None:
                        hi(nxt, u + ahead - phase[2])

            def norm(n):
                for q in range(4):
                    act.wait_ge(yc_ready, 4 * n + q + 1)
                    if q >= 2:
                        act.wait_ge(sq_used, 3 * n + q - 1)
                    act.activation(tmp[:, 2 * (q % 2):2 * (q % 2) + 2, :], yT[:, 2 * q:2 * q + 2, :], ACT.Square).then_inc(sq_ready, 1)
                act.wait_ge(var_ready, n + 1)
                act.activation(tmp[:, 0, :], bank[:, 1, 0:T], ACT.Sqrt, bias=con[:, C_EPS:C_EPS + 1]).then_inc(std_ready, 1)
                for q in range(NCH):
                    act.wait_ge(xn_ready, 4 * n + q // 2 + 1)
                    act.activation(xT[:, q, :], yT[:, q, :], ACT.Identity, scale=par1[:, 72 + 8 * n + q:73 + 8 * n + q],
                                   bias=par1[:, 96 + 8 * n + q:97 + 8 * n + q]).then_inc(x_ready, 1)
                    if n < 2 and q >= 1:
                        act.wait_ge(m_ready, 8 * (1 + 2 * n) + q)
                        act.copy(mh[:, q - 1, :], yT[:, q - 1, :]).then_inc(mh_ready, 1)
                if n < 2:
                    act.wait_ge(m_ready, 8 * (2 + 2 * n))
                    act.copy(mh[:, 7, :], yT[:, 7, :]).then_inc(mh_ready, 1)

            up(0, UP1, DN1)
            down(DN1, WIN)
            norm(0)

            for u, b in enumerate(WIN_ORDER):
                for cc in range(2):
                    act.wait_ge(*((win_mm, u + 1) if cc == 0 else (w_used, WIN[0] + u + 1)))
                    c = 2 * b + cc
                    src = bank[:, 2 * (u % 2) + cc, 0:T]
                    if c >= 16:
                        act.activation(yT[:, c - 16, :], src, ACT.Sigmoid).then_inc(sig_ready, 1)
                    elif c < 4:
                        act.mul(uT[:, c, :], src, HD ** -0.5).then_inc(u_out, 1)
                    elif c < 12:
                        act.copy(uT[:, c, :], src).then_inc(u_out, 1)
                if u + 3 < WIN[2]:
                    hi(WIN, u + 3)

            for g in range(2):
                act.wait_ge(st_t, g + 1)
                act.copy(cbuf[:, :, ST + SEQ + 4 * g * SB:ST + SEQ + 4 * (g + 1) * SB].rearrange("p c (b k) -> p c b k", b=4)[:, :, :, 0:ST],
                         bank[:, 4 + g, 0:480].rearrange("p (c b k) -> p c b k", c=NCC, b=4)).then_inc(st_in, 1)
            dst = [vtok[:, 0, :], vtok[:, 1, :], vsam[:, :], ktok[:, 0, :], ktok[:, 1, :], ksam]
            for n in range(6):
                act.wait_ge(tok_t, n + 1)
                w = P if n % 3 < 2 else NS
                act.copy(dst[n], bank[0:w, n % 4, :]).then_inc(tok_out, 1)
            act.wait_ge(glu_ready, NCC)
            act.copy(gsam.rearrange("p c (b t) -> p c b t", b=DB),
                     cbuf[:, :, ST + SEQ:CB].rearrange("p c (b k) -> p c b k", b=DB)[:, :, :, ST:SB]).then_inc(gs_copy, 1)
            act.wait_ge(gl_t, 1)
            act.copy(cout, bank[0:ST, 6, :]).then_inc(gl_out, 1)
            act.wait_ge(gl_t, 2)
            act.copy(csam, bank[0:NS, 7, :]).then_inc(gl_out, 1)
            act.wait_ge(u_out, 12)
            act.wait_ge(q_zero, 4)
            act.copy(khn, uT[:, 4:8, SEQ:T])
            act.copy(qh, uT[:, 0:NHP, SEQ:T]).then_inc(qs_hi, 1)
            act.wait_ge(qs_hi, 1)
            for e in range(2):
                ins = act.copy(koh[0:64, :, :].rearrange("p (m e) t -> p m e t", e=2)[:, :, e, :], khn[64 * e:64 * e + 64, :, :].bitcast(F32))
            ins.then_inc(ko_hi, 1)
            def prompt_exp(h):
                act.wait_ge(pmax_ready, h + 1)
                for q, (a, b) in enumerate(((0, P), (P, 3 * P))):
                    ins = act.activation(ps_[:, h % 3, a:b], ps_[:, h % 3, a:b], ACT.Exp, bias=pm[:, h % 3, q:q + 1],
                                         accum_out=pz[:, h % 3, q:q + 1])
                ins.then_inc(pexp, 1)

            def prompt_turned(h):
                act.wait_ge(pp_t, h + 1)
                if h >= 2:
                    act.wait_ge(pv_mm, h - 1)
                act.copy(ppT[:, h % 2, :], bank[:, 2 + h % 2, 0:384]).then_inc(pp_out, 1)

            def prompt_out(m):
                act.wait_ge(pv_mm, 2 * m + 2)
                act.copy(yT[:, m, 0:SEQ], bank[:, 4 + m % 2, 0:SEQ]).then_inc(pv_out, 1)

            prompt_exp(0)
            prompt_exp(1)
            for h in range(NH):
                if h + 2 < NH:
                    prompt_exp(h + 2)
                prompt_turned(h)
                if h and h % 2 == 0:
                    prompt_out(h // 2 - 1)
            prompt_out(NHP - 1)

            def q_high(j, b2, first=False):
                if first:
                    act.wait_ge(qs_hi, 1)
                elif b2:
                    act.wait_ge(own_ready, 2 * j + 1)
                else:
                    act.wait_ge(own_ready, 2 * j)
                for r in range(2):
                    for e in range(2):
                        at = 64 * r + QPITCH * e
                        ins = act.copy(qbh[64 * r:64 * r + 64, at:at + NHP * 2 * QPITCH].rearrange("p (m c) -> p m c", m=NHP)[:, :, 0:DT],
                                       qh[64 * e:64 * e + 64, :, bass.ds(DT * (2 * j + b2), DT)].bitcast(F32))
                ins.then_inc(q_hi, 1)

            q_high(0, 0, True)

            def act_pages(cache, seq, c, k, wait=None):
                load_pages(act, cache, seq, c, k, (2, 3), wait)

            def attn_out(j):
                act.wait_ge(at_mm, j + 1)
                act.copy(yT[:, 0:NHP, bass.ds(SEQ + 2 * DT * j, 2 * DT)].rearrange("p m (b t) -> p m b t", b=2),
                         bank[:, 7, 0:NS].rearrange("p (b m t) -> p m b t", b=2, m=NHP)).then_inc(av_evac, 1)

            def pair_body(j, first=False, last=False):
                for k in range(8):
                    for hf in range(2):
                        act.wait_ge(kt_ready, 16 * j + 2 * k + hf + 1)
                        if hf == 0 and not (first and k < 2):
                            act.wait_ge(k_used, 8 * j + k - 1)
                        act.copy(kh[:, k % 2, 2 * hf:2 * hf + 2, :], bank[:, 2 * hf:2 * hf + 2, :]).then_inc(kt_hi, 1)
                    if k < RING:
                        act_pages("k", 2 * j + (k + RING) // 4, k, k)
                    elif first:
                        act_pages("k", 2, k - RING, k)
                    else:
                        act_pages("v", 2 * (j - 1), k - RING, k)
                    if k == 4:
                        q_high(j, 1)

                def behind_values(k):
                    wait = (v_used, 8 * (j - 1) + k + 1)
                    if k < RING:
                        act_pages("v", 2 * (j - 1) + 1, k, k, wait)
                    elif last:
                        act_pages("v", 2 * j, k - RING, k, wait)
                    else:
                        act_pages("k", 2 * (j + 1), k - RING, k, wait)

                if not first:
                    for k in range(3):
                        behind_values(k)
                act.wait_ge(eb_ready, j + 1)
                for b2 in range(2):
                    ins = act.activation(s[:, b2, :], s[:, b2, :], ACT.Exp, bias=ebias[:, b2:b2 + 1], accum_out=rt[:, b2:b2 + 1])
                ins.then_inc(ex_ready, 1)
                if not last:
                    q_high(j + 1, 0)
                if not first:
                    for k in range(3, 8):
                        behind_values(k)
                for r in range(4):
                    act.wait_ge(pt_ready, 5 * j + r + 1)
                    act.copy(pT[:, 512 * r:512 * r + 512], bank[:, 4 + r % 2, :]).then_inc(pt_evac, 1)
                act.wait_ge(pt_ready, 5 * j + 5)
                act.copy(po[:, :], bank[0:NS, 6, 0:2 * P]).then_inc(pt_evac, 1)
                if not first:
                    attn_out(j - 1)

            act.wait_ge(stored_early, 16 * N_EARLY)
            pair_body(0, first=True)
            with act.Fori(1, 3) as j:
                pair_body(j)
            pair_body(3, last=True)

            for c in range(NCC):
                act.wait_ge(gc_ready, c + 1)
                act.activation(tmp[:, c, :], yT[:, NCC + c, :], ACT.Square).then_inc(gq_ready, 1)
            for k in range(RING):
                act_pages("v", 7, k, k, (v_used, 24 + k + 1))
            for c in range(NCC):
                act.wait_ge(gv_mm, c + 1)
                act.activation(tmp[:, c, :], bank[:, 4 + c, 0:T], ACT.Sqrt, bias=con[:, C_EPS:C_EPS + 1]).then_inc(gs_ready, 1)
            for c in range(NCC):
                act.wait_ge(gx_ready, c + 1)
                act.activation(tmp[:, c, :], yT[:, NCC + c, :], ACT.Silu, scale=par2[:, 4 + c:5 + c], bias=par2[:, 8 + c:9 + c]).then_inc(gy_ready, 1)
            for n, c in enumerate(MIX_ORDER):
                act.wait_ge(m_ready, 16 + n + 1)
                act.copy(mh[:, c, :], yT[:, c, :]).then_inc(mh_ready, 1)
                if n == NCC - 1:
                    act.wait_ge(k_used, 32)
                    attn_out(3)
                    hi(WOUT, 0)
                    hi(WOUT, 1)
            for u in range(WOUT[2]):
                if u < 2:
                    hi(WOUT, u + 2)
                else:
                    hi(UP2, u - 2)
            norm(1)
            up(1, UP2, DN2)
            down(DN2, None)
            norm(2)
            for n in range(6):
                act.wait_ge(out_t, n + 1)
                tt, half = n // 2, n % 2
                w = P if tt < 2 else NS
                act.copy(yrow[0:w, tt, 512 * half:512 * half + 512], bank[0:w, 2 + n, :]).then_inc(out_row, 1)

        @block.vector
        def _(dve):
            step = [0]

            def link(ins):
                ins.then_inc(dve_step, 1)
                step[0] = step[0] + 1
                dve.wait_ge(dve_step, step[0])

            def lo(phase, u, size=NCH * UC, more=0):
                k = (phase[1] + u) % RING
                dve.wait_ge(w_hi, phase[0] + u + 1 + more)
                dve.tensor_tensor(wlo[:, slot_w(phase, u), 0:size], raw[:, k, 0:size], whi[:, slot_w(phase, u), 0:size].bitcast(F32),
                                  ALU.subtract).then_inc(w_lo, 1)

            def lo_down(phase, u):
                lo(phase, u, DN_CHUNKS[u % 3] * UC)

            dve.wait_ge(c_hi, 1)
            dve.tensor_tensor(chl[:, :, 9:18].rearrange("p k r -> p r k"), cT[:, :].rearrange("p (r k) -> p r k", r=9),
                              chl[:, :, 0:9].rearrange("p k r -> p r k").bitcast(F32), ALU.subtract).then_inc(c_lo, 1)
            for u in range(3):
                lo(ADA, u)
            dve.wait_ge(par_t, 1)
            dve.tensor_copy(par1[:, :], bank[:, 1, 0:120]).then_inc(par_ready, 1)
            dve.tensor_copy(par2[:, :], bank[:, 1, 128:148])
            dve.tensor_copy(dwT[:, :], bank[:, 1, 256:380]).then_inc(par_ready, 1)
            dve.wait_ge(par_ready, 2)
            one = par1[:, 0:72].rearrange("p (a b n) -> p a b n", a=3, b=3)[:, :, 1, :]
            link(dve.tensor_scalar(one, one, 1.0, None, ALU.add))

            def ada_turn(a, a_):
                dve.wait_ge(ada_t, a + 1)
                dve.tensor_tensor(adaT[:, bass.ds(2 * a, 2), :], bank[:, 6 + a_ % 2, 0:18].rearrange("p (c r) -> p c r", c=2),
                                  par1[:, bass.ds(2 * a, 2)].unsqueeze(2).to_broadcast([P, 2, 9]), ALU.add).then_inc(ada_out, 1)

            def half_gate(sub):
                g = adaT[:, (3 * sub + 2) * NCH:(3 * sub + 3) * NCH, :]
                link(dve.tensor_scalar(g, g, 0.5, None, ALU.mult))

            def samples(ap):
                return ap[:, SEQ:T].rearrange("p (b t) -> p b t", b=DB)

            def vec(sub, kind, n):
                return adaT[:, (3 * sub + kind) * NCH + n, :]

            def per_seq(v):
                return v[:, 1:9].unsqueeze(2).to_broadcast([P, DB, DT])

            def modulate(sub, n):
                x, y = xT[:, n, :], yT[:, n, :]
                sc, sh = vec(sub, 1, n), vec(sub, 0, n)
                dve.tensor_scalar(y[:, 0:SEQ], x[:, 0:SEQ], sc[:, 0:1], sh[:, 0:1], ALU.mult, ALU.add)
                link(dve.tensor_tensor(samples(y), samples(x), per_seq(sc), ALU.mult))
                dve.tensor_tensor(samples(y), samples(y), per_seq(sh), ALU.add).then_inc(m_ready, 1)

            def low(n, count):
                dve.wait_ge(mh_ready, count)
                dve.tensor_tensor(ml[:, n, :], yT[:, n, :], mh[:, n, :].bitcast(F32), ALU.subtract).then_inc(ml_ready, 1)

            def add_residual(sub, n, src, ready):
                dve.wait_ge(*ready)
                g = vec(sub, 2, n)
                dve.scalar_tensor_tensor(yT[:, n, 0:SEQ], src[:, 0:SEQ], g[:, 0:1], xT[:, n, 0:SEQ], ALU.mult, ALU.add)
                link(dve.tensor_tensor(samples(yT[:, n, :]), samples(src), per_seq(g), ALU.mult))
                dve.tensor_tensor(samples(yT[:, n, :]), samples(yT[:, n, :]), samples(xT[:, n, :]), ALU.add).then_inc(y_ready, 1)

            def up(ffn, phase, down):
                sr, ur, hr, hhr, hlr = silu_ready[ffn], u_ready[ffn], h_ready[ffn], hh_ready[ffn], hl_ready[ffn]

                per = stride(ffn)

                def body(pair, pair_):
                    def lo_next(n):
                        n += per * pair_
                        if n < phase[2]:
                            lo(phase, n, more=per * (pair - pair_))
                        else:
                            lo_down(down, n - phase[2])

                    if ffn == 0:
                        lo_next(3)
                        ada_turn(ADA[2] + 2 * pair - 1, ADA[2] + 2 * pair_ - 1)
                        lo_next(4)
                    else:
                        lo_next(2)
                    for cc in range(2):
                        dve.wait_ge(sr, 2 * pair + cc + 1)
                        dve.wait_ge(*((ur, pair + 1) if cc == 0 else (w_used, phase[0] + per * pair + per // 2 + 1)))
                        if pair_:
                            dve.wait_ge(hlr, 2 * pair + cc - 1)
                        dve.tensor_tensor(tmp[:, 2 + cc, :], bank[:, 2 + cc, 0:T], tmp[:, cc, :], ALU.mult).then_inc(hr, 1)
                    if ffn == 0:
                        ada_turn(ADA[2] + 2 * pair, ADA[2] + 2 * pair_)
                        lo_next(5)
                    else:
                        lo_next(3)
                    for cc in range(2):
                        dve.wait_ge(hhr, 2 * pair + cc + 1)
                        f = bass.ds(2 * pair + cc, 1)
                        dve.tensor_tensor(hl[:, f, :].rearrange("p a t -> p (a t)"), tmp[:, 2 + cc, :],
                                          hh[:, f, :].rearrange("p a t -> p (a t)").bitcast(F32), ALU.subtract).then_inc(hlr, 1)
                    if ffn == 0:
                        lo_next(6)
                up_pairs(dve, ffn, body)

            def down(sub, phase, nxt, n0):
                dve.wait_ge(ax_ready, sub + 1)
                ahead = slots(phase)
                for u in range(phase[2]):
                    if u + ahead < phase[2]:
                        lo_down(phase, u + ahead)
                    elif nxt is not None:
                        lo(nxt, u + ahead - phase[2])
                    if u % 3 == 2:
                        for cc in range(2):
                            n = 2 * (u // 3) + cc
                            add_residual(sub, n, bank[:, 4 + 2 * (u // 3 % 2) + cc, :],
                                         (n_ready, n0 + u // 3 + 1) if cc == 0 else (w_used, phase[0] + u + 1))

            def norm(n):
                dve.wait_ge(mean_ready, n + 1)
                dve.wait_ge(y_ready, 8 * (n + 1))
                for q in range(4):
                    y = yT[:, 2 * q:2 * q + 2, :]
                    dve.tensor_tensor(y, y, bank[:, 0:1, 0:T].to_broadcast([P, 2, T]), ALU.subtract).then_inc(yc_ready, 1)
                dve.wait_ge(std_ready, n + 1)
                link(dve.reciprocal(tmp[:, 1, :], tmp[:, 0, :]))
                dve.wait_ge(sq_ready, 4 * n + 4)

                def scale(q):
                    y = yT[:, 2 * q:2 * q + 2, :]
                    dve.tensor_tensor(y, y, tmp[:, 1:2, :].to_broadcast([P, 2, T]), ALU.mult).then_inc(xn_ready, 1)

                scale(0)
                for q in range(NCH):
                    if q % 2 == 0 and q < 6:
                        scale(q // 2 + 1)
                    if n < 2:
                        dve.wait_ge(x_ready, 8 * n + q + 1)
                        modulate(n + 1, q)
                        if q:
                            low(q - 1, 8 * (n + 1 + (n == 1)) + q)
                if n < 2:
                    low(7, 8 * (n + 1 + (n == 1)) + 8)

            for u in range(ADA[2]):
                if u + 3 < ADA[2]:
                    lo(ADA, u + 3)
                else:
                    lo(UP1, u + 3 - ADA[2])
                if u >= 1:
                    ada_turn(u - 1, u - 1)
                if u == MOD_AT:
                    dve.wait_ge(ada_out, 8)
                    dve.wait_ge(x_in, 6)
                for n in mod_chunks(u):
                    modulate(0, n)
                for n in mod_chunks(u - 1):
                    low(n, n + 1)
            for n in mod_chunks(ADA[2] - 1):
                low(n, n + 1)
            dve.wait_ge(ada_out, 12)
            half_gate(0)

            up(0, UP1, DN1)
            ada_turn(ADAN - 1, ADAN - 1)
            dve.wait_ge(ada_out, ADAN)
            half_gate(2)
            down(0, DN1, WIN, 0)
            norm(0)

            for u, b in enumerate(WIN_ORDER):
                if u + 3 < WIN[2]:
                    lo(WIN, u + 3)
                if u in (2, 3):
                    for cc in range(2):
                        c = 2 * (u - 2) + cc
                        dve.wait_ge(*((win_mm, u + 1) if cc == 0 else (w_used, WIN[0] + u + 1)))
                        dve.wait_ge(sig_ready, c + 1)
                        src = bank[:, 2 * (u % 2) + cc, :]
                        dve.tensor_tensor(cbuf[:, c, ST:ST + SEQ], src[:, 0:SEQ], yT[:, c, 0:SEQ], ALU.mult)
                        dve.tensor_tensor(cbuf[:, c, ST + SEQ:CB].rearrange("p (b k) -> p b k", b=DB)[:, :, ST:SB],
                                          samples(src), samples(yT[:, c, :]), ALU.mult).then_inc(glu_ready, 1)

            def prompt_scores(h):
                dve.wait_ge(ps_mm, h + 1)
                if h >= 3:
                    dve.wait_ge(pp_t, h - 2)
                sc = ps_[:, h % 3, :]
                dve.scalar_tensor_tensor(sc, con[:, C_REL:C_REL + 384], 2.0 ** -(h + 1), bank[:, h % 2, 0:384], ALU.mult, ALU.add).then_inc(ps_ready, 1)
                dve.wait_ge(ps_ready, h + 1)
                dve.tensor_reduce(pm[:, h % 3, 0:1], sc[:, 0:P], AX, ALU.max, negate=True)
                dve.tensor_reduce(pm[:, h % 3, 1:2], sc[:, P:3 * P], AX, ALU.max, negate=True).then_inc(pmax_ready, 1)

            def prompt_probs(h):
                dve.wait_ge(pexp, h + 1)
                link(dve.reciprocal(pr[:, h % 3, :], pz[:, h % 3, :]))
                dve.tensor_scalar(ps_[:, h % 3, 0:P], ps_[:, h % 3, 0:P], pr[:, h % 3, 0:1], None, ALU.mult)
                dve.tensor_scalar(ps_[:, h % 3, P:3 * P], ps_[:, h % 3, P:3 * P], pr[:, h % 3, 1:2], None, ALU.mult).then_inc(pp_ready, 1)

            prompt_scores(0)
            prompt_scores(1)
            for h in range(NH):
                if h + 2 < NH:
                    prompt_scores(h + 2)
                prompt_probs(h)
            dve.wait_ge(qs_hi, 1)
            dve.tensor_tensor(kln, uT[:, 4:8, SEQ:T], khn.bitcast(F32), ALU.subtract)
            dve.tensor_tensor(ql, uT[:, 0:NHP, SEQ:T], qh.bitcast(F32), ALU.subtract).then_inc(qs_lo, 1)
            dve.wait_ge(qs_lo, 1)
            dve.wait_ge(ko_hi, 1)
            for e in range(2):
                ins = dve.tensor_copy(kol[0:64, :, :].rearrange("p (m e) t -> p m e t", e=2)[:, :, e, :], kln[64 * e:64 * e + 64, :, :].bitcast(F32))
            ins.then_inc(ko_lo, 1)

            def q_low(j, b2, first=False):
                if first:
                    dve.wait_ge(qs_lo, 1)
                dve.wait_ge(q_hi, 2 * j + b2 + 1)
                for r in range(2):
                    for e in range(2):
                        at = 64 * r + QPITCH * e
                        ins = dve.tensor_copy(qbl[64 * r:64 * r + 64, at:at + NHP * 2 * QPITCH].rearrange("p (m c) -> p m c", m=NHP)[:, :, 0:DT],
                                              ql[64 * e:64 * e + 64, :, bass.ds(DT * (2 * j + b2), DT)].bitcast(F32))
                ins.then_inc(q_lo, 1)

            def score_chunk(j, g):
                b2, n = g // 2, 4 * (g % 2)
                dve.wait_ge(k_used, 8 * j + 2 * g + 2)
                sbk = bank[:, 4 + g % 2, :].rearrange("p (n k) -> p n k", n=4)
                sc = s[:, b2, P * n:P * n + 512].rearrange("p (n k) -> p n k", n=4)
                dve.tensor_reduce(gsum[:, b2, n:n + 4], sbk, AX, ALU.add)
                dve.scalar_tensor_tensor(sc, con[:, C_POS:C_POS + P].unsqueeze(1).to_broadcast([P, 4, P]), con[:, C_M:C_M + 1], sbk,
                                         ALU.mult, ALU.add).then_inc(s_evac, 1)
                dve.wait_ge(s_evac, 4 * j + g + 1)
                dve.tensor_reduce(bmax[:, b2, n:n + 4], sc, AX, ALU.max)

            def attn_rows(j):
                for b2 in range(2):
                    dve.wait_ge(acc_ready, 2 * j + b2 + 1)
                    for g in range(4):
                        rr = slice(32 * g, 32 * g + 32)
                        acc = bank[rr, 2 * b2 + g % 2, :].rearrange("p (h r d) -> p h r d", h=4, r=2)[:, :, g // 2, :]
                        ins = dve.tensor_tensor(ahead[rr, b2], acc, con[rr, C_HEAD:C_HEAD + 4].unsqueeze(2).to_broadcast([32, 4, HD]), ALU.mult)
                    link(ins)
                    dve.tensor_reduce(arow[:, b2, :], ahead[:, b2].rearrange("p h d -> p d h"), AX, ALU.add).then_inc(arow_ready, 1)

            def pair_body(j, first=False, last=False):
                for k in range(8):
                    for hf in range(2):
                        dve.wait_ge(kt_hi, 16 * j + 2 * k + hf + 1)
                        dve.tensor_tensor(kl[:, k % 2, 2 * hf:2 * hf + 2, :], bank[:, 2 * hf:2 * hf + 2, :],
                                          kh[:, k % 2, 2 * hf:2 * hf + 2, :].bitcast(F32), ALU.subtract).then_inc(kt_lo, 1)
                    if k == 2 and not first:
                        dve.wait_ge(pt_ready, 5 * j)
                    if k == 4:
                        q_low(j, 1)
                    if k % 2 == 0 and k:
                        score_chunk(j, k // 2 - 1)
                score_chunk(j, 3)
                dve.wait_ge(own_ready, 2 * j + 2)
                for b2 in range(2):
                    ins = dve.tensor_tensor(s[:, b2, PAST // 2:], bank[:, 6, NS * b2:NS * b2 + NS],
                                            con[:, bass.ds(C_OWN + 56 - DT * (2 * j + b2), NS)], ALU.add)
                ins.then_inc(gsum_ready, 1)
                dve.wait_ge(gsum_ready, j + 1)
                dve.wait_ge(gate_mm, j + 1)
                link(dve.tensor_copy(gate[:, :, :], bank[:, 6, 256:272].rearrange("p (b n) -> p b n", b=2)))
                dve.tensor_reduce(bmax[:, 0:1, 8:9], s[:, 0:1, PAST // 2:], AX, ALU.max)
                for b2 in range(2):
                    ins = dve.max(gmax[:, b2, :], gate[:, b2, :])
                link(ins)
                dve.tensor_reduce(bmax[:, 1:2, 8:9], s[:, 1:2, PAST // 2:], AX, ALU.max)
                for b2 in range(2):
                    ins = dve.max_index(gidx[:, b2, :], gmax[:, b2, :], gate[:, b2, :])
                link(ins)
                link(dve.tensor_copy(gidf[:, :, :], gidx[:, :, :]))
                for b2 in range(2):
                    ins = dve.tensor_tensor(hit[:, b2], con[:, C_IOTA:C_IOTA + 8].unsqueeze(2).to_broadcast([P, 8, 3]),
                                            gidf[:, b2, 0:3].unsqueeze(1).to_broadcast([P, 8, 3]), ALU.is_equal)
                link(ins)
                link(dve.tensor_reduce(ebase[:, :, :], hit[:, :, :, :], AX, ALU.add))
                link(dve.tensor_scalar(ebase[:, :, :], ebase[:, :, :], -1.0, -NEG, ALU.add, ALU.mult))
                link(dve.tensor_tensor(ebase[:, :, :], ebase[:, :, :], con[:, C_RC:C_RC + 8].unsqueeze(1).to_broadcast([P, 2, 8]), ALU.add))
                link(dve.tensor_tensor(bmax[:, :, 0:8], bmax[:, :, 0:8], ebase[:, :, :], ALU.add))
                dve.tensor_reduce(nmax[:, :], bmax[:, :, :], AX, ALU.max, negate=True).then_inc(nmax_ready, 1)
                for b2 in range(2):
                    sc = s[:, b2, 0:PAST // 2].rearrange("p (n k) -> p n k", n=NBLK)
                    dve.tensor_tensor(sc, sc, ebase[:, b2, :].unsqueeze(2).to_broadcast([P, NBLK, P]), ALU.add)
                dve.wait_ge(swap_mm, j + 1)
                dve.tensor_tensor(ebias[:, :], nmax[:, :], bank[:, 6, 288:290], ALU.min).then_inc(eb_ready, 1)
                dve.wait_ge(rsum_mm, j + 1)
                link(dve.reciprocal(ri[:, :], bank[:, 6, 320:322]))
                dve.tensor_scalar(s[:, 0, :], s[:, 0, :], ri[:, 0:1], None, ALU.mult)
                dve.tensor_scalar(s[:, 1, :], s[:, 1, :], ri[:, 1:2], None, ALU.mult).then_inc(p_ready, 1)
                if not first:
                    attn_rows(j - 1)
                if not last:
                    q_low(j + 1, 0)

            q_low(0, 0, True)
            dve.wait_ge(stored_early, 16 * N_EARLY)
            pair_body(0, first=True)
            before = step[0]
            PAIR_STEPS = 12
            with dve.Fori(1, 3) as j:
                step[0] = before + PAIR_STEPS * (j - 1)
                pair_body(j)
            step[0] = before + 2 * PAIR_STEPS
            pair_body(3, last=True)

            for c in range(NCC):
                dve.wait_ge(gm_mm, c + 1)
                y = yT[:, NCC + c, :]
                dve.tensor_tensor(y, y, bank[:, 4 + c, 0:T], ALU.subtract).then_inc(gc_ready, 1)
            for c in range(NCC):
                dve.wait_ge(gs_ready, c + 1)
                y = yT[:, NCC + c, :]
                link(dve.reciprocal(tmp[:, c, :], tmp[:, c, :]))
                dve.tensor_tensor(y, y, tmp[:, c, :], ALU.mult).then_inc(gx_ready, 1)
            for c in range(NCC):
                dve.wait_ge(gy_ready, c + 1)
                dve.tensor_scalar(yT[:, NCC + c, :], tmp[:, c, :], par2[:, 16 + c:17 + c], None, ALU.mult).then_inc(m_ready, 1)
                if c:
                    low(NCC + c - 1, 16 + c)
            low(7, 16 + NCC)
            attn_rows(3)
            lo(WOUT, 0)
            lo(WOUT, 1)
            dve.wait_ge(av_evac, 4)
            dve.wait_ge(pv_out, 4)
            for c in range(NHP):
                dve.tensor_scalar(yT[:, c, :], yT[:, c, :], par2[:, 12 + c:13 + c], None, ALU.mult).then_inc(m_ready, 1)
                if c:
                    low(c - 1, 16 + NCC + c)
            low(NHP - 1, 24)

            dve.wait_ge(ax_ready, 2)
            for u in range(WOUT[2]):
                if u < 2:
                    lo(WOUT, u + 2)
                else:
                    lo(UP2, u - 2)
                for cc in range(2):
                    n = 2 * u + cc
                    add_residual(1, n, bank[:, 4 + 2 * (u % 2) + cc, :], (n_ready, 4 + u + 1) if cc == 0 else (w_used, WOUT[0] + u + 1))
            norm(1)
            up(1, UP2, DN2)
            down(2, DN2, None, 8)
            norm(2)

        @block.tensor
        def _(pe):
            pe.wait_ge(ld_con, 16)
            pe.wait_ge(ld_c, 32)
            pe.transpose(bank[:, 0, 384:456], prow[0:72, 3, :], ident[0:72, 0:72]).then_inc(c_t, 1)

            def turn_params():
                pe.wait_ge(ld_par, 16 * 9)
                pe.transpose(bank[:, 1, 0:120], prow[0:120, 0, :], ident[0:120, 0:120])
                pe.transpose(bank[:, 1, 128:148], prow[0:20, 1, :], ident[0:20, 0:20])
                pe.transpose(bank[:, 1, 256:380], prow[0:TAPS * NCC, 2, :], ident[0:124, 0:124]).then_inc(par_t, 1)

            def turn_x():
                pe.wait_ge(ld_x, 32)
                pe.wait_ge(par_ready, 2)
                for n in range(6):
                    tt, half = n // 2, n % 2
                    w = P if tt < 2 else NS
                    if n >= 4:
                        pe.wait_ge(x_in, n - 3)
                    for c in range(4):
                        ins = pe.transpose(bank[:, n % 4, P * c:P * c + w], xrow[0:w, tt, 512 * half + P * c:512 * half + P * c + P], ident[0:w, 0:w])
                    ins.then_inc(x_t, 1)

            def ada_turn(a, a_):
                pe.wait_ge(ada_row, a + 1)
                if a_ >= 2:
                    pe.wait_ge(ada_out, a - 1)
                for cc in range(2):
                    ins = pe.matmul(bank[:, 6 + a_ % 2, 9 * cc:9 * cc + 9], rows[:, a_ % 2, P * cc:P * cc + P], con[0:18, C_SEL:C_SEL + 9],
                                    start=True, stop=True)
                ins.then_inc(ada_t, 1)

            def ada_product(a, a_, slot, ready):
                pe.wait_ge(w_lo, ready)
                if a_ >= 2:
                    pe.wait_ge(ada_row, a - 1)
                for kk in range(NCH):
                    for x, w in enumerate((whi, wlo)):
                        ins = pe.matmul(bank[0:18, 4 + a_ % 2, 0:UC], chl[:, kk, :], w[:, slot, UC * kk:UC * kk + UC],
                                        start=(kk == 0 and x == 0), stop=(kk == NCH - 1 and x == 1))
                ins.then_inc(w_used, 1)

            pe.wait_ge(c_lo, 1)
            for u in range(ADA[2]):
                ada_product(u, u, slot_w(ADA, u), u + 1)
                if u == 1:
                    turn_params()
                if u >= 1:
                    ada_turn(u - 1, u - 1)
                if u == X_AT:
                    turn_x()

            def product(b, slot, cc, parts, start=True, stop=True, ready=None):
                for n, (kk, h_, l_) in enumerate(parts):
                    if ready is not None:
                        ready(n)
                    c = slice(UC * kk + P * cc, UC * kk + P * cc + P)
                    pe.matmul(bank[:, b, 0:T], whi[:, slot, c], h_, start=(start and n == 0), stop=False)
                    pe.matmul(bank[:, b, 0:T], whi[:, slot, c], l_, start=False, stop=False)
                    ins = pe.matmul(bank[:, b, 0:T], wlo[:, slot, c], h_, start=False, stop=(stop and n == len(parts) - 1))
                return ins

            def m_parts(order):
                return [(kk, mh[:, kk, :], ml[:, kk, :]) for kk in order]

            def up(ffn, phase, ml0):
                gr, sr, ur, hr = g_ready[ffn], silu_ready[ffn], u_ready[ffn], h_ready[ffn]

                per = stride(ffn)

                def body(pair, pair_):
                    for x in range(2):
                        u, u_ = per * pair + per // 2 * x, per * pair_ + per // 2 * x
                        pe.wait_ge(w_lo, phase[0] + u + 1)
                        for cc in range(2):
                            if pair_:
                                pe.wait_ge((sr, hr)[x], 2 * pair + cc - 1)
                            ready = (lambda n: pe.wait_ge(ml_ready, ml0 + n + 1)) if pair_ == 0 and x == 0 and cc == 0 else None
                            ins = product(2 * x + cc, slot_w(phase, u_), cc, m_parts(range(NCH)), ready=ready)
                            ins.then_inc((gr, ur)[x] if cc == 0 else w_used, 1)
                            if ffn == 0 and cc == 0:
                                ada_turn(ADA[2] + 2 * pair + x - 1, ADA[2] + 2 * pair_ + x - 1)
                        if ffn == 0:
                            ada_product(ADA[2] + 2 * pair + x, ADA[2] + 2 * pair_ + x, slot_w(phase, u_ + 1), phase[0] + u + 2)
                up_pairs(pe, ffn, body)
                if ffn == 0:
                    ada_turn(ADAN - 1, ADAN - 1)

            def down(ffn, phase, n0):
                hlr = hl_ready[ffn]
                for u in range(phase[2]):
                    nb, third = u // 3, u % 3
                    if ffn == 0 and u == 3:
                        pe.wait_ge(ada_out, ADAN)
                    pe.wait_ge(w_lo, phase[0] + u + 1)
                    for cc in range(2):
                        if nb >= 2 and third == 0:
                            pe.wait_ge(y_ready, n0 + 2 * (nb - 2) + cc + 1)
                        ready = (lambda n: pe.wait_ge(hlr, 8 * third + n + 1)) if nb == 0 and cc == 0 else None
                        parts = [(kk, hh[:, 8 * third + kk, :], hl[:, 8 * third + kk, :]) for kk in range(DN_CHUNKS[third])]
                        ins = product(4 + 2 * (nb % 2) + cc, slot_w(phase, u), cc, parts, start=third == 0, stop=third == 2, ready=ready)
                        if cc:
                            ins.then_inc(w_used, 1)
                        elif third == 2:
                            ins.then_inc(n_ready, 1)

            def norm(n):
                for q in range(NCH):
                    pe.wait_ge(y_ready, 8 * n + q + 1)
                    ins = pe.matmul(bank[:, 0, 0:T], lnones, yT[:, q, :], start=(q == 0), stop=(q == NCH - 1))
                ins.then_inc(mean_ready, 1)
                for q in range(4):
                    pe.wait_ge(sq_ready, 4 * n + q + 1)
                    for x in range(2):
                        ins = pe.matmul(bank[:, 1, 0:T], lnones, tmp[:, 2 * (q % 2) + x, :], start=(q == 0 and x == 0), stop=(q == 3 and x == 1))
                    ins.then_inc(sq_used if q < 3 else var_ready, 1)

            up(0, UP1, 0)
            down(0, DN1, 0)
            norm(0)

            for u, b in enumerate(WIN_ORDER):
                pe.wait_ge(w_lo, WIN[0] + u + 1)
                for cc in range(2):
                    if u in (2, 3):
                        pe.wait_ge(sig_ready, 2 * (u - 2) + cc + 1)
                    elif u in (4, 5):
                        pe.wait_ge(glu_ready, 2 * (u - 4) + cc + 1)
                    elif u >= 6:
                        pe.wait_ge(u_out, 2 * (u - 6) + cc + 1)
                    else:
                        pe.wait_ge(x_ready, 1)
                    ready = (lambda n: pe.wait_ge(ml_ready, 8 + n + 1)) if u == 0 and cc == 0 else None
                    ins = product(2 * (u % 2) + cc, slot_w(WIN, u), cc, m_parts(range(NCH)), ready=ready)
                    ins.then_inc(win_mm if cc == 0 else w_used, 1)

            pe.wait_ge(ld_state, 32)
            for g in range(2):
                for c in range(NCC):
                    ins = pe.transpose(bank[:, 4 + g, 120 * c:120 * c + 120], strow[:, g, P * c:P * c + P], ident[0:120, 0:120])
                ins.then_inc(st_t, 1)
            pe.wait_ge(u_out, 12)
            for n in range(6):
                w = P if n % 3 < 2 else NS
                if n >= 4:
                    pe.wait_ge(tok_out, n - 3)
                for c in range(NHP):
                    ins = pe.transpose(bank[0:w, n % 4, P * c:P * c + P], uT[:, (8 if n < 3 else 4) + c, P * (n % 3):P * (n % 3) + w], ident)
                ins.then_inc(tok_t, 1)
            pe.wait_ge(glu_ready, NCC)
            for c in range(NCC):
                ins = pe.transpose(bank[0:ST, 6, P * c:P * c + P], cbuf[:, c, SEQ:SEQ + ST], ident)
            ins.then_inc(gl_t, 1)
            pe.wait_ge(gs_copy, 1)
            for c in range(NCC):
                ins = pe.transpose(bank[0:NS, 7, P * c:P * c + P], gsam[:, c, :], ident)
            ins.then_inc(gl_t, 1)

            def prompt_qk(h):
                r = slice(64 * (h % 2), 64 * (h % 2) + 64)
                if h >= 2:
                    pe.wait_ge(ps_ready, h - 1)
                q, k = uT[r, h // 2, :], uT[r, 4 + h // 2, :]
                pe.matmul(bank[:, h % 2, 0:P], q[:, 0:P], k[:, 0:P], start=True, stop=True)
                pe.matmul(bank[:, h % 2, P:3 * P], q[:, P:2 * P], k[:, 0:2 * P], start=True, stop=True).then_inc(ps_mm, 1)

            def prompt_turn(h):
                pe.wait_ge(pp_ready, h + 1)
                if h >= 2:
                    pe.wait_ge(pp_out, h - 1)
                for n in range(3):
                    ins = pe.transpose(bank[:, 2 + h % 2, P * n:P * n + P], ps_[:, h % 3, P * n:P * n + P], ident)
                ins.then_inc(pp_t, 1)

            def prompt_pv(h):
                pe.wait_ge(pp_out, h + 1)
                if h >= 4:
                    pe.wait_ge(pv_out, h // 2 - 1)
                r = slice(64 * (h % 2), 64 * (h % 2) + 64)
                b = 4 + h // 2 % 2
                v = [vtok[:, n, HD * h:HD * h + HD] for n in range(2)]
                p_ = ppT[:, h % 2, :]
                pe.matmul(bank[r, b, 0:P], v[0], p_[:, 0:P], start=True, stop=True)
                pe.matmul(bank[r, b, P:2 * P], v[0], p_[:, P:2 * P], start=True, stop=False)
                pe.matmul(bank[r, b, P:2 * P], v[1], p_[:, 2 * P:3 * P], start=False, stop=True).then_inc(pv_mm, 1)

            pe.wait_ge(tok_out, 6)
            pe.wait_ge(st_in, 2)
            prompt_qk(0)
            prompt_qk(1)
            for h in range(NH):
                if h + 2 < NH:
                    prompt_qk(h + 2)
                prompt_turn(h)
                if h:
                    prompt_pv(h - 1)
            prompt_pv(NH - 1)

            def scores(j, k, hf, first):
                g, b2 = k // 2, k // 4
                pe.wait_ge(kt_lo, 16 * j + 2 * k + hf + 1)
                if hf == 0 and k % 4 == 0:
                    pe.wait_ge(q_lo, 2 * j + b2 + 1)
                if hf == 0 and k % 2 == 0 and not (first and g < 2):
                    pe.wait_ge(s_evac, 4 * j + g - 1)
                for h in range(4 * hf, 4 * hf + 4):
                    for x, (q, kk) in enumerate(((qbh, kh), (qbh, kl), (qbl, kh))):
                        ins = pe.matmul(bank[:, 4 + g % 2, BLK * (k % 2):BLK * (k % 2) + BLK], q[:, P * h:P * h + P],
                                        kk[:, k % 2, h // 2, BLK * (h % 2):BLK * (h % 2) + BLK],
                                        start=(h == 0 and x == 0), stop=(h == NH - 1 and x == 2))
                if hf:
                    ins.then_inc(k_used, 1)

            def own_scores(b2):
                for h in range(NH):
                    for x, (q, kk) in enumerate(((qbh, koh), (qbh, kol), (qbl, koh))):
                        ins = pe.matmul(bank[:, 6, NS * b2:NS * b2 + NS], q[:, P * h:P * h + P], kk[:, h, :],
                                        start=(h == 0 and x == 0), stop=(h == NH - 1 and x == 2))
                ins.then_inc(own_ready, 1)

            def page_view(k, pp, h):
                at = 1024 * pp + P * h
                return raw[:, k % RING, at:at + P]

            def raw_wait(k, kv4, turns):
                pe.wait_ge(raw_in[k % RING], raw_count_kv(RING * (kv4 + k // RING)) + turns)

            def pair_keys(j, kv4, turns, first=False):
                for k in range(8):
                    raw_wait(k, kv4, turns)
                    for hf in range(2):
                        if not (first and k == 0):
                            pe.wait_ge(kt_lo, 16 * j + 2 * k + hf - 1)
                        for h in range(4 * hf, 4 * hf + 4):
                            for pp in range(2):
                                at = BLK * (h % 2) + P * pp
                                ins = pe.transpose(bank[:, h // 2, at:at + P], page_view(k, pp, h), ident)
                        ins.then_inc(kt_ready, 1)
                        if k:
                            scores(j, k - 1, hf, first)
                        if k == 4 and hf:
                            own_scores(0)
                scores(j, 7, 0, first)
                scores(j, 7, 1, first)
                own_scores(1)

            def parities(ready, count, matrix, at, src, n, done):
                pe.wait_ge(ready, count)
                pe.matmul(bank[:, 6, at:at + n], con[:, matrix:matrix + P], src, start=True, stop=True).then_inc(done, 1)

            def gate_sum(j):
                parities(gsum_ready, j + 1, C_SUM, 256, gsum[:, :, :].rearrange("p b n -> p (b n)"), 16, gate_mm)

            def max_swap(j):
                parities(nmax_ready, j + 1, C_SWAP, 288, nmax[:, :], 2, swap_mm)

            def prob_sum(j):
                parities(ex_ready, j + 1, C_SUM, 320, rt[:, :], 2, rsum_mm)

            def pair_probs(j):
                pe.wait_ge(p_ready, j + 1)
                for r in range(4):
                    if r >= 2:
                        pe.wait_ge(pt_evac, 5 * j + r - 1)
                    for x in range(4):
                        n = 4 * (r % 2) + x
                        ins = pe.transpose(bank[:, 4 + r % 2, P * x:P * x + P], s[:, r // 2, P * n:P * n + P], ident)
                    ins.then_inc(pt_ready, 1)
                for b2 in range(2):
                    ins = pe.transpose(bank[0:NS, 6, P * b2:P * b2 + P], s[:, b2, PAST // 2:], ident)
                ins.then_inc(pt_ready, 1)

            def pair_values(j, kv4, turns, between=None):
                pe.wait_ge(pt_evac, 5 * j + 5)
                for k in range(8):
                    c, b2 = k % 4, k // 4
                    raw_wait(k, kv4, turns)
                    for pp in range(2):
                        n = NBLK * b2 + 2 * c + pp
                        for hf in range(2):
                            at = 1024 * pp + 512 * hf
                            ins = pe.matmul(bank[:, 2 * b2 + hf, :], pT[:, P * n:P * n + P], raw[:, k % RING, at:at + 512],
                                            start=(c == 0 and pp == 0), stop=False)
                    ins.then_inc(v_used, 1)
                    if between is not None and k in between:
                        between[k]()
                    if c == 3:
                        for hf in range(2):
                            ins = pe.matmul(bank[:, 2 * b2 + hf, :].rearrange("p (h r d) -> p h r d", h=4, r=2)[:, :, 0, :],
                                            po[:, P * b2:P * b2 + P], vsam[:, 256 * hf:256 * hf + 256].rearrange("k (h d) -> k h d", h=4),
                                            start=False, stop=True)
                        ins.then_inc(acc_ready, 1)

            def attn_turn(j, first=False):
                if not first:
                    pe.wait_ge(av_evac, j)
                for b2 in range(2):
                    pe.wait_ge(arow_ready, 2 * j + b2 + 1)
                    for e in range(2):
                        cols = con[:, C_SUM:C_SUM + NS].rearrange("p (m e t) -> p m e t", m=NHP, e=2)[:, :, e, :]
                        at = 32 * b2
                        ins = pe.matmul(bank[64 * e:64 * e + 64, 7, at:at + 32], arow[:, b2, :], cols, start=True, stop=True)
                ins.then_inc(at_mm, 1)

            pe.wait_ge(ko_lo, 1)
            pe.wait_ge(gl_out, 2)
            pe.wait_ge(pv_out, 4)
            pair_keys(0, 0, 0, first=True)
            gate_sum(0)
            max_swap(0)
            prob_sum(0)
            pair_probs(0)

            def next_pair(j, kv4, turns, first=False):
                pe.wait_ge(pt_evac, 5 * j)
                pair_keys(j, kv4, turns)
                pair_values(j - 1, kv4 + 2, turns, {0: lambda: gate_sum(j), 2: lambda: max_swap(j), 5: lambda: prob_sum(j)})
                pair_probs(j)
                attn_turn(j - 1, first)

            next_pair(1, 2, 0, first=True)
            with pe.Fori(2, 4) as j:
                next_pair(j, 6, 64 * 4 * (j - 2))

            pe.wait_ge(pt_evac, 20)
            pe.wait_ge(conv_ready, NCC)
            pe.wait_ge(av_evac, 3)
            for c in range(NCC):
                pe.matmul(bank[:, 4 + c, 0:T], gnones, yT[:, NCC + c, :], start=True, stop=True).then_inc(gm_mm, 1)

            def group_variances():
                for c in range(NCC):
                    pe.wait_ge(gq_ready, c + 1)
                    pe.matmul(bank[:, 4 + c, 0:T], gnones, tmp[:, c, :], start=True, stop=True).then_inc(gv_mm, 1)

            pair_values(3, 14, 0, {RING - 1: group_variances})
            attn_turn(3)

            for u in range(WOUT[2]):
                pe.wait_ge(w_lo, WOUT[0] + u + 1)
                for cc in range(2):
                    if u >= 2:
                        pe.wait_ge(y_ready, 8 + 2 * (u - 2) + cc + 1)
                    ready = (lambda n: pe.wait_ge(ml_ready, 16 + n + 1)) if u == 0 and cc == 0 else None
                    ins = product(4 + 2 * (u % 2) + cc, slot_w(WOUT, u), cc, m_parts(MIX_ORDER), ready=ready)
                    ins.then_inc(n_ready if cc == 0 else w_used, 1)
            norm(1)
            up(1, UP2, 24)
            down(1, DN2, 16)
            norm(2)
            for n in range(6):
                tt, half = n // 2, n % 2
                w = P if tt < 2 else NS
                pe.wait_ge(x_ready, 16 + 4 * half + 4)
                for c in range(4):
                    ins = pe.transpose(bank[0:w, 2 + n, P * c:P * c + P], xT[:, 4 * half + c, P * tt:P * tt + w], ident)
                ins.then_inc(out_t, 1)


_INS = ["x_prompt", "x_sample", "cache_k", "cache_v", "state_conv", "page_table", "c_prompt", "c_sample", "w_ada", "b_ada",
        "ffn1_wg", "ffn1_wu", "ffn1_wd", "w_in", "w_dw", "b_dw", "gn_g", "gn_b", "beta_attn", "beta_conv", "w_out",
        "ffn2_wg", "ffn2_wu", "ffn2_wd", "ln_g", "ln_b"]
_OUTS = [("y_prompt", (1, SEQ, D)), ("y_sample", (DB, DT, D)), ("k_prompt_new", (1, 1, SEQ // PAGE, NH, PAGE, HD)),
         ("v_prompt_new", (1, 1, SEQ // PAGE, NH, PAGE, HD)), ("conv_prompt_new", (1, 1, ST, CC)),
         ("k_sample_new", (1, DB, NH, DT, HD)), ("v_sample_new", (1, DB, NH, DT, HD)), ("conv_sample_new", (1, DB, ST, CC))]


def kernel(**inputs):
    import concourse.bacc as bacc
    from concourse.bass_utils import run_bass_kernel_spmd

    nc = bacc.Bacc("TRN2", target_bir_lowering=False, num_devices=1)
    arrays, ins, outs = {}, {}, {}
    for name in _INS + ["consts"]:
        a = constants() if name == "consts" else np.ascontiguousarray(inputs[name])
        arrays[f"in_{name}"] = a
        ins[name] = nc.dram_tensor(f"in_{name}", a.shape, mybir.dt.from_np(a.dtype), kind="ExternalInput").ap()
    for name, shape in _OUTS:
        outs[name] = nc.dram_tensor(f"out_{name}", shape, F32, kind="ExternalOutput").ap()
    build(nc, ins, outs)
    r = run_bass_kernel_spmd(nc, [arrays], core_ids=[0])
    return tuple(r.results[0][f"out_{name}"] for name, _ in _OUTS)
```

```python
from contextlib import ExitStack

import numpy as np

import concourse.bass as bass
from concourse import mybir

F32 = mybir.dt.float32
F32R = mybir.dt.float32r
I32 = mybir.dt.int32
U32 = mybir.dt.uint32
ALU = mybir.AluOpType
ACT = mybir.ActivationFunctionType
AX = mybir.AxisListType.X

P = 128
D = 1024
NCH = D // P
SEQ = 256
DB, DT = 8, 8
NS = DB * DT
T = SEQ + NS
NH, HD = 8, 64
AW = NH * HD
NHP = AW // P
CC = 512
NCC = CC // P
TAPS = 31
ST = TAPS - 1
PAST, PAGE, BLK = 2048, 128, 256
NPG = PAST // PAGE
NBLK = PAST // BLK
NPOOL = 160
FF = 2816
NF = FF // P
ALPHA = 2.0 ** 0.25
EPS = 1e-5
NEG = -1e30
UC = 256
RING = 4
UMAX = NCH * UC
CB = ST + SEQ + DB * (ST + DT)
SB = ST + DT
QPITCH = P + DT
QB = 64 + P + DT + NHP * 2 * QPITCH

C_ID, C_LN, C_GN, C_REL, C_SEL = 0, P, 2 * P, 3 * P, 6 * P
C_POS = C_SEL + 16
C_OWN = C_POS + P
C_IOTA = C_OWN + 120
C_RC = C_IOTA + 8
C_M = C_RC + 8
C_EPS = C_M + 1
C_SUM = C_EPS + 1
C_SWAP = C_SUM + P
C_HEAD = C_SWAP + P
C_N = C_HEAD + 4


def constants():
    c = np.zeros((P, C_N), np.float32)
    p = np.arange(P)
    c[:, C_ID:C_ID + P] = np.eye(P)
    c[:, C_LN:C_LN + P] = 1.0 / D
    c[:, C_GN:C_GN + P] = (p[:, None] // 64 == p[None, :] // 64) / 64.0
    for at, q0, keys in ((0, 0, P), (P, P, 2 * P)):
        rel = np.arange(keys)[None, :] - (q0 + p[:, None])
        c[:, C_REL + at:C_REL + at + keys] = np.where(rel <= 0, rel, -3e34)
    for r in range(18):
        c[r, C_SEL + r % 9] = 1.0
    c[:, C_POS:C_POS + P] = (p // 64 * P + 2 * (p % 64))[None, :]
    r, h, t = p // 64, p % 64 // 8, p % 8
    m = 2.0 ** (-(h + 1.0))
    key = np.arange(120) - 56
    ok = (key[None, :] >= 0) & (key[None, :] <= t[:, None]) & (r[:, None] == 0)
    c[:, C_OWN:C_OWN + 120] = np.where(ok, m[:, None] * (key[None, :] - t[:, None]), NEG)
    c[:, C_IOTA:C_IOTA + 8] = np.arange(8)[None, :]
    c[:, C_RC:C_RC + 8] = m[:, None] * (BLK * np.arange(8)[None, :] - PAST + (r - t)[:, None])
    c[:, C_M] = m
    c[:, C_EPS] = EPS
    c[:, C_SUM:C_SUM + P] = p[:, None] % 64 == p[None, :] % 64
    c[:, C_SWAP:C_SWAP + P] = (p[:, None] + 64) % P == p[None, :]
    c[:, C_HEAD:C_HEAD + 4] = h[:, None] % 4 == np.arange(4)[None, :]
    return c


ADA, UP1, DN1, WIN, WOUT, UP2, DN2 = (0, 0, 10), (10, 10, 44), (54, 54, 16), (70, 70, 10), (80, 144, 4), (84, 148, 22), (106, 170, 12)
KV0, KVN = 80, 64
ADAN = 9 * D // UC
ADA_DN = ADAN - 4
DN_CHUNKS = (8, 8, 6)


def down_unit(phase, n):
    return (n // 4, n % 4 - 1) if phase[0] == DN1[0] else (n // 3, n % 3)


def down_size(phase, n):
    return (DN_CHUNKS + (NCH,))[down_unit(phase, n)[1]] * UC
WIN_ORDER = [8, 9, 6, 7, 2, 3, 4, 5, 0, 1]
MIX_ORDER = [4, 5, 6, 7, 0, 1, 2, 3]


def raw_count(turn):
    before = KV0 // RING
    return 16 * (turn + 1) if turn < before else 16 * (turn + 1 - KVN // RING) + 64 * (KVN // RING)


def raw_count_w(phase, u, turns=0):
    return raw_count((phase[1] + u) // RING) + 16 * turns


def raw_count_kv(kvi, turns=0):
    return 16 * (KV0 // RING) + 64 * (kvi // RING + 1) + 64 * turns


def slots(phase):
    return 3 if phase[0] <= WOUT[0] else 2


def slot_w(phase, u):
    return (phase[0] + u) % slots(phase)


def build(nc, i, o):
    es = ExitStack()
    with es:
        def sb(name, shape, dt=F32, stack=es):
            return stack.enter_context(nc.sbuf_tensor(name, shape, dt))

        def sem(name):
            return es.enter_context(nc.semaphore(name))

        bank = es.enter_context(nc.psum_tensor("bank", [P, 8, 512], F32))
        con = sb("con", [P, C_N])
        xT = sb("xT", [P, NCH, T])
        yT = sb("yT", [P, NCH, T])
        mh = sb("mh", [P, NCH, T], F32R)
        ml = sb("ml", [P, NCH, T], F32R)
        adaT = sb("adaT", [P, 72, 9])
        raw = sb("raw", [P, RING, UMAX])
        whi = sb("whi", [P, 3, UMAX], F32R)
        wlo = sb("wlo", [P, 3, UMAX], F32R)
        par1 = sb("par1", [P, 120])
        par2 = sb("par2", [P, 20])
        dwT = sb("dwT", [P, TAPS * NCC])
        fold_g = sb("fold_g", [P, 2, NCH, 9])
        fold_b = sb("fold_b", [P, 2, NCH, 9])
        cT = sb("cT", [P, 72])
        chl = sb("chl", [P, NCH, 18], F32R)
        pages = sb("pages", [1, DB * NPG], I32)
        tmp = sb("tmp", [P, 4, T])
        rows = sb("rows", [18, 2, UC])

        with ExitStack() as scope:
            hh = sb("hh", [P, NF, T], F32R, scope)
            hl = sb("hl", [P, NF, T], F32R, scope)
        with ExitStack() as scope:
            xrow = sb("xrow", [P, 3, D], F32, scope)
            prow = sb("prow", [P, 4, P], F32, scope)
        with ExitStack() as scope:
            yrow = sb("yrow", [P, 3, D], F32, scope)
        with ExitStack() as scope:
            uT = sb("uT", [P, 12, T], F32, scope)
            cbuf = sb("cbuf", [P, NCC, CB], F32, scope)
            s = sb("s", [P, 2, PAST // 2 + NS], F32, scope)
            pT = sb("pT", [P, 2 * NBLK * P], F32, scope)
            po = sb("po", [NS, 2 * P], F32, scope)
            qbh = sb("qbh", [P, QB], F32R, scope)
            qbl = sb("qbl", [P, QB], F32R, scope)
            koh = sb("koh", [P, NH, NS], F32R, scope)
            kol = sb("kol", [P, NH, NS], F32R, scope)
            vtok = sb("vtok", [P, 2, AW], F32, scope)
            vsam = sb("vsam", [NS, AW], F32, scope)
            gsum = sb("gsum", [P, 2, 8], F32, scope)
            gate = sb("gate", [P, 2, 8], F32, scope)
            gmax = sb("gmax", [P, 2, 8], F32, scope)
            gidx = sb("gidx", [P, 2, 8], U32, scope)
            gidf = sb("gidf", [P, 2, 8], F32, scope)
            hit = sb("hit", [P, 2, 8, 3], F32, scope)
            ebase = sb("ebase", [P, 2, 8], F32, scope)
            bmax = sb("bmax", [P, 2, 9], F32, scope)
            nmax = sb("nmax", [P, 2], F32, scope)
            ebias = sb("ebias", [P, 2], F32, scope)
            rt = sb("rt", [P, 2], F32, scope)
            ri = sb("ri", [P, 2], F32, scope)
            ps_ = sb("ps_", [P, 3, 3 * P], F32, scope)
            pm = sb("pm", [P, 3, 2], F32, scope)
            pz = sb("pz", [P, 3, 2], F32, scope)
            pr = sb("pr", [P, 3, 2], F32, scope)
        khn, kln, qh, ql = (t_[:, n, 0:NHP * NS].rearrange("p (m t) -> p m t", m=NHP)
                            for t_, n in ((mh, 0), (ml, 0), (mh, 1), (ml, 1)))
        sflat = s[:, :, :].rearrange("p b c -> p (b c)")
        strow = pT[0:4 * ST, 0:2 * CC].rearrange("p (g c) -> p g c", g=2)
        ksam = sflat[0:NS, 768:768 + AW]
        cout = sflat[0:ST, 1280:1280 + CC]
        ppT = pT[:, 0:768].rearrange("p (a c) -> p a c", a=2)
        ktok = pT[:, 1024:2048].rearrange("p (g c) -> p g c", g=2)
        csam = tmp[:, :, :].rearrange("p a t -> p (a t)")[0:NS, 2 * T:2 * T + CC]
        tmp2 = tmp[:, 2:4, :].rearrange("p a t -> p (a t)")
        ahead = tmp2[:, 0:8 * HD].rearrange("p (b h d) -> p b h d", b=2, h=4)
        arow = tmp2[:, 8 * HD:10 * HD].rearrange("p (b d) -> p b d", b=2)

        def squares(q):
            return tmp[:, 2 * q:2 * q + 2, :] if q < 2 else uT[:, 4 + 2 * q:6 + 2 * q, :]

        gsam = yT[:, 0, 0:NCC * NS].rearrange("p (c k) -> p c k", c=NCC)
        kh = whi[:, 0:2, :].rearrange("p s (m c) -> p s m c", m=NHP)
        kl = wlo[:, 0:2, :].rearrange("p s (m c) -> p s m c", m=NHP)

        ident = con[:, C_ID:C_ID + P]
        lnones = con[:, C_LN:C_LN + P]
        gnones = con[:, C_GN:C_GN + P]

        ld_c, c_t, ld_ident = sem("ld_c"), sem("c_t"), sem("ld_ident")
        ld_con, ld_par, ld_x, ld_pages, ld_state = sem("ld_con"), sem("ld_par"), sem("ld_x"), sem("ld_pages"), sem("ld_state")
        raw_in = [sem(f"raw_in{k}") for k in range(RING)]
        w_hi, w_lo, w_used = sem("w_hi"), sem("w_lo"), sem("w_used")
        par_t, x_t, c_silu, c_hi, c_lo, par_ready, x_in = (sem(n) for n in ("par_t", "x_t", "c_silu", "c_hi", "c_lo", "par_ready", "x_in"))
        ada_row, ada_t, ada_out = (sem(n) for n in ("ada_row", "ada_t", "ada_out"))
        m_ready, mh_ready, ml_ready, ax_ready, y_ready = (sem(n) for n in ("m_ready", "mh_ready", "ml_ready", "ax_ready", "y_ready"))
        mean_ready, yc_ready, sq_ready, sqsum_ready, var_ready, std_ready, xn_ready, x_ready = (
            sem(n) for n in ("mean_ready", "yc_ready", "sq_ready", "sqsum_ready", "var_ready", "std_ready", "xn_ready", "x_ready"))
        g_ready = [sem("g_ready1"), sem("g_ready2")]
        silu_ready = [sem("silu_ready1"), sem("silu_ready2")]
        u_ready = [sem("u_ready1"), sem("u_ready2")]
        h_ready = [sem("h_ready1"), sem("h_ready2")]
        hh_ready = [sem("hh_ready1"), sem("hh_ready2")]
        hl_ready = [sem("hl_ready1"), sem("hl_ready2")]
        n_ready = sem("n_ready")
        dve_step, act_step, pool_step = sem("dve_step"), sem("act_step"), sem("pool_step")
        win_mm, sig_ready, glu_ready, u_out = (sem(n) for n in ("win_mm", "sig_ready", "glu_ready", "u_out"))
        tok_t, tok_out, st_t, st_in, gl_t, gl_out = (sem(n) for n in ("tok_t", "tok_out", "st_t", "st_in", "gl_t", "gl_out"))
        pad_ready, conv_ready = sem("pad_ready"), sem("conv_ready")
        ps_mm, ps_ready, pmax_ready, pexp, pp_ready, pp_t, pp_out, pv_mm, pv_out = (
            sem(n) for n in ("ps_mm", "ps_ready", "pmax_ready", "pexp", "pp_ready", "pp_t", "pp_out", "pv_mm", "pv_out"))
        ko_hi, ko_lo, q_zero, q_hi, q_lo = (
            sem(n) for n in ("ko_hi", "ko_lo", "q_zero", "q_hi", "q_lo"))
        qs_hi, qs_lo, gs_copy, gsum_ready, gate_mm, nmax_ready, swap_mm, rsum_mm = (
            sem(n) for n in ("qs_hi", "qs_lo", "gs_copy", "gsum_ready", "gate_mm", "nmax_ready", "swap_mm", "rsum_mm"))
        kt_ready, kt_hi, kt_lo, k_used, s_evac, own_ready, eb_ready, ex_ready, p_ready, pt_ready, pt_evac, v_used, av_evac = (
            sem(n) for n in ("kt_ready", "kt_hi", "kt_lo", "k_used", "s_evac", "own_ready", "eb_ready", "ex_ready", "p_ready",
                             "pt_ready", "pt_evac", "v_used", "av_evac"))
        acc_ready, arow_ready, at_mm = sem("acc_ready"), sem("arow_ready"), sem("at_mm")
        gm_mm, gc_ready, gq_ready, gv_mm, gs_ready, gx_ready, gy_ready = (
            sem(n) for n in ("gm_mm", "gc_ready", "gq_ready", "gv_mm", "gs_ready", "gx_ready", "gy_ready"))
        ysum_step = sem("ysum_step")
        fold_step, fold_ready = sem("fold_step"), sem("fold_ready")
        out_t, out_row, stored = sem("out_t"), sem("out_row"), sem("stored")
        stored_early = sem("stored_early")
        N_EARLY = 1 + 3 * DB + 4
        X_AT = 4
        MOD_AT = 8

        def mod_chunks(u):
            return range(NCH) if u == MOD_AT else ()

        block = es.enter_context(nc.Block())

        def up_pairs(eng, ffn, body):
            body(0, 0)
            if ffn == 0:
                with eng.Fori(0, 3) as g:
                    for n in range(3):
                        body(1 + 3 * g + n, 1 + n)
            else:
                with eng.Fori(0, 4) as g:
                    body(1 + 2 * g, 1)
                    body(2 + 2 * g, 2)
                body(9, 9)
            body(10, 10)

        def stride(ffn):
            return 4 if ffn == 0 else 2

        def load_pages(eng, cache, seq, c, k, which, wait):
            engine = mybir.EngineType.SP if eng is nc.sync else mybir.EngineType.Activation
            page = [nc.values_load(pages[0:1, bass.ds(NPG * seq + 4 * c + x, 1)], engines=[engine], min_val=0, max_val=NPOOL - 1,
                                   skip_runtime_bounds_check_because="a page table holds indices into the pool, as the reference reads it")
                    for x in which]
            if wait is not None:
                eng.wait_ge(*wait)
            for x, at in zip(which, page):
                eng.dma_start(raw[64 * (x % 2):64 * (x % 2) + 64, k % RING, 1024 * (x // 2):1024 * (x // 2) + 1024]
                              .rearrange("p (h f) -> p h f", h=NH),
                              i["cache_" + cache][0][bass.ds(at, 1)].rearrange("a h (p r) d -> p (a h) (r d)", r=2)).then_inc(raw_in[k % RING], 16)

        @block.sync
        def _(sp):
            sp.dma_start(con[:, 0:P], i["consts"][:, 0:P]).then_inc(ld_ident, 16)
            def slot_of(phase, u):
                return (phase[1] + u) % RING

            def load(phase, u, src, size, wait, turns=0):
                if wait is not None:
                    sp.wait_ge(*wait)
                k = slot_of(phase, u)
                sp.dma_start(raw[:, k, 0:size].rearrange("p (k c) -> p k c", c=UC), src).then_inc(raw_in[k], 16)

            def w_free(phase, u):
                return (w_lo, phase[0] + u - RING + 1)

            def cols(w, c):
                return w[0].rearrange("(k p) c -> p k c", p=P)[:, :, c]

            def load_ada(phase, u, n, wait):
                load(phase, u, cols(i["w_ada"], bass.ds(UC * n, UC)), NCH * UC, wait)

            for u in range(4):
                load_ada(ADA, u, u, None)
                if u == 0:
                    sp.dma_start(con[:, P:C_N], i["consts"][:, P:C_N]).then_inc(ld_con, 16)
            sp.dma_start(xrow[:, 0:2, :], i["x_prompt"][0].rearrange("(t p) f -> p t f", p=P)).then_inc(ld_x, 16)
            sp.dma_start(xrow[0:NS, 2, :], i["x_sample"].rearrange("b t f -> (b t) f")).then_inc(ld_x, 16)
            for u in range(4, ADA[2]):
                load_ada(ADA, u, u, w_free(ADA, u))
            sp.dma_start(pages[:, :], i["page_table"].rearrange("b n -> (b n)").unsqueeze(0)).then_inc(ld_pages, 16)
            sp.dma_start(o["conv_sample_new"][0, :, 0:ST - DT, :], i["state_conv"][0, :, DT:ST, :]).then_inc(stored, 16)

            def load_up(phase, ffn):
                n = stride(ffn)

                def body(pair, pair_):
                    for x, w in enumerate((i[f"ffn{ffn + 1}_wg"], i[f"ffn{ffn + 1}_wu"])):
                        load(phase, n * pair_ + n // 2 * x, cols(w, bass.ds(UC * pair, UC)), NCH * UC, w_free(phase, n * pair + n // 2 * x))
                        if ffn == 0:
                            load_ada(phase, n * pair_ + 2 * x + 1, ADA[2] + 2 * pair + x, w_free(phase, n * pair + 2 * x + 1))
                up_pairs(sp, ffn, body)

            def load_down(phase, ffn):
                w = i[f"ffn{ffn + 1}_wd"][0].rearrange("(k p) c -> p k c", p=P)
                for u in range(phase[2]):
                    nb, third = down_unit(phase, u)
                    n = DN_CHUNKS[third]
                    if third < 0:
                        load_ada(phase, u, ADA_DN + nb, w_free(phase, u))
                    else:
                        load(phase, u, w[:, 8 * third:8 * third + n, UC * nb:UC * nb + UC], n * UC, w_free(phase, u))

            load_up(UP1, 0)
            load_down(DN1, 0)
            for u, b in enumerate(WIN_ORDER):
                load(WIN, u, cols(i["w_in"], slice(UC * b, UC * b + UC)), NCH * UC, w_free(WIN, u))
            sp.wait_ge(w_used, DN1[0] + DN1[2])
            for g in range(2):
                sp.dma_start(strow[:, g, :], i["state_conv"][0, 4 * g:4 * g + 4].rearrange("b k c -> (b k) c")).then_inc(ld_state, 16)
            sp.wait_ge(ld_pages, 16)

            def store_rows():
                sp.wait_ge(tok_out, 6)
                sp.wait_ge(gl_out, 2)
                for t_, name in ((vtok, "v_prompt_new"), (ktok, "k_prompt_new")):
                    for pg in range(2):
                        sp.dma_start(o[name][0, 0, pg].rearrange("h p d -> p h d"), t_[:, pg, :].rearrange("p (h d) -> p h d", h=NH)).then_inc(stored_early, 16)
                for b in range(DB):
                    r = slice(DT * b, DT * b + DT)
                    sp.dma_start(o["v_sample_new"][0, b].rearrange("h t d -> t h d"), vsam[r, :].rearrange("t (h d) -> t h d", h=NH)).then_inc(stored_early, 16)
                    sp.dma_start(o["k_sample_new"][0, b].rearrange("h t d -> t h d"), ksam[r, :].rearrange("t (h d) -> t h d", h=NH)).then_inc(stored_early, 16)
                    sp.dma_start(o["conv_sample_new"][0, b, ST - DT:ST, :], csam[r, :]).then_inc(stored_early, 16)
                sp.dma_start(o["conv_prompt_new"][0, 0], cout).then_inc(stored_early, 16)

            for k in range(8):
                load_pages(sp, "k", k // 4, k % 4, k, range(4) if k < RING else (0, 1),
                           (w_lo, WIN[0] + WIN[2] - RING + k + 1) if k < RING else (kt_ready, 2 * (k - RING) + 2))
                if k == RING - 1:
                    store_rows()

            def sp_pages(cache, seq, c, k, wait):
                load_pages(sp, cache, seq, c, k, (0, 1), wait)

            def kv_round(j, j_is_1):
                for k in range(8):
                    if k >= RING:
                        wait = (kt_ready, 16 * j + 2 * (k - RING) + 2)
                    elif j_is_1:
                        wait = (kt_ready, 2 * (k + RING) + 2)
                    else:
                        wait = (v_used, 8 * (j - 2) + k + RING + 1)
                    sp_pages("k", 2 * j + k // 4, k % 4, k, wait)
                for k in range(8):
                    wait = (kt_ready, 16 * j + 2 * (k + RING) + 2) if k < RING else (v_used, 8 * (j - 1) + k - RING + 1)
                    sp_pages("v", 2 * (j - 1) + k // 4, k % 4, k, wait)

            kv_round(1, True)
            with sp.Fori(2, 4) as j:
                kv_round(j, False)
            for k in range(8):
                sp_pages("v", 6 + k // 4, k % 4, k, (v_used, 8 * 2 + k + RING + 1) if k < RING else (v_used, 24 + k - RING + 1))
            for u in range(WOUT[2]):
                load(WOUT, u, cols(i["w_out"], slice(UC * u, UC * u + UC)), NCH * UC, (v_used, 24 + RING + u + 1))
            load_up(UP2, 1)
            load_down(DN2, 1)
            for n in range(6):
                half, tt = n // 3, n % 3
                w = P if tt < 2 else NS
                c = slice(512 * half, 512 * half + 512)
                sp.wait_ge(out_row, n + 1)
                dst = o["y_prompt"][0, P * tt:P * tt + P, c] if tt < 2 else o["y_sample"].rearrange("b t f -> (b t) f")[:, c]
                sp.dma_start(dst, yrow[0:w, tt, c]).then_inc(stored, 16)
            sp.wait_ge(stored, 16 * (1 + 6))
            sp.wait_ge(stored_early, 16 * N_EARLY)

        @block.gpsimd
        def _(pool):
            def y_sums(n):
                for q in range(1, NCH - 1):
                    pool.wait_ge(y_ready, 8 * n + q + 1)
                    if q > 1:
                        pool.wait_ge(ysum_step, 6 * n + q - 1)
                    pool.tensor_tensor(tmp[:, 3, :], yT[:, 0, :] if q == 1 else tmp[:, 3, :], yT[:, q, :], ALU.add).then_inc(ysum_step, 1)

            def scale_x(n):
                pool.wait_ge(*((m_ready, 8) if n == 0 else (x_ready, 8 * n)))
                pool.tensor_scalar(xT[:, :, :], xT[:, :, :], ALPHA, None, ALU.mult).then_inc(ax_ready, 1)

            pool.dma_start(prow[0:72, 0, :], i["b_ada"].rearrange("o (r f) -> (o r) f", f=P)).then_inc(ld_par, 16)
            pool.dma_start(prow[72:96, 0, :], i["ln_g"].rearrange("o j (r f) -> (o j r) f", f=P)).then_inc(ld_par, 16)
            pool.dma_start(prow[96:120, 0, :], i["ln_b"].rearrange("o j (r f) -> (o j r) f", f=P)).then_inc(ld_par, 16)
            for n, name in enumerate(("b_dw", "gn_g", "gn_b", "beta_attn", "beta_conv")):
                pool.dma_start(prow[4 * n:4 * n + 4, 1, :], i[name].rearrange("o (r f) -> (o r) f", f=P)).then_inc(ld_par, 16)
            pool.dma_start(prow[0:TAPS * NCC, 2, :], i["w_dw"].rearrange("o k (r f) -> (o k r) f", f=P)).then_inc(ld_par, 16)
            scale_x(0)
            pool.wait_ge(ada_out, ADA_DN)
            sc = adaT[:, :, :].rearrange("p (s k n) r -> p s k n r", s=3, k=3)[:, 1:3, 1]
            sh = adaT[:, :, :].rearrange("p (s k n) r -> p s k n r", s=3, k=3)[:, 1:3, 0]
            for n in range(2):
                pool.tensor_tensor(fold_g[:, n], sc[:, n], par1[:, 72 + 8 * n:80 + 8 * n].unsqueeze(2).to_broadcast([P, 8, 9]), ALU.mult)
                ins = pool.tensor_tensor(fold_b[:, n], sc[:, n], par1[:, 96 + 8 * n:104 + 8 * n].unsqueeze(2).to_broadcast([P, 8, 9]), ALU.mult)
            ins.then_inc(fold_step, 1)
            pool.wait_ge(fold_step, 1)
            for n in range(2):
                ins = pool.tensor_tensor(fold_b[:, n], fold_b[:, n], sh[:, n], ALU.add)
            ins.then_inc(fold_ready, 1)
            y_sums(0)
            pool.wait_ge(w_used, DN1[0] + DN1[2])
            pool.memset(cbuf[:, :, 0:ST], 0.0).then_inc(pad_ready, 1)
            pool.memset(qbh[:, :].bitcast(F32), 0.0).then_inc(q_zero, 1)
            pool.memset(qbl[:, :].bitcast(F32), 0.0).then_inc(q_zero, 1)
            pool.memset(koh[:, :, :].bitcast(F32), 0.0).then_inc(q_zero, 1)
            pool.memset(kol[:, :, :].bitcast(F32), 0.0).then_inc(q_zero, 1)
            scale_x(1)
            pool.wait_ge(glu_ready, NCC)
            pool.wait_ge(st_in, 2)
            pool.wait_ge(pad_ready, 1)
            steps = 0
            for c in range(NCC):
                acc = yT[:, NCC + c, :]
                sam = cbuf[:, c, ST + SEQ:CB].rearrange("p (b k) -> p b k", b=DB)
                for k in range(TAPS):
                    w = dwT[:, NCC * k + c:NCC * k + c + 1]
                    to = acc if k == 0 else tmp[:, k % 2, :]
                    more = (par2[:, c:c + 1], ALU.mult, ALU.add) if k == 0 else (None, ALU.mult)
                    pool.tensor_scalar(to[:, 0:SEQ], cbuf[:, c, k:k + SEQ], w, *more)
                    pool.tensor_scalar(to[:, SEQ:T].rearrange("p (b t) -> p b t", b=DB), sam[:, :, k:k + DT], w, *more).then_inc(pool_step, 1)
                    steps += 1
                    if k:
                        pool.wait_ge(pool_step, steps)
                        last = k == TAPS - 1
                        pool.tensor_tensor(acc, acc, to, ALU.add).then_inc(conv_ready if last else pool_step, 1)
                        steps += not last
                pool.wait_ge(conv_ready, c + 1)
            y_sums(1)
            scale_x(2)
            y_sums(2)

        @block.scalar
        def _(act):
            def hi(phase, u, size=NCH * UC, more=0):
                k = (phase[1] + u) % RING
                act.wait_ge(raw_in[k], raw_count_w(phase, u) + 16 // RING * more)
                n = phase[0] + u - slots(phase) + 1
                if n > 0:
                    act.wait_ge(w_used, n + more)
                act.copy(whi[:, slot_w(phase, u), 0:size], raw[:, k, 0:size]).then_inc(w_hi, 1)

            def hi_down(phase, u):
                hi(phase, u, down_size(phase, u))

            act.dma_start(prow[0:8, 3, :], i["c_prompt"].rearrange("b (r f) -> (b r) f", f=P)).then_inc(ld_c, 16)
            act.dma_start(prow[8:72, 3, :], i["c_sample"].rearrange("b (r f) -> (b r) f", f=P)).then_inc(ld_c, 16)
            act.wait_ge(c_t, 1)
            act.activation(cT[:, :], bank[:, 0, 384:456], ACT.Silu).then_inc(c_silu, 1)
            act.wait_ge(c_silu, 1)
            act.copy(chl[:, :, 0:9].rearrange("p k r -> p r k"), cT[:, :].rearrange("p (r k) -> p r k", r=9)).then_inc(c_hi, 1)
            for u in range(3):
                hi(ADA, u)

            def ada_rows(a, a_, used, b=4):
                act.wait_ge(w_used, used)
                if a_ >= 2:
                    act.wait_ge(ada_t, a - 1)
                act.copy(rows[:, a_ % 2, :], bank[0:18, b + a_ % 2, 0:UC]).then_inc(ada_row, 1)

            def split_m(u):
                for n in mod_chunks(u):
                    act.wait_ge(m_ready, n + 1)
                    act.copy(mh[:, n, :], yT[:, n, :]).then_inc(mh_ready, 1)

            for u in range(ADA[2]):
                ada_rows(u, u, u + 1)
                split_m(u)
                if u + 3 < ADA[2]:
                    hi(ADA, u + 3)
                else:
                    hi(UP1, u + 3 - ADA[2])
                if u == X_AT:
                    for n in range(6):
                        act.wait_ge(x_t, n + 1)
                        tt, half = n // 2, n % 2
                        w = P if tt < 2 else NS
                        act.copy(xT[:, 4 * half:4 * half + 4, P * tt:P * tt + w],
                                 bank[:, n % 4, :].rearrange("p (c t) -> p c t", t=P)[:, :, 0:w]).then_inc(x_in, 1)

            def up(ffn, phase, down):
                gr, sr, hr, hhr = g_ready[ffn], silu_ready[ffn], h_ready[ffn], hh_ready[ffn]

                per = stride(ffn)

                def body(pair, pair_):
                    more = per * (pair - pair_)

                    def hi_next(n):
                        n += per * pair_
                        if n < phase[2]:
                            hi(phase, n, more=more)
                        else:
                            hi_down(down, n - phase[2])

                    for cc in range(2):
                        if cc == 0:
                            act.wait_ge(gr, pair + 1)
                        else:
                            act.wait_ge(w_used, phase[0] + per * pair + 1)
                        if pair_:
                            act.wait_ge(hr, 2 * pair + cc - 1)
                        act.activation(tmp[:, cc, :], bank[:, cc, 0:T], ACT.Silu).then_inc(sr, 1)
                    if ffn == 0:
                        hi_next(3)
                        ada_rows(ADA[2] + 2 * pair, ADA[2] + 2 * pair_, phase[0] + per * pair + 2)
                        hi_next(4)
                    else:
                        hi_next(2)
                        hi_next(3)
                    for cc in range(2):
                        act.wait_ge(hr, 2 * pair + cc + 1)
                        act.copy(hh[:, bass.ds(2 * pair + cc, 1), :].rearrange("p a t -> p (a t)"), tmp[:, 2 + cc, :]).then_inc(hhr, 1)
                    if ffn == 0:
                        hi_next(5)
                        ada_rows(ADA[2] + 2 * pair + 1, ADA[2] + 2 * pair_ + 1, phase[0] + per * pair + 4)
                        hi_next(6)
                up_pairs(act, ffn, body)

            def down(phase, nxt):
                ahead = slots(phase)
                for u in range(phase[2]):
                    nb, third = down_unit(phase, u)
                    if third < 0:
                        ada_rows(ADA_DN + nb, ADA_DN + nb, phase[0] + u + 1, b=0)
                    if u + ahead < phase[2]:
                        hi_down(phase, u + ahead)
                    elif nxt is not None:
                        hi(nxt, u + ahead - phase[2])

            def norm(n):
                for q in range(4):
                    act.wait_ge(yc_ready, 4 * n + q + 1)
                    act.activation(squares(q), yT[:, 2 * q:2 * q + 2, :], ACT.Square).then_inc(sq_ready, 1)
                act.wait_ge(var_ready, n + 1)
                act.activation(tmp[:, 0, :], bank[:, 1, 0:T], ACT.Sqrt, bias=con[:, C_EPS:C_EPS + 1]).then_inc(std_ready, 1)
                for q in range(NCH):
                    if n < 2:
                        act.wait_ge(m_ready, 8 * (1 + 2 * n) + q + 1)
                        act.copy(mh[:, q, :], uT[:, q, :]).then_inc(mh_ready, 1)
                    act.wait_ge(xn_ready, 8 * n + q + 1)
                    act.activation(xT[:, q, :], yT[:, q, :], ACT.Identity, scale=par1[:, 72 + 8 * n + q:73 + 8 * n + q],
                                   bias=par1[:, 96 + 8 * n + q:97 + 8 * n + q]).then_inc(x_ready, 1)

            up(0, UP1, DN1)
            down(DN1, WIN)
            norm(0)

            for u, b in enumerate(WIN_ORDER):
                for cc in range(2):
                    act.wait_ge(*((win_mm, u + 1) if cc == 0 else (w_used, WIN[0] + u + 1)))
                    c = 2 * b + cc
                    src = bank[:, 2 * (u % 2) + cc, 0:T]
                    if c >= 16:
                        act.activation(yT[:, c - 16, :], src, ACT.Sigmoid).then_inc(sig_ready, 1)
                    elif c < 4:
                        act.mul(uT[:, c, :], src, HD ** -0.5).then_inc(u_out, 1)
                    elif c < 12:
                        act.copy(uT[:, c, :], src).then_inc(u_out, 1)
                if u + 3 < WIN[2]:
                    hi(WIN, u + 3)

            for g in range(2):
                act.wait_ge(st_t, g + 1)
                act.copy(cbuf[:, :, ST + SEQ + 4 * g * SB:ST + SEQ + 4 * (g + 1) * SB].rearrange("p c (b k) -> p c b k", b=4)[:, :, :, 0:ST],
                         bank[:, 4 + g, 0:480].rearrange("p (c b k) -> p c b k", c=NCC, b=4)).then_inc(st_in, 1)
            dst = [vtok[:, 0, :], vtok[:, 1, :], vsam[:, :], ktok[:, 0, :], ktok[:, 1, :], ksam]
            for n in range(6):
                act.wait_ge(tok_t, n + 1)
                w = P if n % 3 < 2 else NS
                act.copy(dst[n], bank[0:w, n % 4, :]).then_inc(tok_out, 1)
            act.wait_ge(glu_ready, NCC)
            act.copy(gsam.rearrange("p c (b t) -> p c b t", b=DB),
                     cbuf[:, :, ST + SEQ:CB].rearrange("p c (b k) -> p c b k", b=DB)[:, :, :, ST:SB]).then_inc(gs_copy, 1)
            act.wait_ge(gl_t, 1)
            act.copy(cout, bank[0:ST, 6, :]).then_inc(gl_out, 1)
            act.wait_ge(gl_t, 2)
            act.copy(csam, bank[0:NS, 7, :]).then_inc(gl_out, 1)
            act.wait_ge(u_out, 12)
            act.wait_ge(q_zero, 4)
            act.copy(khn, uT[:, 4:8, SEQ:T])
            act.copy(qh, uT[:, 0:NHP, SEQ:T]).then_inc(qs_hi, 1)
            act.wait_ge(qs_hi, 1)
            for e in range(2):
                ins = act.copy(koh[0:64, :, :].rearrange("p (m e) t -> p m e t", e=2)[:, :, e, :], khn[64 * e:64 * e + 64, :, :].bitcast(F32))
            ins.then_inc(ko_hi, 1)
            def prompt_exp(h):
                act.wait_ge(pmax_ready, h + 1)
                for q, (a, b) in enumerate(((0, P), (P, 3 * P))):
                    ins = act.activation(ps_[:, h % 3, a:b], ps_[:, h % 3, a:b], ACT.Exp, bias=pm[:, h % 3, q:q + 1],
                                         accum_out=pz[:, h % 3, q:q + 1])
                ins.then_inc(pexp, 1)

            def prompt_turned(h):
                act.wait_ge(pp_t, h + 1)
                if h >= 2:
                    act.wait_ge(pv_mm, h - 1)
                act.copy(ppT[:, h % 2, :], bank[:, 2 + h % 2, 0:384]).then_inc(pp_out, 1)

            def prompt_out(m):
                act.wait_ge(pv_mm, 2 * m + 2)
                act.copy(yT[:, m, 0:SEQ], bank[:, 4 + m % 2, 0:SEQ]).then_inc(pv_out, 1)

            prompt_exp(0)
            prompt_exp(1)
            for h in range(NH):
                prompt_turned(h)
                if h + 2 < NH:
                    prompt_exp(h + 2)
                if h and h % 2 == 0:
                    prompt_out(h // 2 - 1)
            prompt_out(NHP - 1)

            def q_high(j, b2, first=False):
                if first:
                    act.wait_ge(qs_hi, 1)
                elif b2:
                    act.wait_ge(own_ready, 2 * j + 1)
                else:
                    act.wait_ge(own_ready, 2 * j)
                for r in range(2):
                    for e in range(2):
                        at = 64 * r + QPITCH * e
                        ins = act.copy(qbh[64 * r:64 * r + 64, at:at + NHP * 2 * QPITCH].rearrange("p (m c) -> p m c", m=NHP)[:, :, 0:DT],
                                       qh[64 * e:64 * e + 64, :, bass.ds(DT * (2 * j + b2), DT)].bitcast(F32))
                ins.then_inc(q_hi, 1)

            q_high(0, 0, True)

            def act_pages(cache, seq, c, k, wait=None):
                load_pages(act, cache, seq, c, k, (2, 3), wait)

            def attn_out(j, b=7):
                act.wait_ge(at_mm, j + 1)
                act.copy(yT[:, 0:NHP, bass.ds(SEQ + 2 * DT * j, 2 * DT)].rearrange("p m (b t) -> p m b t", b=2),
                         bank[:, b, 0:NS].rearrange("p (b m t) -> p m b t", b=2, m=NHP)).then_inc(av_evac, 1)

            def pair_body(j, first=False, last=False):
                for k in range(8):
                    for hf in range(2):
                        act.wait_ge(kt_ready, 16 * j + 2 * k + hf + 1)
                        if hf == 0 and not (first and k < 2):
                            act.wait_ge(k_used, 8 * j + k - 1)
                        act.copy(kh[:, k % 2, 2 * hf:2 * hf + 2, :], bank[:, 2 * hf:2 * hf + 2, :]).then_inc(kt_hi, 1)
                    if k < RING:
                        act_pages("k", 2 * j + (k + RING) // 4, k, k)
                    elif first:
                        act_pages("k", 2, k - RING, k)
                    else:
                        act_pages("v", 2 * (j - 1), k - RING, k)
                    if k == 4:
                        q_high(j, 1)

                def behind_values(k):
                    wait = (v_used, 8 * (j - 1) + k + 1)
                    if k < RING:
                        act_pages("v", 2 * (j - 1) + 1, k, k, wait)
                    elif last:
                        act_pages("v", 2 * j, k - RING, k, wait)
                    else:
                        act_pages("k", 2 * (j + 1), k - RING, k, wait)

                if not first:
                    for k in range(3):
                        behind_values(k)
                act.wait_ge(eb_ready, j + 1)
                for b2 in range(2):
                    ins = act.activation(s[:, b2, :], s[:, b2, :], ACT.Exp, bias=ebias[:, b2:b2 + 1], accum_out=rt[:, b2:b2 + 1])
                ins.then_inc(ex_ready, 1)
                if not last:
                    q_high(j + 1, 0)
                if not first:
                    for k in range(3, 8):
                        behind_values(k)
                for r in range(4):
                    act.wait_ge(pt_ready, 5 * j + r + 1)
                    act.copy(pT[:, 512 * r:512 * r + 512], bank[:, 4 + r % 2, :]).then_inc(pt_evac, 1)
                act.wait_ge(pt_ready, 5 * j + 5)
                act.copy(po[:, :], bank[0:NS, 6, 0:2 * P]).then_inc(pt_evac, 1)
                if not first:
                    attn_out(j - 1)

            act.wait_ge(stored_early, 16 * N_EARLY)
            pair_body(0, first=True)
            with act.Fori(1, 3) as j:
                pair_body(j)
            pair_body(3, last=True)

            for c in range(NCC):
                act.wait_ge(gc_ready, c + 1)
                act.activation(tmp[:, c, :], yT[:, NCC + c, :], ACT.Square).then_inc(gq_ready, 1)
            def behind_last_values(k):
                act_pages("v", 7, k, k, (v_used, 24 + k + 1))

            behind_last_values(0)
            for c in range(NCC):
                act.wait_ge(gv_mm, c + 1)
                act.activation(tmp[:, c, :], bank[:, 4 + c, 0:T], ACT.Sqrt, bias=con[:, C_EPS:C_EPS + 1]).then_inc(gs_ready, 1)
            behind_last_values(1)
            for c in range(NCC):
                act.wait_ge(gx_ready, c + 1)
                act.activation(tmp[:, c, :], yT[:, NCC + c, :], ACT.Silu, scale=par2[:, 4 + c:5 + c], bias=par2[:, 8 + c:9 + c]).then_inc(gy_ready, 1)
                if c in (1, 2):
                    behind_last_values(c + 1)
            for n, c in enumerate(MIX_ORDER):
                act.wait_ge(m_ready, 16 + n + 1)
                act.copy(mh[:, c, :], yT[:, c, :]).then_inc(mh_ready, 1)
                if n == NCC - 1:
                    act.wait_ge(k_used, 32)
                    hi(WOUT, 0)
                    hi(WOUT, 1)
                    attn_out(3, 0)
            for u in range(WOUT[2]):
                if u < 2:
                    hi(WOUT, u + 2)
                else:
                    hi(UP2, u - 2)
            norm(1)
            up(1, UP2, DN2)
            down(DN2, None)
            norm(2)

        @block.vector
        def _(dve):
            step = [0]

            def link(ins):
                ins.then_inc(dve_step, 1)
                step[0] = step[0] + 1
                dve.wait_ge(dve_step, step[0])

            def lo(phase, u, size=NCH * UC, more=0):
                k = (phase[1] + u) % RING
                dve.wait_ge(w_hi, phase[0] + u + 1 + more)
                dve.tensor_tensor(wlo[:, slot_w(phase, u), 0:size], raw[:, k, 0:size], whi[:, slot_w(phase, u), 0:size].bitcast(F32),
                                  ALU.subtract).then_inc(w_lo, 1)

            def lo_down(phase, u):
                lo(phase, u, down_size(phase, u))

            dve.wait_ge(c_hi, 1)
            dve.tensor_tensor(chl[:, :, 9:18].rearrange("p k r -> p r k"), cT[:, :].rearrange("p (r k) -> p r k", r=9),
                              chl[:, :, 0:9].rearrange("p k r -> p r k").bitcast(F32), ALU.subtract).then_inc(c_lo, 1)
            for u in range(3):
                lo(ADA, u)
            dve.wait_ge(par_t, 1)
            dve.tensor_copy(par1[:, :], bank[:, 1, 0:120]).then_inc(par_ready, 1)
            dve.tensor_copy(par2[:, :], bank[:, 1, 128:148])
            dve.tensor_copy(dwT[:, :], bank[:, 1, 256:380]).then_inc(par_ready, 1)
            dve.wait_ge(par_ready, 2)
            one = par1[:, 0:72].rearrange("p (a b n) -> p a b n", a=3, b=3)[:, :, 1, :]
            link(dve.tensor_scalar(one, one, 1.0, None, ALU.add))

            def ada_turn(a, a_, b=6):
                dve.wait_ge(ada_t, a + 1)
                dve.tensor_tensor(adaT[:, bass.ds(2 * a, 2), :], bank[:, b + a_ % 2, 0:18].rearrange("p (c r) -> p c r", c=2),
                                  par1[:, bass.ds(2 * a, 2)].unsqueeze(2).to_broadcast([P, 2, 9]), ALU.add).then_inc(ada_out, 1)

            def half_gate(sub):
                g = adaT[:, (3 * sub + 2) * NCH:(3 * sub + 3) * NCH, :]
                link(dve.tensor_scalar(g, g, 0.5, None, ALU.mult))

            def samples(ap):
                return ap[:, SEQ:T].rearrange("p (b t) -> p b t", b=DB)

            def vec(sub, kind, n):
                return adaT[:, (3 * sub + kind) * NCH + n, :]

            def per_seq(v):
                return v[:, 1:9].unsqueeze(2).to_broadcast([P, DB, DT])

            def modulate(sub, n):
                x, y = xT[:, n, :], yT[:, n, :]
                sc, sh = vec(sub, 1, n), vec(sub, 0, n)
                dve.tensor_scalar(y[:, 0:SEQ], x[:, 0:SEQ], sc[:, 0:1], sh[:, 0:1], ALU.mult, ALU.add)
                link(dve.tensor_tensor(samples(y), samples(x), per_seq(sc), ALU.mult))
                dve.tensor_tensor(samples(y), samples(y), per_seq(sh), ALU.add).then_inc(m_ready, 1)

            def low(n, count, src=yT):
                dve.wait_ge(mh_ready, count)
                dve.tensor_tensor(ml[:, n, :], src[:, n, :], mh[:, n, :].bitcast(F32), ALU.subtract).then_inc(ml_ready, 1)

            def add_residual(sub, n, src, ready):
                dve.wait_ge(*ready)
                g = vec(sub, 2, n)
                dve.scalar_tensor_tensor(yT[:, n, 0:SEQ], src[:, 0:SEQ], g[:, 0:1], xT[:, n, 0:SEQ], ALU.mult, ALU.add)
                link(dve.tensor_tensor(samples(yT[:, n, :]), samples(src), per_seq(g), ALU.mult))
                dve.tensor_tensor(samples(yT[:, n, :]), samples(yT[:, n, :]), samples(xT[:, n, :]), ALU.add).then_inc(y_ready, 1)

            def up(ffn, phase, down):
                sr, ur, hr, hhr, hlr = silu_ready[ffn], u_ready[ffn], h_ready[ffn], hh_ready[ffn], hl_ready[ffn]

                per = stride(ffn)

                def body(pair, pair_):
                    def lo_next(n):
                        n += per * pair_
                        if n < phase[2]:
                            lo(phase, n, more=per * (pair - pair_))
                        else:
                            lo_down(down, n - phase[2])

                    if ffn == 0:
                        lo_next(3)
                        ada_turn(ADA[2] + 2 * pair - 1, ADA[2] + 2 * pair_ - 1)
                        lo_next(4)
                    else:
                        lo_next(2)
                    for cc in range(2):
                        dve.wait_ge(sr, 2 * pair + cc + 1)
                        dve.wait_ge(*((ur, pair + 1) if cc == 0 else (w_used, phase[0] + per * pair + per // 2 + 1)))
                        if pair_:
                            dve.wait_ge(hlr, 2 * pair + cc - 1)
                        dve.tensor_tensor(tmp[:, 2 + cc, :], bank[:, 2 + cc, 0:T], tmp[:, cc, :], ALU.mult).then_inc(hr, 1)
                    if ffn == 0:
                        ada_turn(ADA[2] + 2 * pair, ADA[2] + 2 * pair_)
                        lo_next(5)
                    else:
                        lo_next(3)
                    for cc in range(2):
                        dve.wait_ge(hhr, 2 * pair + cc + 1)
                        f = bass.ds(2 * pair + cc, 1)
                        dve.tensor_tensor(hl[:, f, :].rearrange("p a t -> p (a t)"), tmp[:, 2 + cc, :],
                                          hh[:, f, :].rearrange("p a t -> p (a t)").bitcast(F32), ALU.subtract).then_inc(hlr, 1)
                    if ffn == 0:
                        lo_next(6)
                up_pairs(dve, ffn, body)

            def down(sub, phase, nxt, n0):
                dve.wait_ge(ax_ready, sub + 1)
                ahead = slots(phase)
                for u in range(phase[2]):
                    nb, third = down_unit(phase, u)
                    last = u == phase[2] - 1
                    if u + ahead < phase[2]:
                        lo_down(phase, u + ahead)
                    elif nxt is not None and not last:
                        lo(nxt, u + ahead - phase[2])
                    if phase is DN1 and third == (1 if nb else 2):
                        ada_turn(ADA_DN + nb, ADA_DN + nb, b=2)
                    if third == 2:
                        for cc in range(2):
                            n = 2 * nb + cc
                            add_residual(sub, n, bank[:, 4 + 2 * (nb % 2) + cc, :],
                                         (n_ready, n0 + nb + 1) if cc == 0 else (w_used, phase[0] + u + 1))

            def norm(n, meanwhile=lambda: None):
                dve.wait_ge(mean_ready, n + 1)
                dve.wait_ge(y_ready, 8 * (n + 1))
                for q in range(4):
                    y = yT[:, 2 * q:2 * q + 2, :]
                    dve.tensor_tensor(y, y, bank[:, 0:1, 0:T].to_broadcast([P, 2, T]), ALU.subtract).then_inc(yc_ready, 1)
                for q in range(4):
                    dve.wait_ge(sq_ready, 4 * n + q + 1)
                    two = squares(q)
                    dve.tensor_tensor(two[:, 0, :], two[:, 0, :], two[:, 1, :], ALU.add).then_inc(sqsum_ready, 1)
                meanwhile()
                dve.wait_ge(std_ready, n + 1)
                link(dve.reciprocal(tmp[:, 1, :], tmp[:, 0, :]))
                dve.wait_ge(fold_ready, 1)

                def scale(q):
                    y = yT[:, q, :]
                    dve.tensor_tensor(y, y, tmp[:, 1, :], ALU.mult).then_inc(xn_ready, 1)

                scale(0)
                for q in range(NCH):
                    if q + 1 < NCH:
                        scale(q + 1)
                    if n < 2:
                        dve.wait_ge(xn_ready, 8 * n + q + 1)
                        y, m = yT[:, q, :], uT[:, q, :]
                        g, b = fold_g[:, n, q, :], fold_b[:, n, q, :]
                        dve.tensor_scalar(m[:, 0:SEQ], y[:, 0:SEQ], g[:, 0:1], b[:, 0:1], ALU.mult, ALU.add)
                        link(dve.tensor_tensor(samples(m), samples(y), per_seq(g), ALU.mult))
                        dve.tensor_tensor(samples(m), samples(m), per_seq(b), ALU.add).then_inc(m_ready, 1)
                        if q:
                            low(q - 1, 8 * (n + 1 + (n == 1)) + q, uT)
                if n < 2:
                    low(7, 8 * (n + 1 + (n == 1)) + 8, uT)

            for u in range(ADA[2]):
                if u >= 1:
                    ada_turn(u - 1, u - 1)
                if u == MOD_AT:
                    dve.wait_ge(ada_out, 8)
                    dve.wait_ge(x_in, 6)
                for n in mod_chunks(u):
                    modulate(0, n)
                    if n:
                        low(n - 1, n)
                if u == MOD_AT:
                    low(7, 8)
                if u + 3 < ADA[2]:
                    lo(ADA, u + 3)
                else:
                    lo(UP1, u + 3 - ADA[2])
            up(0, UP1, DN1)
            ada_turn(ADA_DN - 1, ADA_DN - 1)
            dve.wait_ge(ada_out, ADA_DN)
            half_gate(0)
            down(0, DN1, WIN, 0)
            norm(0, lambda: lo(WIN, slots(DN1) - 1))
            dve.wait_ge(ada_out, ADAN)
            half_gate(2)

            for u, b in enumerate(WIN_ORDER):
                if u + 3 < WIN[2]:
                    lo(WIN, u + 3)
                if u in (2, 3):
                    for cc in range(2):
                        c = 2 * (u - 2) + cc
                        dve.wait_ge(*((win_mm, u + 1) if cc == 0 else (w_used, WIN[0] + u + 1)))
                        dve.wait_ge(sig_ready, c + 1)
                        src = bank[:, 2 * (u % 2) + cc, :]
                        dve.tensor_tensor(cbuf[:, c, ST:ST + SEQ], src[:, 0:SEQ], yT[:, c, 0:SEQ], ALU.mult)
                        dve.tensor_tensor(cbuf[:, c, ST + SEQ:CB].rearrange("p (b k) -> p b k", b=DB)[:, :, ST:SB],
                                          samples(src), samples(yT[:, c, :]), ALU.mult).then_inc(glu_ready, 1)

            def prompt_scores(h):
                dve.wait_ge(ps_mm, h + 1)
                if h >= 3:
                    dve.wait_ge(pp_t, h - 2)
                sc = ps_[:, h % 3, :]
                dve.scalar_tensor_tensor(sc, con[:, C_REL:C_REL + 384], 2.0 ** -(h + 1), bank[:, h % 2, 0:384], ALU.mult, ALU.add).then_inc(ps_ready, 1)
                dve.wait_ge(ps_ready, h + 1)
                dve.tensor_reduce(pm[:, h % 3, 0:1], sc[:, 0:P], AX, ALU.max, negate=True)
                dve.tensor_reduce(pm[:, h % 3, 1:2], sc[:, P:3 * P], AX, ALU.max, negate=True).then_inc(pmax_ready, 1)

            def prompt_probs(h):
                dve.wait_ge(pexp, h + 1)
                link(dve.reciprocal(pr[:, h % 3, :], pz[:, h % 3, :]))
                dve.tensor_scalar(ps_[:, h % 3, 0:P], ps_[:, h % 3, 0:P], pr[:, h % 3, 0:1], None, ALU.mult)
                dve.tensor_scalar(ps_[:, h % 3, P:3 * P], ps_[:, h % 3, P:3 * P], pr[:, h % 3, 1:2], None, ALU.mult).then_inc(pp_ready, 1)

            prompt_scores(0)
            prompt_scores(1)
            for h in range(NH):
                prompt_probs(h)
                if h + 2 < NH:
                    prompt_scores(h + 2)
            dve.wait_ge(qs_hi, 1)
            dve.tensor_tensor(kln, uT[:, 4:8, SEQ:T], khn.bitcast(F32), ALU.subtract)
            dve.tensor_tensor(ql, uT[:, 0:NHP, SEQ:T], qh.bitcast(F32), ALU.subtract).then_inc(qs_lo, 1)
            dve.wait_ge(qs_lo, 1)
            dve.wait_ge(ko_hi, 1)
            for e in range(2):
                ins = dve.tensor_copy(kol[0:64, :, :].rearrange("p (m e) t -> p m e t", e=2)[:, :, e, :], kln[64 * e:64 * e + 64, :, :].bitcast(F32))
            ins.then_inc(ko_lo, 1)

            def q_low(j, b2, first=False):
                if first:
                    dve.wait_ge(qs_lo, 1)
                dve.wait_ge(q_hi, 2 * j + b2 + 1)
                for r in range(2):
                    for e in range(2):
                        at = 64 * r + QPITCH * e
                        ins = dve.tensor_copy(qbl[64 * r:64 * r + 64, at:at + NHP * 2 * QPITCH].rearrange("p (m c) -> p m c", m=NHP)[:, :, 0:DT],
                                              ql[64 * e:64 * e + 64, :, bass.ds(DT * (2 * j + b2), DT)].bitcast(F32))
                ins.then_inc(q_lo, 1)

            def score_chunk(j, g):
                b2, n = g // 2, 4 * (g % 2)
                dve.wait_ge(k_used, 8 * j + 2 * g + 2)
                sbk = bank[:, 4 + g % 2, :].rearrange("p (n k) -> p n k", n=4)
                sc = s[:, b2, P * n:P * n + 512].rearrange("p (n k) -> p n k", n=4)
                dve.tensor_reduce(gsum[:, b2, n:n + 4], sbk, AX, ALU.add)
                dve.scalar_tensor_tensor(sc, con[:, C_POS:C_POS + P].unsqueeze(1).to_broadcast([P, 4, P]), con[:, C_M:C_M + 1], sbk,
                                         ALU.mult, ALU.add).then_inc(s_evac, 1)
                dve.wait_ge(s_evac, 4 * j + g + 1)
                dve.tensor_reduce(bmax[:, b2, n:n + 4], sc, AX, ALU.max)

            def attn_rows(j, seqs=(0, 1)):
                for b2 in seqs:
                    dve.wait_ge(acc_ready, 2 * j + b2 + 1)
                    for g in range(4):
                        rr = slice(32 * g, 32 * g + 32)
                        acc = bank[rr, 2 * b2 + g % 2, :].rearrange("p (h r d) -> p h r d", h=4, r=2)[:, :, g // 2, :]
                        ins = dve.tensor_tensor(ahead[rr, b2], acc, con[rr, C_HEAD:C_HEAD + 4].unsqueeze(2).to_broadcast([32, 4, HD]), ALU.mult)
                    link(ins)
                    dve.tensor_reduce(arow[:, b2, :], ahead[:, b2].rearrange("p h d -> p d h"), AX, ALU.add).then_inc(arow_ready, 1)

            def pair_body(j, first=False, last=False):
                for k in range(8):
                    for hf in range(2):
                        dve.wait_ge(kt_hi, 16 * j + 2 * k + hf + 1)
                        dve.tensor_tensor(kl[:, k % 2, 2 * hf:2 * hf + 2, :], bank[:, 2 * hf:2 * hf + 2, :],
                                          kh[:, k % 2, 2 * hf:2 * hf + 2, :].bitcast(F32), ALU.subtract).then_inc(kt_lo, 1)
                    if k == 2 and not first:
                        dve.wait_ge(pt_ready, 5 * j)
                    if k == 4:
                        q_low(j, 1)
                    if k % 2 == 0 and k:
                        score_chunk(j, k // 2 - 1)
                score_chunk(j, 3)
                dve.wait_ge(own_ready, 2 * j + 2)
                for b2 in range(2):
                    ins = dve.tensor_tensor(s[:, b2, PAST // 2:], bank[:, 6, NS * b2:NS * b2 + NS],
                                            con[:, bass.ds(C_OWN + 56 - DT * (2 * j + b2), NS)], ALU.add)
                ins.then_inc(gsum_ready, 1)
                dve.wait_ge(gsum_ready, j + 1)
                dve.wait_ge(gate_mm, j + 1)
                link(dve.tensor_copy(gate[:, :, :], bank[:, 6, 256:272].rearrange("p (b n) -> p b n", b=2)))
                dve.tensor_reduce(bmax[:, 0:1, 8:9], s[:, 0:1, PAST // 2:], AX, ALU.max)
                for b2 in range(2):
                    ins = dve.max(gmax[:, b2, :], gate[:, b2, :])
                link(ins)
                dve.tensor_reduce(bmax[:, 1:2, 8:9], s[:, 1:2, PAST // 2:], AX, ALU.max)
                for b2 in range(2):
                    ins = dve.max_index(gidx[:, b2, :], gmax[:, b2, :], gate[:, b2, :])
                link(ins)
                link(dve.tensor_copy(gidf[:, :, :], gidx[:, :, :]))
                for b2 in range(2):
                    ins = dve.tensor_tensor(hit[:, b2], con[:, C_IOTA:C_IOTA + 8].unsqueeze(2).to_broadcast([P, 8, 3]),
                                            gidf[:, b2, 0:3].unsqueeze(1).to_broadcast([P, 8, 3]), ALU.is_equal)
                link(ins)
                link(dve.tensor_reduce(ebase[:, :, :], hit[:, :, :, :], AX, ALU.add))
                link(dve.tensor_scalar(ebase[:, :, :], ebase[:, :, :], -1.0, -NEG, ALU.add, ALU.mult))
                link(dve.tensor_tensor(ebase[:, :, :], ebase[:, :, :], con[:, C_RC:C_RC + 8].unsqueeze(1).to_broadcast([P, 2, 8]), ALU.add))
                link(dve.tensor_tensor(bmax[:, :, 0:8], bmax[:, :, 0:8], ebase[:, :, :], ALU.add))
                dve.tensor_reduce(nmax[:, :], bmax[:, :, :], AX, ALU.max, negate=True).then_inc(nmax_ready, 1)
                for b2 in range(2):
                    sc = s[:, b2, 0:PAST // 2].rearrange("p (n k) -> p n k", n=NBLK)
                    dve.tensor_tensor(sc, sc, ebase[:, b2, :].unsqueeze(2).to_broadcast([P, NBLK, P]), ALU.add)
                dve.wait_ge(swap_mm, j + 1)
                dve.tensor_tensor(ebias[:, :], nmax[:, :], bank[:, 6, 288:290], ALU.min).then_inc(eb_ready, 1)
                dve.wait_ge(rsum_mm, j + 1)
                link(dve.reciprocal(ri[:, :], bank[:, 6, 320:322]))
                dve.tensor_scalar(s[:, 0, :], s[:, 0, :], ri[:, 0:1], None, ALU.mult)
                dve.tensor_scalar(s[:, 1, :], s[:, 1, :], ri[:, 1:2], None, ALU.mult).then_inc(p_ready, 1)
                if not first:
                    attn_rows(j - 1)
                if not last:
                    q_low(j + 1, 0)

            q_low(0, 0, True)
            dve.wait_ge(stored_early, 16 * N_EARLY)
            pair_body(0, first=True)
            before = step[0]
            PAIR_STEPS = 12
            with dve.Fori(1, 3) as j:
                step[0] = before + PAIR_STEPS * (j - 1)
                pair_body(j)
            step[0] = before + 2 * PAIR_STEPS
            pair_body(3, last=True)

            for c in range(NCC):
                dve.wait_ge(gm_mm, c + 1)
                y = yT[:, NCC + c, :]
                dve.tensor_tensor(y, y, bank[:, 4 + c, 0:T], ALU.subtract).then_inc(gc_ready, 1)
            for c in range(NCC):
                dve.wait_ge(gs_ready, c + 1)
                y = yT[:, NCC + c, :]
                link(dve.reciprocal(tmp[:, c, :], tmp[:, c, :]))
                dve.tensor_tensor(y, y, tmp[:, c, :], ALU.mult).then_inc(gx_ready, 1)
            for c in range(NCC):
                dve.wait_ge(gy_ready, c + 1)
                dve.tensor_scalar(yT[:, NCC + c, :], tmp[:, c, :], par2[:, 16 + c:17 + c], None, ALU.mult).then_inc(m_ready, 1)
                if c:
                    low(NCC + c - 1, 16 + c)
            low(7, 16 + NCC)
            attn_rows(3, (0,))
            lo(WOUT, 0)
            attn_rows(3, (1,))
            lo(WOUT, 1)
            dve.wait_ge(av_evac, 4)
            dve.wait_ge(pv_out, 4)
            for c in range(NHP):
                dve.tensor_scalar(yT[:, c, :], yT[:, c, :], par2[:, 12 + c:13 + c], None, ALU.mult).then_inc(m_ready, 1)
                if c:
                    low(c - 1, 16 + NCC + c)
            low(NHP - 1, 24)

            dve.wait_ge(ax_ready, 2)
            for u in range(WOUT[2]):
                if u < 2:
                    lo(WOUT, u + 2)
                elif u == 3:
                    lo(UP2, 0)
                for cc in range(2):
                    n = 2 * u + cc
                    add_residual(1, n, bank[:, 4 + 2 * (u % 2) + cc, :], (n_ready, 4 + u + 1) if cc == 0 else (w_used, WOUT[0] + u + 1))
            norm(1, lambda: lo(UP2, 1))
            up(1, UP2, DN2)
            down(2, DN2, None, 8)
            norm(2)
            for n in range(6):
                dve.wait_ge(out_t, n + 1)
                half, tt = n // 3, n % 3
                w = P if tt < 2 else NS
                dve.tensor_copy(yrow[0:w, tt, 512 * half:512 * half + 512], bank[0:w, 2 + n, :]).then_inc(out_row, 1)

        @block.tensor
        def _(pe):
            pe.wait_ge(ld_ident, 16)
            pe.wait_ge(ld_c, 32)
            pe.transpose(bank[:, 0, 384:456], prow[0:72, 3, :], ident[0:72, 0:72]).then_inc(c_t, 1)

            def turn_params():
                pe.wait_ge(ld_con, 16)
                pe.wait_ge(ld_par, 16 * 9)
                pe.transpose(bank[:, 1, 0:120], prow[0:120, 0, :], ident[0:120, 0:120])
                pe.transpose(bank[:, 1, 128:148], prow[0:20, 1, :], ident[0:20, 0:20])
                pe.transpose(bank[:, 1, 256:380], prow[0:TAPS * NCC, 2, :], ident[0:124, 0:124]).then_inc(par_t, 1)

            def turn_x():
                pe.wait_ge(ld_x, 32)
                pe.wait_ge(par_ready, 2)
                for n in range(6):
                    tt, half = n // 2, n % 2
                    w = P if tt < 2 else NS
                    if n >= 4:
                        pe.wait_ge(x_in, n - 3)
                    for c in range(4):
                        ins = pe.transpose(bank[:, n % 4, P * c:P * c + w], xrow[0:w, tt, 512 * half + P * c:512 * half + P * c + P], ident[0:w, 0:w])
                    ins.then_inc(x_t, 1)

            def ada_turn(a, a_, b=6):
                pe.wait_ge(ada_row, a + 1)
                if a_ >= 2:
                    pe.wait_ge(ada_out, a - 1)
                for cc in range(2):
                    ins = pe.matmul(bank[:, b + a_ % 2, 9 * cc:9 * cc + 9], rows[:, a_ % 2, P * cc:P * cc + P], con[0:18, C_SEL:C_SEL + 9],
                                    start=True, stop=True)
                ins.then_inc(ada_t, 1)

            def ada_product(a, a_, slot, ready, b=4):
                pe.wait_ge(w_lo, ready)
                if a_ >= 2:
                    pe.wait_ge(ada_row, a - 1)
                for kk in range(NCH):
                    for x, w in enumerate((whi, wlo)):
                        ins = pe.matmul(bank[0:18, b + a_ % 2, 0:UC], chl[:, kk, :], w[:, slot, UC * kk:UC * kk + UC],
                                        start=(kk == 0 and x == 0), stop=(kk == NCH - 1 and x == 1))
                ins.then_inc(w_used, 1)

            pe.wait_ge(c_lo, 1)
            for u in range(ADA[2]):
                ada_product(u, u, slot_w(ADA, u), u + 1)
                if u == 1:
                    turn_params()
                if u >= 1:
                    ada_turn(u - 1, u - 1)
                if u == X_AT:
                    turn_x()

            def product(b, slot, cc, parts, start=True, stop=True, ready=None):
                for n, (kk, h_, l_) in enumerate(parts):
                    if ready is not None:
                        ready(n)
                    c = slice(UC * kk + P * cc, UC * kk + P * cc + P)
                    pe.matmul(bank[:, b, 0:T], whi[:, slot, c], h_, start=(start and n == 0), stop=False)
                    pe.matmul(bank[:, b, 0:T], whi[:, slot, c], l_, start=False, stop=False)
                    ins = pe.matmul(bank[:, b, 0:T], wlo[:, slot, c], h_, start=False, stop=(stop and n == len(parts) - 1))
                return ins

            def products(targets, parts, ready, start=True, stop=True):
                for n, (kk, h_, l_) in enumerate(parts):
                    ready(n)
                    for b, slot, cc, done in targets:
                        c = slice(UC * kk + P * cc, UC * kk + P * cc + P)
                        last = stop and n == len(parts) - 1
                        pe.matmul(bank[:, b, 0:T], whi[:, slot, c], h_, start=start and n == 0, stop=False)
                        pe.matmul(bank[:, b, 0:T], whi[:, slot, c], l_, start=False, stop=False)
                        ins = pe.matmul(bank[:, b, 0:T], wlo[:, slot, c], h_, start=False, stop=last)
                        if last:
                            ins.then_inc(done, 1)

            def m_parts(order):
                return [(kk, mh[:, kk, :], ml[:, kk, :]) for kk in order]

            def up(ffn, phase, ml0):
                gr, sr, ur, hr = g_ready[ffn], silu_ready[ffn], u_ready[ffn], h_ready[ffn]

                per = stride(ffn)

                def body(pair, pair_):
                    if pair_ == 0 and ffn == 1:
                        pe.wait_ge(w_lo, phase[0] + 2)
                        products([(0, slot_w(phase, 0), 0, gr), (1, slot_w(phase, 0), 1, w_used), (2, slot_w(phase, 1), 0, ur)],
                                 m_parts(range(NCH)), lambda n: pe.wait_ge(ml_ready, ml0 + n + 1))
                        product(3, slot_w(phase, 1), 1, m_parts(range(NCH))).then_inc(w_used, 1)
                        return
                    for x in range(2):
                        u, u_ = per * pair + per // 2 * x, per * pair_ + per // 2 * x
                        pe.wait_ge(w_lo, phase[0] + u + 1)
                        if pair_ == 0 and x == 0:
                            products([(cc, slot_w(phase, u_), cc, (gr, w_used)[cc]) for cc in range(2)],
                                     m_parts(range(NCH)), lambda n: pe.wait_ge(ml_ready, ml0 + n + 1))
                        for cc in range(2):
                            if pair_:
                                pe.wait_ge((sr, hr)[x], 2 * pair + cc - 1)
                            if pair_ or x:
                                ins = product(2 * x + cc, slot_w(phase, u_), cc, m_parts(range(NCH)))
                                ins.then_inc((gr, ur)[x] if cc == 0 else w_used, 1)
                            if ffn == 0 and cc == 0:
                                ada_turn(ADA[2] + 2 * pair + x - 1, ADA[2] + 2 * pair_ + x - 1)
                        if ffn == 0:
                            ada_product(ADA[2] + 2 * pair + x, ADA[2] + 2 * pair_ + x, slot_w(phase, u_ + 1), phase[0] + u + 2)
                up_pairs(pe, ffn, body)
                if ffn == 0:
                    ada_turn(ADA_DN - 1, ADA_DN - 1)

            def down(ffn, phase, n0):
                hlr = hl_ready[ffn]
                if ffn == 0:
                    pe.wait_ge(silu_ready[0], NF)
                for u in range(phase[2]):
                    nb, third = down_unit(phase, u)
                    if third < 0:
                        ada_product(ADA_DN + nb, ADA_DN + nb, slot_w(phase, u), phase[0] + u + 1, b=0)
                        continue
                    if ffn == 0 and nb == 1 and third == 0:
                        pe.wait_ge(ada_out, ADA_DN)
                    pe.wait_ge(w_lo, phase[0] + u + 1)
                    for cc in range(2):
                        if nb >= 2 and third == 0:
                            pe.wait_ge(y_ready, n0 + 2 * (nb - 2) + cc + 1)
                        ready = (lambda n: pe.wait_ge(hlr, 8 * third + n + 1)) if nb == 0 and cc == 0 else None
                        parts = [(kk, hh[:, 8 * third + kk, :], hl[:, 8 * third + kk, :]) for kk in range(DN_CHUNKS[third])]
                        ins = product(4 + 2 * (nb % 2) + cc, slot_w(phase, u), cc, parts, start=third == 0, stop=third == 2, ready=ready)
                        if cc:
                            ins.then_inc(w_used, 1)
                        elif third == 2:
                            ins.then_inc(n_ready, 1)
                    if ffn == 0 and third == (1 if nb else 2):
                        ada_turn(ADA_DN + nb, ADA_DN + nb, b=2)

            def keep_clock(b, count):
                for _ in range(count):
                    pe.matmul(bank[:, b, 0:T], lnones, con[:, C_REL:C_REL + T], start=True, stop=True)

            def norm(n):
                pe.wait_ge(ysum_step, 6 * n + 6)
                pe.matmul(bank[:, 0, 0:T], lnones, tmp[:, 3, :], start=True, stop=False)
                pe.wait_ge(y_ready, 8 * n + 8)
                pe.matmul(bank[:, 0, 0:T], lnones, yT[:, 7, :], start=False, stop=True).then_inc(mean_ready, 1)
                keep_clock(2, 4)
                for q in range(4):
                    pe.wait_ge(sqsum_ready, 4 * n + q + 1)
                    ins = pe.matmul(bank[:, 1, 0:T], lnones, squares(q)[:, 0, :], start=q == 0, stop=q == 3)
                ins.then_inc(var_ready, 1)
                keep_clock(0, 8)

            up(0, UP1, 0)
            down(0, DN1, 0)
            norm(0)

            pe.wait_ge(w_lo, WIN[0] + 2)
            products([(2 * u + cc, slot_w(WIN, u), cc, (win_mm, w_used)[cc]) for u in range(2) for cc in range(2)],
                     m_parts(range(NCH)), lambda n: pe.wait_ge(ml_ready, 8 + n + 1))
            for u in range(2, WIN[2]):
                pe.wait_ge(w_lo, WIN[0] + u + 1)
                for cc in range(2):
                    if u in (2, 3):
                        pe.wait_ge(sig_ready, 2 * (u - 2) + cc + 1)
                    elif u in (4, 5):
                        pe.wait_ge(glu_ready, 2 * (u - 4) + cc + 1)
                    else:
                        pe.wait_ge(u_out, 2 * (u - 6) + cc + 1)
                    ins = product(2 * (u % 2) + cc, slot_w(WIN, u), cc, m_parts(range(NCH)))
                    ins.then_inc(win_mm if cc == 0 else w_used, 1)

            pe.wait_ge(ld_state, 32)
            for g in range(2):
                for c in range(NCC):
                    ins = pe.transpose(bank[:, 4 + g, 120 * c:120 * c + 120], strow[:, g, P * c:P * c + P], ident[0:120, 0:120])
                ins.then_inc(st_t, 1)
            pe.wait_ge(u_out, 12)
            for n in range(6):
                w = P if n % 3 < 2 else NS
                if n >= 4:
                    pe.wait_ge(tok_out, n - 3)
                for c in range(NHP):
                    ins = pe.transpose(bank[0:w, n % 4, P * c:P * c + P], uT[:, (8 if n < 3 else 4) + c, P * (n % 3):P * (n % 3) + w], ident)
                ins.then_inc(tok_t, 1)
            pe.wait_ge(glu_ready, NCC)
            for c in range(NCC):
                ins = pe.transpose(bank[0:ST, 6, P * c:P * c + P], cbuf[:, c, SEQ:SEQ + ST], ident)
            ins.then_inc(gl_t, 1)
            pe.wait_ge(gs_copy, 1)
            for c in range(NCC):
                ins = pe.transpose(bank[0:NS, 7, P * c:P * c + P], gsam[:, c, :], ident)
            ins.then_inc(gl_t, 1)

            def prompt_qk(h):
                r = slice(64 * (h % 2), 64 * (h % 2) + 64)
                if h >= 2:
                    pe.wait_ge(ps_ready, h - 1)
                q, k = uT[r, h // 2, :], uT[r, 4 + h // 2, :]
                pe.matmul(bank[:, h % 2, 0:P], q[:, 0:P], k[:, 0:P], start=True, stop=True)
                pe.matmul(bank[:, h % 2, P:3 * P], q[:, P:2 * P], k[:, 0:2 * P], start=True, stop=True).then_inc(ps_mm, 1)

            def prompt_turn(h):
                pe.wait_ge(pp_ready, h + 1)
                if h >= 2:
                    pe.wait_ge(pp_out, h - 1)
                for n in range(3):
                    ins = pe.transpose(bank[:, 2 + h % 2, P * n:P * n + P], ps_[:, h % 3, P * n:P * n + P], ident)
                ins.then_inc(pp_t, 1)

            def prompt_pv(h):
                pe.wait_ge(pp_out, h + 1)
                if h >= 4:
                    pe.wait_ge(pv_out, h // 2 - 1)
                r = slice(64 * (h % 2), 64 * (h % 2) + 64)
                b = 4 + h // 2 % 2
                v = [vtok[:, n, HD * h:HD * h + HD] for n in range(2)]
                p_ = ppT[:, h % 2, :]
                pe.matmul(bank[r, b, 0:P], v[0], p_[:, 0:P], start=True, stop=True)
                pe.matmul(bank[r, b, P:2 * P], v[0], p_[:, P:2 * P], start=True, stop=False)
                pe.matmul(bank[r, b, P:2 * P], v[1], p_[:, 2 * P:3 * P], start=False, stop=True).then_inc(pv_mm, 1)

            pe.wait_ge(tok_out, 6)
            pe.wait_ge(st_in, 2)
            prompt_qk(0)
            prompt_qk(1)
            for h in range(NH):
                if h + 2 < NH:
                    prompt_qk(h + 2)
                prompt_turn(h)
                if h:
                    prompt_pv(h - 1)
            prompt_pv(NH - 1)

            def scores(j, k, hf, first):
                g, b2 = k // 2, k // 4
                pe.wait_ge(kt_lo, 16 * j + 2 * k + hf + 1)
                if hf == 0 and k % 4 == 0:
                    pe.wait_ge(q_lo, 2 * j + b2 + 1)
                if hf == 0 and k % 2 == 0 and not (first and g < 2):
                    pe.wait_ge(s_evac, 4 * j + g - 1)
                for h in range(4 * hf, 4 * hf + 4):
                    for x, (q, kk) in enumerate(((qbh, kh), (qbh, kl), (qbl, kh))):
                        ins = pe.matmul(bank[:, 4 + g % 2, BLK * (k % 2):BLK * (k % 2) + BLK], q[:, P * h:P * h + P],
                                        kk[:, k % 2, h // 2, BLK * (h % 2):BLK * (h % 2) + BLK],
                                        start=(h == 0 and x == 0), stop=(h == NH - 1 and x == 2))
                if hf:
                    ins.then_inc(k_used, 1)

            def own_scores(b2):
                for h in range(NH):
                    for x, (q, kk) in enumerate(((qbh, koh), (qbh, kol), (qbl, koh))):
                        ins = pe.matmul(bank[:, 6, NS * b2:NS * b2 + NS], q[:, P * h:P * h + P], kk[:, h, :],
                                        start=(h == 0 and x == 0), stop=(h == NH - 1 and x == 2))
                ins.then_inc(own_ready, 1)

            def page_view(k, pp, h):
                at = 1024 * pp + P * h
                return raw[:, k % RING, at:at + P]

            def raw_wait(k, kv4, turns):
                pe.wait_ge(raw_in[k % RING], raw_count_kv(RING * (kv4 + k // RING)) + turns)

            def pair_keys(j, kv4, turns, first=False):
                for k in range(8):
                    raw_wait(k, kv4, turns)
                    for hf in range(2):
                        if not (first and k == 0):
                            pe.wait_ge(kt_lo, 16 * j + 2 * k + hf - 1)
                        for h in range(4 * hf, 4 * hf + 4):
                            for pp in range(2):
                                at = BLK * (h % 2) + P * pp
                                ins = pe.transpose(bank[:, h // 2, at:at + P], page_view(k, pp, h), ident)
                        ins.then_inc(kt_ready, 1)
                        if k:
                            scores(j, k - 1, hf, first)
                        if k == 4 and hf:
                            own_scores(0)
                scores(j, 7, 0, first)
                scores(j, 7, 1, first)
                own_scores(1)

            def parities(ready, count, matrix, at, src, n, done):
                pe.wait_ge(ready, count)
                pe.matmul(bank[:, 6, at:at + n], con[:, matrix:matrix + P], src, start=True, stop=True).then_inc(done, 1)

            def gate_sum(j):
                parities(gsum_ready, j + 1, C_SUM, 256, gsum[:, :, :].rearrange("p b n -> p (b n)"), 16, gate_mm)

            def max_swap(j):
                parities(nmax_ready, j + 1, C_SWAP, 288, nmax[:, :], 2, swap_mm)

            def prob_sum(j):
                parities(ex_ready, j + 1, C_SUM, 320, rt[:, :], 2, rsum_mm)

            def pair_probs(j):
                pe.wait_ge(p_ready, j + 1)
                for r in range(4):
                    if r >= 2:
                        pe.wait_ge(pt_evac, 5 * j + r - 1)
                    for x in range(4):
                        n = 4 * (r % 2) + x
                        ins = pe.transpose(bank[:, 4 + r % 2, P * x:P * x + P], s[:, r // 2, P * n:P * n + P], ident)
                    ins.then_inc(pt_ready, 1)
                for b2 in range(2):
                    ins = pe.transpose(bank[0:NS, 6, P * b2:P * b2 + P], s[:, b2, PAST // 2:], ident)
                ins.then_inc(pt_ready, 1)

            def pair_values(j, kv4, turns, between=None):
                pe.wait_ge(pt_evac, 5 * j + 5)
                for k in range(8):
                    c, b2 = k % 4, k // 4
                    raw_wait(k, kv4, turns)
                    for pp in range(2):
                        n = NBLK * b2 + 2 * c + pp
                        for hf in range(2):
                            at = 1024 * pp + 512 * hf
                            ins = pe.matmul(bank[:, 2 * b2 + hf, :], pT[:, P * n:P * n + P], raw[:, k % RING, at:at + 512],
                                            start=(c == 0 and pp == 0), stop=False)
                    ins.then_inc(v_used, 1)
                    if between is not None and k in between:
                        between[k]()
                    if c == 3:
                        for hf in range(2):
                            ins = pe.matmul(bank[:, 2 * b2 + hf, :].rearrange("p (h r d) -> p h r d", h=4, r=2)[:, :, 0, :],
                                            po[:, P * b2:P * b2 + P], vsam[:, 256 * hf:256 * hf + 256].rearrange("k (h d) -> k h d", h=4),
                                            start=False, stop=True)
                        ins.then_inc(acc_ready, 1)

            def attn_turn(j, first=False, b=7):
                if not first:
                    pe.wait_ge(av_evac, j)
                for b2 in range(2):
                    pe.wait_ge(arow_ready, 2 * j + b2 + 1)
                    for e in range(2):
                        cols = con[:, C_SUM:C_SUM + NS].rearrange("p (m e t) -> p m e t", m=NHP, e=2)[:, :, e, :]
                        at = 32 * b2
                        ins = pe.matmul(bank[64 * e:64 * e + 64, b, at:at + 32], arow[:, b2, :], cols, start=True, stop=True)
                ins.then_inc(at_mm, 1)

            pe.wait_ge(ko_lo, 1)
            pe.wait_ge(gl_out, 2)
            pe.wait_ge(pv_out, 4)
            pair_keys(0, 0, 0, first=True)
            gate_sum(0)
            keep_clock(0, 5)
            max_swap(0)
            keep_clock(0, 7)
            prob_sum(0)
            keep_clock(0, 2)
            pair_probs(0)

            def next_pair(j, kv4, turns, first=False):
                pe.wait_ge(pt_evac, 5 * j)
                pair_keys(j, kv4, turns)
                pair_values(j - 1, kv4 + 2, turns, {0: lambda: gate_sum(j), 2: lambda: max_swap(j), 5: lambda: prob_sum(j)})
                pair_probs(j)
                attn_turn(j - 1, first)

            next_pair(1, 2, 0, first=True)
            with pe.Fori(2, 4) as j:
                next_pair(j, 6, 64 * 4 * (j - 2))

            pe.wait_ge(pt_evac, 20)
            pe.wait_ge(conv_ready, NCC)
            pe.wait_ge(av_evac, 3)
            for c in range(NCC):
                pe.matmul(bank[:, 4 + c, 0:T], gnones, yT[:, NCC + c, :], start=True, stop=True).then_inc(gm_mm, 1)

            def group_variances():
                for c in range(NCC):
                    pe.wait_ge(gq_ready, c + 1)
                    pe.matmul(bank[:, 4 + c, 0:T], gnones, tmp[:, c, :], start=True, stop=True).then_inc(gv_mm, 1)

            pair_values(3, 14, 0, {0: group_variances})

            first = [(4 + 2 * u + cc, slot_w(WOUT, u), cc, (n_ready, w_used)[cc]) for u in range(2) for cc in range(2)]
            for u in range(2):
                pe.wait_ge(w_lo, WOUT[0] + u + 1)
                products(first[2 * u:2 * u + 2], m_parts(MIX_ORDER[:NCC]), lambda n: pe.wait_ge(ml_ready, 16 + n + 1), stop=False)
                if u == 0:
                    attn_turn(3, b=0)
            products(first, m_parts(MIX_ORDER[NCC:]), lambda n: pe.wait_ge(ml_ready, 16 + NCC + n + 1), start=False)
            for u in range(2, WOUT[2]):
                pe.wait_ge(w_lo, WOUT[0] + u + 1)
                for cc in range(2):
                    pe.wait_ge(y_ready, 8 + 2 * (u - 2) + cc + 1)
                    ins = product(4 + 2 * (u % 2) + cc, slot_w(WOUT, u), cc, m_parts(MIX_ORDER))
                    ins.then_inc(n_ready if cc == 0 else w_used, 1)
            norm(1)
            up(1, UP2, 24)
            down(1, DN2, 16)
            norm(2)
            for n in range(6):
                half, tt = n // 3, n % 3
                w = P if tt < 2 else NS
                for c in range(4):
                    if tt == 0:
                        pe.wait_ge(x_ready, 16 + 4 * half + c + 1)
                    ins = pe.transpose(bank[0:w, 2 + n, P * c:P * c + P], xT[:, 4 * half + c, P * tt:P * tt + w], ident)
                ins.then_inc(out_t, 1)


_INS = ["x_prompt", "x_sample", "cache_k", "cache_v", "state_conv", "page_table", "c_prompt", "c_sample", "w_ada", "b_ada",
        "ffn1_wg", "ffn1_wu", "ffn1_wd", "w_in", "w_dw", "b_dw", "gn_g", "gn_b", "beta_attn", "beta_conv", "w_out",
        "ffn2_wg", "ffn2_wu", "ffn2_wd", "ln_g", "ln_b"]
_OUTS = [("y_prompt", (1, SEQ, D)), ("y_sample", (DB, DT, D)), ("k_prompt_new", (1, 1, SEQ // PAGE, NH, PAGE, HD)),
         ("v_prompt_new", (1, 1, SEQ // PAGE, NH, PAGE, HD)), ("conv_prompt_new", (1, 1, ST, CC)),
         ("k_sample_new", (1, DB, NH, DT, HD)), ("v_sample_new", (1, DB, NH, DT, HD)), ("conv_sample_new", (1, DB, ST, CC))]


def kernel(**inputs):
    import concourse.bacc as bacc
    from concourse.bass_utils import run_bass_kernel_spmd

    nc = bacc.Bacc("TRN2", target_bir_lowering=False, num_devices=1)
    arrays, ins, outs = {}, {}, {}
    for name in _INS + ["consts"]:
        a = constants() if name == "consts" else np.ascontiguousarray(inputs[name])
        arrays[f"in_{name}"] = a
        ins[name] = nc.dram_tensor(f"in_{name}", a.shape, mybir.dt.from_np(a.dtype), kind="ExternalInput").ap()
    for name, shape in _OUTS:
        outs[name] = nc.dram_tensor(f"out_{name}", shape, F32, kind="ExternalOutput").ap()
    build(nc, ins, outs)
    r = run_bass_kernel_spmd(nc, [arrays], core_ids=[0])
    return tuple(r.results[0][f"out_{name}"] for name, _ in _OUTS)
```
